# Optimizing a Trainium2 kernel written in Bass

```python
import math
import jax, jax.numpy as jnp
from jax import lax
import numpy as np

D_MODEL = 1024
BATCH = 1
SEQ = 512
DEPTH = 2

GRID_W = 64
CTX_LEN = 256
N_MIXERS = 4
EPS = 1e-6
NEG_INF = -1e30
CHUNK = 64

HG_HEADS = 8
HG_DK = 128
HG_DV = D_MODEL // HG_HEADS
HG_IN = 3 * HG_HEADS * HG_DK + HG_HEADS * HG_DV + D_MODEL

SSM_D_INNER = 2 * D_MODEL
SSM_HEADDIM = 64
SSM_HEADS = SSM_D_INNER // SSM_HEADDIM
SSM_GROUPS = 4
SSM_STATE = 128
SSM_CONV = 5
SSM_CONV_DIM = SSM_D_INNER + 2 * SSM_GROUPS * SSM_STATE
SSM_IN_DIM = SSM_D_INNER + SSM_CONV_DIM + 2 * SSM_HEADS

POOL_WINDOWS = (2, 4, 8, 16)
POOL_GROUP = D_MODEL // len(POOL_WINDOWS)

ATT_HEAD_DIM = 64
ATT_Q_HEADS = D_MODEL // ATT_HEAD_DIM
ATT_KV_HEADS = 4
ATT_WINDOW = 128
ATT_BLOCK = 128
ROPE_THETA = 10000.0

FFN_HIDDEN = -(-8 * D_MODEL // (3 * 256)) * 256

N_OCC = tuple((DEPTH - m + N_MIXERS - 1) // N_MIXERS for m in range(N_MIXERS))

kernel_name = "hybrid_interleaved_dit_prefix_ctx"

def rmsnorm(x, w):
    xf = x.astype(jnp.float32)
    y = xf * lax.rsqrt(jnp.mean(xf * xf, axis=-1, keepdims=True) + EPS)
    return (y * w.astype(jnp.float32)).astype(x.dtype)

def swiglu(h, w_in, w_out):
    gate, up = jnp.split(h @ w_in, 2, axis=-1)
    return (jax.nn.silu(gate) * up) @ w_out

def flip(t):
    return jnp.flip(t, axis=1)

def gla_chunk_scan(q, k, v, log_f, s0):
    f32 = jnp.float32
    b, n, h, dk = q.shape
    dv = v.shape[-1]
    nc = n // CHUNK
    qc, kc, lf = (t.astype(f32).reshape(b, nc, CHUNK, h, dk) for t in (q, k, log_f))
    vc = v.astype(f32).reshape(b, nc, CHUNK, h, dv)
    cum = jnp.cumsum(lf, axis=2)
    ref = cum[:, :, CHUNK // 2 - 1:CHUNK // 2]
    qr = qc * jnp.exp(cum - ref)
    kr = kc * jnp.exp(ref - cum)
    causal = jnp.tril(jnp.ones((CHUNK, CHUNK), bool))
    att = jnp.where(causal, jnp.einsum('bclhd,bcshd->bchls', qr, kr), 0.0)
    o_intra = jnp.einsum('bchls,bcshv->bclhv', att, vc)
    last = cum[:, :, -1:]
    ds = jnp.einsum('bcshd,bcshv->bchdv', kc * jnp.exp(last - cum), vc)
    decay = jnp.exp(last[:, :, 0])

    def step(s, inp):
        g, d = inp
        return g[..., None] * s + d, s

    s_fin, s_in = lax.scan(step, s0.astype(f32), (jnp.moveaxis(decay, 1, 0), jnp.moveaxis(ds, 1, 0)))
    s_in = jnp.moveaxis(s_in, 0, 1)
    o_inter = jnp.einsum('bclhd,bchdv->bclhv', qc * jnp.exp(cum), s_in)
    o = (o_intra + o_inter).reshape(b, n, h, dv)
    return o.astype(v.dtype), s_fin

def hgrn2_mixer(h_lat, h_ctx, w_in, lb_f, lb_b, gn_w, w_out, need_ctx):
    f32 = jnp.float32
    hk = HG_HEADS * HG_DK

    def prep(h):
        bsz, m, _ = h.shape
        q, zf, zb, v, g = jnp.split(h @ w_in, [hk, 2 * hk, 3 * hk, 3 * hk + HG_HEADS * HG_DV], axis=-1)

        def gate(z, lb):
            z32 = z.astype(f32)
            log_f = jnp.log(lb + (1.0 - lb) * jax.nn.sigmoid(z32))
            k = (1.0 - lb) * jax.nn.sigmoid(-z32)
            return k.reshape(bsz, m, HG_HEADS, HG_DK), log_f.reshape(bsz, m, HG_HEADS, HG_DK)

        kf, lff = gate(zf, lb_f)
        kb, lfb = gate(zb, lb_b)
        q = jax.nn.silu(q).reshape(bsz, m, HG_HEADS, HG_DK)
        v = v.reshape(bsz, m, HG_HEADS, HG_DV)
        return q, kf, lff, kb, lfb, v, g

    def readout(o, g):
        bsz, m = o.shape[:2]
        o = rmsnorm(o, gn_w).reshape(bsz, m, HG_HEADS * HG_DV).astype(g.dtype)
        return (o * jax.nn.silu(g)) @ w_out

    bsz = h_lat.shape[0]
    s0 = jnp.zeros((bsz, HG_HEADS, HG_DK, HG_DV), f32)
    qc, kfc, lfc, kbc, lbc, vc, gc = prep(h_ctx)
    oc_f, sc_f = gla_chunk_scan(qc, kfc, vc, lfc, s0)
    oc_b, sc_b = gla_chunk_scan(flip(qc), flip(kbc), flip(vc), flip(lbc), s0)
    ql, kfl, lfl, kbl, lbl, vl, gl = prep(h_lat)
    ol_f, _ = gla_chunk_scan(ql, kfl, vl, lfl, sc_f)
    ol_b, _ = gla_chunk_scan(flip(ql), flip(kbl), flip(vl), flip(lbl), sc_b)
    y_lat = readout(ol_f + flip(ol_b), gl)
    y_ctx = readout(oc_f + flip(oc_b), gc) if need_ctx else None
    return y_lat, y_ctx

def ssd_chunk_scan(x, dt, a, bm, cm, s0):
    f32 = jnp.float32
    b, n, h, p = x.shape
    g, ns = bm.shape[2], bm.shape[3]
    hpg = h // g
    nc = n // CHUNK
    xc = x.astype(f32).reshape(b, nc, CHUNK, g, hpg, p)
    dtc = dt.astype(f32).reshape(b, nc, CHUNK, g, hpg)
    bc = bm.astype(f32).reshape(b, nc, CHUNK, g, ns)
    cc = cm.astype(f32).reshape(b, nc, CHUNK, g, ns)
    cum = jnp.cumsum(dtc * a.reshape(g, hpg), axis=2)
    seg = cum[:, :, :, None] - cum[:, :, None]
    causal = jnp.tril(jnp.ones((CHUNK, CHUNK), bool))[:, :, None, None]
    lmat = jnp.exp(jnp.where(causal, seg, -jnp.inf))
    cb = jnp.einsum('bctgn,bcsgn->bctsg', cc, bc)
    xdt = xc * dtc[..., None]
    y_diag = jnp.einsum('bctsgh,bcsghp->bctghp', cb[..., None] * lmat, xdt)
    last = cum[:, :, -1:]
    ds = jnp.einsum('bcsgn,bcsgh,bcsghp->bcghpn', bc, jnp.exp(last - cum), xdt)
    decay = jnp.exp(last[:, :, 0])

    def step(s, inp):
        d, u = inp
        return d[..., None, None] * s + u, s

    s_fin, s_in = lax.scan(step, s0.astype(f32), (jnp.moveaxis(decay, 1, 0), jnp.moveaxis(ds, 1, 0)))
    s_in = jnp.moveaxis(s_in, 0, 1)
    y_off = jnp.einsum('bctgn,bcghpn,bctgh->bctghp', cc, s_in, jnp.exp(cum))
    y = (y_diag + y_off).reshape(b, n, h, p)
    return y.astype(x.dtype), s_fin

def centred_depthwise_conv(x, w, bias):
    width, ch = w.shape
    half = width // 2
    y = lax.conv_general_dilated(x, w[:, None, :].astype(x.dtype), window_strides=(1,),
                                 padding=[(half, width - 1 - half)],
                                 dimension_numbers=('NWC', 'WIO', 'NWC'), feature_group_count=ch)
    return y + bias

def mamba2_mixer(h_lat, h_ctx, w_in, conv_w, conv_b, dt_bias, a_log, d_skip, norm_w, w_out, need_ctx):
    f32 = jnp.float32
    gn = SSM_GROUPS * SSM_STATE
    a = -jnp.exp(a_log.astype(f32))

    def prep(h):
        bsz, m, _ = h.shape
        z, xbc, dt = jnp.split(h @ w_in, [SSM_D_INNER, SSM_D_INNER + SSM_CONV_DIM], axis=-1)
        xbc = jax.nn.silu(centred_depthwise_conv(xbc, conv_w, conv_b))
        xs, bm, cm = jnp.split(xbc, [SSM_D_INNER, SSM_D_INNER + gn], axis=-1)
        xs = xs.reshape(bsz, m, SSM_HEADS, SSM_HEADDIM)
        bm = bm.reshape(bsz, m, SSM_GROUPS, SSM_STATE)
        cm = cm.reshape(bsz, m, SSM_GROUPS, SSM_STATE)
        dt = jax.nn.softplus(dt.astype(f32).reshape(bsz, m, 2, SSM_HEADS) + dt_bias.astype(f32))
        return z, xs, bm, cm, dt

    def readout(y_f, y_b, xs, z):
        bsz, m = xs.shape[:2]
        y = (y_f + y_b + d_skip[:, None] * xs).reshape(bsz, m, SSM_D_INNER) * jax.nn.silu(z)
        y = rmsnorm(y.reshape(bsz, m, SSM_GROUPS, SSM_D_INNER // SSM_GROUPS),
                    norm_w.reshape(SSM_GROUPS, -1)).reshape(bsz, m, SSM_D_INNER)
        return y @ w_out

    bsz = h_lat.shape[0]
    s0 = jnp.zeros((bsz, SSM_GROUPS, SSM_HEADS // SSM_GROUPS, SSM_HEADDIM, SSM_STATE), f32)
    zc, xc, bc, cc, dtc = prep(h_ctx)
    yc_f, sc_f = ssd_chunk_scan(xc, dtc[:, :, 0], a[0], bc, cc, s0)
    yc_b, sc_b = ssd_chunk_scan(flip(xc), flip(dtc[:, :, 1]), a[1], flip(bc), flip(cc), s0)
    zl, xl, bl, cl, dtl = prep(h_lat)
    yl_f, _ = ssd_chunk_scan(xl, dtl[:, :, 0], a[0], bl, cl, sc_f)
    yl_b, _ = ssd_chunk_scan(flip(xl), flip(dtl[:, :, 1]), a[1], flip(bl), flip(cl), sc_b)
    y_lat = readout(yl_f, flip(yl_b), xl, zl)
    y_ctx = readout(yc_f, flip(yc_b), xc, zc) if need_ctx else None
    return y_lat, y_ctx

def pool_mixer(h, w_grp, ch_scale):
    f32 = jnp.float32
    bsz, m, _ = h.shape
    hf = h.astype(f32)
    cs = jnp.concatenate([jnp.zeros((bsz, 1, D_MODEL), f32), jnp.cumsum(hf, axis=1)], axis=1)
    t = jnp.arange(m)
    outs = []
    for gi, win in enumerate(POOL_WINDOWS):
        lo = jnp.clip(t - win // 2, 0, m)
        hi = jnp.clip(t + win - win // 2, 0, m)
        sl = slice(gi * POOL_GROUP, (gi + 1) * POOL_GROUP)
        cg = cs[:, :, sl]
        mean = (cg[:, hi] - cg[:, lo]) / (hi - lo).astype(f32)[None, :, None]
        delta = (mean - hf[:, :, sl]).astype(h.dtype)
        outs.append(delta @ w_grp[gi])
    return jnp.concatenate(outs, axis=-1) * ch_scale

def axial_rope_tables(row_ids, col_ids):
    f32 = jnp.float32
    half = ATT_HEAD_DIM // 2
    inv = ROPE_THETA ** (-jnp.arange(0, half, 2, dtype=f32) / half)

    def tab(pos):
        ang = pos.astype(f32)[:, None] * inv[None]
        ang = jnp.concatenate([ang, ang], axis=-1)
        return jnp.cos(ang), jnp.sin(ang)

    cr, sr = tab(row_ids)
    cc, sc = tab(col_ids)
    return jnp.concatenate([cr, cc], -1), jnp.concatenate([sr, sc], -1)

def rotate_half(x):
    x1, x2 = jnp.split(x, 2, axis=-1)
    return jnp.concatenate([-x2, x1], axis=-1)

def apply_axial_rope(x, cos, sin):
    xr, xc = jnp.split(x, 2, axis=-1)
    rot = jnp.concatenate([rotate_half(xr), rotate_half(xc)], axis=-1)
    return (x * cos + rot * sin).astype(x.dtype)

def softmax_with_sink(scores, sink):
    s = jnp.concatenate([scores, jnp.broadcast_to(sink, scores.shape[:-1] + (1,))], axis=-1)
    return jax.nn.softmax(s, axis=-1)[..., :-1]

def window_gqa_mixer(h_lat, h_ctx, w_qkv, sink, w_out, cos, sin, need_ctx):
    f32 = jnp.float32
    grp = ATT_Q_HEADS // ATT_KV_HEADS
    qd, kd = ATT_Q_HEADS * ATT_HEAD_DIM, ATT_KV_HEADS * ATT_HEAD_DIM
    scale = ATT_HEAD_DIM ** -0.5

    def proj(h):
        bsz, m, _ = h.shape
        q, k, v = jnp.split(h @ w_qkv, [qd, qd + kd], axis=-1)
        return (q.reshape(bsz, m, ATT_KV_HEADS, grp, ATT_HEAD_DIM),
                k.reshape(bsz, m, ATT_KV_HEADS, ATT_HEAD_DIM),
                v.reshape(bsz, m, ATT_KV_HEADS, ATT_HEAD_DIM))

    bsz, n, _ = h_lat.shape
    ql, kl, vl = proj(h_lat)
    qc, kc, vc = proj(h_ctx)
    ql = apply_axial_rope(ql, cos[:, None, None], sin[:, None, None])
    kl = apply_axial_rope(kl, cos[:, None], sin[:, None])
    sink_l = sink.astype(f32).reshape(ATT_KV_HEADS, grp)[None, :, :, None, None]

    span = ATT_BLOCK + 2 * ATT_WINDOW
    pad = ((0, 0), (ATT_WINDOW, ATT_WINDOW), (0, 0), (0, 0))
    kp = jnp.pad(kl, pad)
    vp = jnp.pad(vl, pad)
    k_rel = jnp.arange(span) - ATT_WINDOW
    band = jnp.abs(k_rel[None, :] - jnp.arange(ATT_BLOCK)[:, None]) <= ATT_WINDOW

    def block(bi):
        start = bi * ATT_BLOCK
        qb = lax.dynamic_slice_in_dim(ql, start, ATT_BLOCK, axis=1)
        kb = lax.dynamic_slice_in_dim(kp, start, span, axis=1)
        vb = lax.dynamic_slice_in_dim(vp, start, span, axis=1)
        kpos = start + k_rel
        valid = band & ((kpos >= 0) & (kpos < n))[None, :]
        s_lat = jnp.where(valid, jnp.einsum('bqkgd,bmkd->bkgqm', qb, kb).astype(f32) * scale, NEG_INF)
        s_ctx = jnp.einsum('bqkgd,bckd->bkgqc', qb, kc).astype(f32) * scale
        p = softmax_with_sink(jnp.concatenate([s_lat, s_ctx], axis=-1), sink_l).astype(vl.dtype)
        return (jnp.einsum('bkgqm,bmkd->bqkgd', p[..., :span], vb)
                + jnp.einsum('bkgqc,bckd->bqkgd', p[..., span:], vc))

    o = lax.map(block, jnp.arange(n // ATT_BLOCK))
    y_lat = jnp.moveaxis(o, 0, 1).reshape(bsz, n, D_MODEL) @ w_out
    y_ctx = None
    if need_ctx:
        m = h_ctx.shape[1]
        s = jnp.einsum('bqkgd,bckd->bkgqc', qc, kc).astype(f32) * scale
        p = softmax_with_sink(s, sink_l).astype(vc.dtype)
        y_ctx = jnp.einsum('bkgqc,bckd->bqkgd', p, vc).reshape(bsz, m, D_MODEL) @ w_out
    return y_lat, y_ctx

def setup_inputs(seed: int = 0) -> dict:
    key = jax.random.key(seed)
    ks = iter(jax.random.split(key, 40))
    f32 = jnp.float32
    D = D_MODEL
    n_a, n_b, n_c, n_d = N_OCC

    def nrm(shape, s):
        return jax.random.normal(next(ks), shape, f32) * s

    def unif(shape, lo, hi):
        return jax.random.uniform(next(ks), shape, f32, lo, hi)

    dt0 = jnp.exp(unif((n_b, 2, SSM_HEADS), math.log(1e-3), math.log(1e-1)))
    return {
        "x": nrm((BATCH, SEQ, D), 1.0),
        "c": nrm((BATCH, D), 1.0),
        "ctx": nrm((BATCH, CTX_LEN, D), 1.0),
        "c_ctx": nrm((D,), 1.0),
        "ada_w": nrm((DEPTH, D, 6 * D), 0.5 * D ** -0.5),
        "ada_b": nrm((DEPTH, 6 * D), 0.02),
        "norm_w": 1.0 + nrm((DEPTH, 2, D), 0.02),
        "ffn_w_in": nrm((DEPTH, D, 2 * FFN_HIDDEN), D ** -0.5),
        "ffn_w_out": nrm((DEPTH, FFN_HIDDEN, D), FFN_HIDDEN ** -0.5),
        "final_norm_w": 1.0 + nrm((D,), 0.02),
        "hg_w_in": nrm((n_a, D, HG_IN), D ** -0.5),
        "hg_lb": nrm((2, DEPTH + 1, HG_HEADS * HG_DK), 0.1),
        "hg_norm_w": 1.0 + nrm((n_a, HG_DV), 0.02),
        "hg_w_out": nrm((n_a, HG_HEADS * HG_DV, D), (HG_HEADS * HG_DV) ** -0.5),
        "ssm_w_in": nrm((n_b, D, SSM_IN_DIM), D ** -0.5),
        "ssm_conv_w": nrm((n_b, SSM_CONV, SSM_CONV_DIM), SSM_CONV ** -0.5),
        "ssm_conv_b": nrm((n_b, SSM_CONV_DIM), 0.02),
        "ssm_dt_bias": dt0 + jnp.log(-jnp.expm1(-dt0)),
        "ssm_a_log": jnp.log(unif((n_b, 2, SSM_HEADS), 1.0, 16.0)),
        "ssm_d": 1.0 + nrm((n_b, SSM_HEADS), 0.02),
        "ssm_norm_w": 1.0 + nrm((n_b, SSM_D_INNER), 0.02),
        "ssm_w_out": nrm((n_b, SSM_D_INNER, D), SSM_D_INNER ** -0.5),
        "pool_w": nrm((n_c, len(POOL_WINDOWS), POOL_GROUP, POOL_GROUP), POOL_GROUP ** -0.5),
        "pool_scale": 1.0 + nrm((n_c, D), 0.02),
        "att_w_qkv": nrm((n_d, D, (ATT_Q_HEADS + 2 * ATT_KV_HEADS) * ATT_HEAD_DIM), D ** -0.5),
        "att_sink": nrm((n_d, ATT_Q_HEADS), 0.5),
        "att_w_out": nrm((n_d, D, D), D ** -0.5),
    }

def reference(x, c, ctx, c_ctx, ada_w, ada_b, norm_w, ffn_w_in, ffn_w_out, final_norm_w,
              hg_w_in, hg_lb, hg_norm_w, hg_w_out,
              ssm_w_in, ssm_conv_w, ssm_conv_b, ssm_dt_bias, ssm_a_log, ssm_d, ssm_norm_w, ssm_w_out,
              pool_w, pool_scale, att_w_qkv, att_sink, att_w_out):
    f32 = jnp.float32
    bsz, n, _ = x.shape
    rows = n // GRID_W
    row_ids = jnp.repeat(jnp.arange(rows), GRID_W)
    col_ids = jnp.tile(jnp.arange(GRID_W), rows)
    cos, sin = axial_rope_tables(row_ids, col_ids)

    lb_tab = jnp.cumsum(jax.nn.softmax(hg_lb.astype(f32), axis=1), axis=1)

    silu_c = jax.nn.silu(c)
    silu_cc = jax.nn.silu(c_ctx)[None]
    x_lat, x_ctx = x, ctx
    for i in range(DEPTH):
        kind, j = i % N_MIXERS, i // N_MIXERS
        need_ctx = i < DEPTH - 1
        mod_l = jnp.split((silu_c @ ada_w[i] + ada_b[i])[:, None], 6, axis=-1)
        mod_c = jnp.split((silu_cc @ ada_w[i] + ada_b[i])[:, None], 6, axis=-1)
        sh_l, sc_l, g_l, sh2_l, sc2_l, g2_l = mod_l
        sh_c, sc_c, g_c, sh2_c, sc2_c, g2_c = mod_c

        h_lat = rmsnorm(x_lat, norm_w[i, 0]) * (1 + sc_l) + sh_l
        h_ctx = rmsnorm(x_ctx, norm_w[i, 0]) * (1 + sc_c) + sh_c if (need_ctx or kind != 2) else None

        if kind == 0:
            y_lat, y_ctx = hgrn2_mixer(h_lat, h_ctx, hg_w_in[j], lb_tab[0, i], lb_tab[1, i],
                                       hg_norm_w[j], hg_w_out[j], need_ctx)
        elif kind == 1:
            y_lat, y_ctx = mamba2_mixer(h_lat, h_ctx, ssm_w_in[j], ssm_conv_w[j], ssm_conv_b[j],
                                        ssm_dt_bias[j], ssm_a_log[j], ssm_d[j], ssm_norm_w[j],
                                        ssm_w_out[j], need_ctx)
        elif kind == 2:
            y_lat = pool_mixer(h_lat, pool_w[j], pool_scale[j])
            y_ctx = pool_mixer(h_ctx, pool_w[j], pool_scale[j]) if need_ctx else None
        else:
            y_lat, y_ctx = window_gqa_mixer(h_lat, h_ctx, att_w_qkv[j], att_sink[j], att_w_out[j],
                                            cos, sin, need_ctx)

        x_lat = x_lat + g_l * y_lat
        x_lat = x_lat + g2_l * swiglu(rmsnorm(x_lat, norm_w[i, 1]) * (1 + sc2_l) + sh2_l,
                                      ffn_w_in[i], ffn_w_out[i])
        if need_ctx:
            x_ctx = x_ctx + g_c * y_ctx
            x_ctx = x_ctx + g2_c * swiglu(rmsnorm(x_ctx, norm_w[i, 1]) * (1 + sc2_c) + sh2_c,
                                          ffn_w_in[i], ffn_w_out[i])
    return rmsnorm(x_lat, final_norm_w)


_drawn_inputs = setup_inputs


def setup_inputs(seed=0):
    import zlib

    import numpy as np

    out = dict(_drawn_inputs(seed))
    spreads = {}
    factors = {'ctx': 4.43,
     'c_ctx': 3.723,
     'norm_w': 4.382,
     'final_norm_w': 8.307,
     'hg_lb': 8.0,
     'hg_norm_w': 8.0,
     'ssm_conv_b': 43.238,
     'ssm_d': 64.0,
     'ssm_norm_w': 64.0}
    for name, (base, spread) in spreads.items():
        noise = np.random.default_rng([zlib.crc32(name.encode()), seed]).standard_normal(out[name].shape)
        drawn = base * np.exp(spread * noise) if base else spread * noise
        out[name] = __import__('jax').numpy.asarray(drawn.astype(out[name].dtype))
    for name, factor in factors.items():
        out[name] = (out[name] * factor).astype(out[name].dtype)
    return out
```

```python
from contextlib import ExitStack

import concourse.bass as bass
from concourse import mybir

F32 = mybir.dt.float32
F32R = mybir.dt.float32r
BF16 = mybir.dt.bfloat16
I32 = mybir.dt.int32
ALU = mybir.AluOpType
ACT = mybir.ActivationFunctionType

P = 128
D = 1024
KT = D // P
NLAT, NCTX = 512, 256
T = NLAT + NCTX
NBLK = T // P
LBLK = NLAT // P
EPS = 1e-6
SEGS = ((0, NLAT), (NLAT, NCTX))

HEADS = 8
CH = 64
NCH = T // CH
LAT_CH = NLAT // CH
ORDER = (list(range(LAT_CH, NCH)) + list(range(LAT_CH)), list(range(NCH - 1, -1, -1)))
REF = (CH // 2 - 1, CH // 2)
LAST = (CH - 1, 0)

FFN = 2816
FH = FFN // P // 2

DI = 2048
GROUPS = 4
HPG = 8
HP = 64
NH = GROUPS * HPG
GW = DI // GROUPS
GT = GW // P
CONV_W = 5
XBC0 = DI
BC0, CC0 = XBC0 + DI, XBC0 + DI + GROUPS * P
SSM_IN = CC0 + GROUPS * P + 2 * NH
BORDER = ([4, 5, 0, 1, 2, 3], [5, 4, 3, 2, 1, 0])

PAN_HG = 0
PAN_HGO = PAN_HG + 5 * HEADS
PAN_F0 = PAN_HGO + KT
PAN_DT = PAN_F0 + 2 * (2 * FH + KT)
PAN_SS = PAN_DT + 1
PAN_SO = PAN_SS + 10 * GROUPS
PAN_F1 = PAN_SO + 2 * KT
PAN_END = PAN_F1 + 2 * (2 * FH + KT)
TIL_SO = PAN_SO
TIL_F1 = TIL_SO + KT

COL_NORM, COL_FIN, COL_C, COL_CC, COL_SN, COL_CB, COL_GN = 0, 32, 40, 48, 56, 72, 96


class At:

    def __init__(self, c, half=0):
        self.c, self.half = c, half

    def __add__(self, n):
        return At(self.c + n, self.half)

    @property
    def slot(self):
        return self.c % 2

    @property
    def turn(self):
        return self.half + self.c // 2

    @property
    def n(self):
        return self.half * 2 + self.c

    def past(self, k):
        return not isinstance(self.half, int) or self.n >= k


def memory(nc):
    m = {}
    base, limit = 16512, 229344

    def run(at, *items):
        for name, shape, *dt in items:
            dt = dt[0] if dt else F32
            n = 2 if dt == BF16 else 4
            for d in shape[1:]:
                n *= d
            end = at + (n + 31) // 32 * 32
            assert end <= limit, (name, end)
            m[name] = nc.alloc_sbuf_tensor_at(name, list(shape), dt, offset=at)
            at = end
        return at

    R = run(base,
            ("ident", (P, P)), ("identb", (P, P), BF16), ("ones", (P, 1)), ("mhalf", (P, 8)), ("carry", (P, 1)),
            ("colA", (P, 97)), ("colC", (P, 120)), ("mods", (P, 2, 48, 2)), ("afac", (P, 2, 2, KT, 2)),
            ("stat", (P, 8)), ("rstd", (P, 8)), ("lb", (P, 2, HEADS)), ("oml", (P, 2, HEADS)),
            ("segm", (P, T)), ("mask0", (P, NBLK, CH), I32), ("mask1", (P, NBLK, CH), I32),
            *[(f"raw{i}", (P, FH, P)) for i in (0, 1)],
            *[(f"w{w}{i}", (P, FH, P), F32R) for i in (0, 1) for w in ("hi", "lo")],
            ("hhi", (P, KT, T), F32R), ("hlo", (P, KT, T), F32R))
    W = 4 * T
    N = limit - 4 * W
    run(N, *[(f"{n}{i}", (P, T)) for n in ("sq", "hn") for i in (0, 1)])
    assert run(R, ("x0", (P, KT, T)), ("xin", (P, NBLK, D)), ("ada0", (P, KT, 512)), ("ada1", (P, KT, 512)),
               ("rowA", (97, P)), ("rowB", (96, P)), ("rowC", (120, P)), ("rowD", (48, P)),
               ("colB", (P, 96)), ("colD", (P, 2, 3, HEADS)), ("csil", (P, KT, 2)),
               ("lbt", (P, 2, HEADS)), ("lbe", (P, 2, 3, HEADS))) <= N
    run(R, ("og", (P, HEADS, T)),
        *[(f"{n}{d}", (P, T)) for n in ("kr", "qr", "qe", "kd", "th", "lf", "cum", "gs") for d in (0, 1)],
        *[(n, (P, T)) for n in ("qs", "vT", "osb", "osq")],
        *[(n, (P, NBLK, P)) for n in ("vtm", "kdtm0", "kdtm1")],
        *[(n, (P, NBLK, CH)) for n in ("att0", "att1", "attS")],
        *[(f"sin{d}", (P, NCH, P)) for d in (0, 1)], *[(f"gl{d}", (P, NCH)) for d in (0, 1)])
    assert run(R, ("mhi", (P, FH, T), F32R), ("x1", (P, KT, T)), ("mlo", (P, FH, T), F32R),
               ("act0", (P, T)), ("act1", (P, T)), ("mid0", (P, T)), ("mid1", (P, T))) <= N
    run(R, *[(n, (2 * NH, NBLK)) for n in ("cl", "dtb", "aneg")], ("dt", (2 * NH, T)), ("cumS", (2 * NH, T)),
        *[(n, (P, NBLK, 2 * NH)) for n in ("ncumT", "dtT", "wT", "ecT", "dec")],
        ("sel", (2 * NH, 2 * HPG)), ("neg0", (P, NLAT), BF16), ("neg1", (P, NLAT), BF16), ("dsk", (P, NH // 2)), ("dall", (P, NH)),
        ("z", (P, 2, GT, NLAT)), ("xpad0", (P, T + 8)), ("xpad1", (P, T + 8)), ("acc", (P, T + 2)),
        ("bfm", (P, T)), ("cfm", (P, T)), ("xfm", (P, GT, T)), ("btm", (P, NBLK, P)), ("xtm", (P, NBLK, GW)),
        ("cb", (P, NLAT)), *[(f"e{d}{i}", (P, NLAT)) for d in (0, 1) for i in (0, 1)],
        ("wx0", (P, GW)), ("wx1", (P, GW)), ("st0", (P, GW)), ("st1", (P, GW)),
        ("sc0", (P, GW)), ("sc1", (P, GW)), ("yb", (P, GT, NLAT)), ("ytm", (P, LBLK, GW)))
    run(R, ("ofin", (P, LBLK, D)))
    return m


def program(nc, x, c, ctx_x, c_ctx, ada_w, ada_b, norm_w, ffn_w_in, ffn_w_out, final_norm_w, hg_w_in, hg_lb,
            hg_norm_w, hg_w_out, ssm_w_in, ssm_conv_w, ssm_conv_b, ssm_dt_bias, ssm_a_log, ssm_d, ssm_norm_w,
            ssm_w_out, out):
    with ExitStack() as ctx:
        m = memory(nc)
        G = ctx.enter_context(nc.psum_tensor("G", [P, 2, 1024], F32))
        S = ctx.enter_context(nc.psum_tensor("S", [P, 4, 512], F32))
        Gq = G[:, :, :].rearrange("p s (h n) -> p (s h) n", h=2)
        Sf = S[:, :, :].rearrange("p b n -> p (b n)")
        PAIR = (Sf[:, 0:1024], Sf[:, 1024:2048])
        x_park = nc.dram_tensor("x_park", (P, KT, NLAT), F32, kind="Internal").ap()
        x_park0 = nc.dram_tensor("x_park0", (P, KT, T), F32, kind="Internal").ap()
        y_park = nc.dram_tensor("y_park", (GROUPS, P, GT, NLAT), F32, kind="Internal").ap()

        names = """rows xin slab0 slab1 raw0 raw1 small parked0 back0 parked1 back1 yout yin0 yin1 outd
            ident const cols tpe tdve ada modev modl afac csil lbs hi lo pan took0 took1
            x sq sqd stat rstd rbc hn hhi hlo rused
            sig lf cum dif ex kd qk vtm kdtm step cp att sf sb osq og0 og osp_hi osp_lo
            act mid mhi mlo
            dskin negz halo dtv dts pdt dtT negm xt eq xp tap conv ytr stc sm em cbs mm yo yd xw ds dsm ymc ym2
            ytt ya yz ysq yr ynorm yh yl fn ft fo ps""".split()
        s = {n: ctx.enter_context(nc.semaphore("s_" + n)) for n in names}
        took = (s["took0"], s["took1"])
        raw, whi, wlo = ([m[f"{n}{i}"] for i in (0, 1)] for n in ("raw", "whi", "wlo"))
        sq, hn = ([m[f"{n}{i}"] for i in (0, 1)] for n in ("sq", "hn"))
        ident, ones = m["ident"], m["ones"]

        def f32(ap):
            return ap.bitcast(F32)

        def mod(l, part, j, seg):
            return m["mods"][:, l, part * KT + j, seg:seg + 1]

        def block(ap, b):
            return ap[:, b * P:(b + 1) * P]

        def cols_of(w, off):
            return w[:, bass.ds(off, P)].rearrange("(k p) n -> p k n", p=P)

        HG_OFF = [0, 4 * D, D, 2 * D, 3 * D]

        def load_panel(sp, pn, src, kt):
            if pn.past(2):
                sp.wait_ge(s["lo"], pn.n - 1)
            sp.dma_start(raw[pn.slot][:, 0:kt, :], src).then_inc(s[f"raw{pn.slot}"], 16)

        def split_hi(act, pn, kt):
            act.wait_ge(s[f"raw{pn.slot}"], (pn.turn + 1) * 16)
            if pn.past(2):
                act.wait_ge(s["pan"], pn.n - 1)
            act.activation(whi[pn.slot][:, 0:kt, :], raw[pn.slot][:, 0:kt, :], ACT.Copy).then_inc(s["hi"], 1)

        def split_lo(dve, pn, kt):
            dve.wait_ge(s["hi"], pn.n + 1)
            dve.tensor_tensor(wlo[pn.slot][:, 0:kt, :], raw[pn.slot][:, 0:kt, :],
                              f32(whi[pn.slot][:, 0:kt, :]), ALU.subtract).then_inc(s["lo"], 1)

        def product(pe, pn, tl, rhi, rlo, kt, segs, k_base=0, first=True, last=True, need=None):
            pe.wait_ge(s["lo"], pn.n + 1)
            if first and tl.past(2):
                pe.wait_ge(took[tl.slot], tl.turn)
            for k in range(kt):
                if need is not None:
                    need(k)
                for i, (w, r) in enumerate(((whi, rhi), (whi, rlo), (wlo, rhi))):
                    for t0, n in segs:
                        ins = pe.matmul(G[:, tl.slot, t0:t0 + n], w[pn.slot][:, k, :],
                                        r[:, k_base + k, t0:t0 + n],
                                        start=(first and k == 0 and i == 0),
                                        stop=(last and k == kt - 1 and i == 2))
            ins.then_inc(s["pan"], 1)

        def done(eng, pn):
            eng.wait_ge(s["pan"], pn.n + 1)

        def squares_act(act, xt, N, segs, ready):
            nt = segs[-1][0] + segs[-1][1]
            for j in range(KT):
                ready(act, j)
                if 8 * N + j >= 2:
                    act.wait_ge(s["sqd"], 8 * N + j - 1)
                act.activation(sq[j % 2][:, 0:nt], xt[:, j, 0:nt], ACT.Square).then_inc(s["sq"], 1)

        def norm_act(act, xt, N, segs, ready, l, i):
            squares_act(act, xt, N, segs, ready)
            for j in range(KT):
                act.wait_ge(s["hn"], 8 * N + j + 1)
                for g, (t0, n) in enumerate(segs):
                    ins = act.activation(m["hhi"][:, j, t0:t0 + n], hn[j % 2][:, t0:t0 + n], ACT.Identity,
                                         bias=mod(l, 3 * i, j, g))
                ins.then_inc(s["hhi"], 1)

        def norm_pe(pe, N, K, nb):
            for j in range(KT):
                pe.wait_ge(s["sq"], 8 * N + j + 1)
                for b in range(nb):
                    ins = pe.matmul(S[:, 0, b:b + 1], block(sq[j % 2], b), ones[:, :],
                                    start=(j == 0 and b == 0), stop=(j == KT - 1), skip_group_check=True)
                ins.then_inc(s["sqd"], 1)
            spread_pe(pe, K, nb, PAIR[1])

        def spread_pe(pe, K, nb, to):
            pe.wait_ge(s["rstd"], K + 1)
            for b in range(nb):
                ins = pe.matmul(block(to, b), m["rstd"][:, b:b + 1].to_broadcast([P, P]), ident[:, :],
                                start=True, stop=True)
            ins.then_inc(s["rbc"], 1)

        def mean_dve(dve, nb, n):
            dve.tensor_scalar(m["stat"][:, 0:nb], S[:, 0, 0:nb], 1.0 / n, EPS, ALU.mult, ALU.add)\
               .then_inc(s["stat"], 1)

        def rsqrt_pool(pool, K, nb):
            pool.wait_ge(s["stat"], K + 1)
            pool.tensor_tensor(m["rstd"][:, 0:nb], m["stat"][:, 0:nb], m["mhalf"][:, 0:nb], ALU.pow)\
                .then_inc(s["rstd"], 1)

        def norm_dve(dve, xt, N, K, segs, l, i):
            dve.wait_ge(s["sqd"], 8 * (N + 1))
            mean_dve(dve, (segs[-1][0] + segs[-1][1]) // P, D)
            dve.wait_ge(s["rbc"], K + 1)

            def scaled(j):
                if j >= 2:
                    dve.wait_ge(s["hlo"], 8 * N + j - 1)
                for g, (t0, n) in enumerate(segs):
                    ins = dve.scalar_tensor_tensor(hn[j % 2][:, t0:t0 + n], xt[:, j, t0:t0 + n],
                                                   m["afac"][:, l, i, j, g:g + 1], PAIR[1][:, t0:t0 + n],
                                                   ALU.mult, ALU.mult)
                ins.then_inc(s["hn"], 1)

            def low(j):
                dve.wait_ge(s["hhi"], 8 * N + j + 1)
                for g, (t0, n) in enumerate(segs):
                    ins = dve.scalar_tensor_tensor(m["hlo"][:, j, t0:t0 + n], hn[j % 2][:, t0:t0 + n],
                                                   mod(l, 3 * i, j, g), f32(m["hhi"][:, j, t0:t0 + n]),
                                                   ALU.add, ALU.subtract)
                ins.then_inc(s["hlo"], 1)

            for j in range(KT + 1):
                if j < KT:
                    scaled(j)
                if j:
                    low(j - 1)

        def h_need(pe, N):
            return lambda k: pe.wait_ge(s["hlo"], 8 * N + k + 1)

        def tile_ready(base):
            def ready(eng, j):
                tl = base + j
                eng.wait_ge(took[tl.slot], tl.turn + 1)
            return ready

        def x_loaded(eng, j):
            eng.wait_ge(s["x"], NBLK * 2)

        heads = HEADS
        th, lf, cum, kr, qr, qe, kd, gs, sin, gl, att, kdtm, mask = (
            [m[f"{n}{d}"] for d in (0, 1)]
            for n in ("th", "lf", "cum", "kr", "qr", "qe", "kd", "gs", "sin", "gl", "att", "kdtm", "mask"))

        def chunks(ap):
            return ap.rearrange("p (c l) -> p c l", l=CH)

        def by_parity(buf):
            return buf[:, :].rearrange("p (b q l) -> p q b l", q=2, l=CH)

        def at_token(ap, t):
            return chunks(ap)[:, :, t:t + 1].to_broadcast([P, NCH, CH])

        def ds_place(d, step):
            if step == 2:
                lot = [(0, c) for c in ORDER[0][8:-1]] + [(1, c) for c in ORDER[1][8:-1]]
            else:
                lot = [(d, c) for c in ORDER[d][:8]]
            seen, res = [0, 0], []
            for dd, cc in lot:
                res.append((dd, cc, cc % 2, seen[cc % 2]))
                seen[cc % 2] += 1
            return res

        def hg_tensor_scan(pe, hp, h, step):
            pair = PAIR[(step - 1) % 2]
            bank = 2 * ((step - 1) % 2)
            if step == 1:
                pe.wait_ge(s["og0"], h + 1)
                v = hp + 4
                pe.wait_ge(took[v.slot], v.turn + 1)
                for b in range(NBLK):
                    ins = pe.transpose(block(pair, b), block(m["vT"][:, :], b), ident[:, :])
            elif step in (2, 3):
                d = step - 2
                if step == 3:
                    pe.wait_ge(s["vtm"], h + 1)
                pe.wait_ge(s["kd"], 2 * h + d + 1)
                for b in range(NBLK):
                    ins = pe.transpose(block(pair, b), block(kd[d][:, :], b), ident[:, :])
            elif step == 4:
                pe.wait_ge(s["kdtm"], 2 * h + 1)
                pe.wait_ge(s["qk"], h + 1)
                H2 = CH // 2
                for d in (0, 1):
                    for c in range(NCH):
                        col, kc, qc = (NBLK * d + c // 2) * CH, chunks(kr[d][:, :])[:, c, :], chunks(qr[d][:, :])[:, c, :]
                        for half in (0, 1):
                            o = CH * (c % 2) + H2 * half
                            q0, q1 = (0, CH) if half == d else (H2 * half, H2 * half + H2)
                            ins = pe.matmul(pair[o:o + H2, col + q0:col + q1],
                                            kc[:, H2 * half:H2 * half + H2], qc[:, q0:q1],
                                            start=True, stop=True)
            elif step in (5, 6, 7):
                if step == 5:
                    pe.wait_ge(s["kdtm"], 2 * h + 2)
                elif step == 6:
                    pe.wait_ge(s["cp"], 2 * h + 2)
                else:
                    pe.wait_ge(s["sf"], 11 * h + 8)
                for d, cc, bk, pos in ds_place(step - 5, step - 5):
                    o = CH * (cc % 2)
                    ins = pe.matmul(S[:, bank + bk, pos * P:(pos + 1) * P], kdtm[d][o:o + CH, cc // 2, :],
                                    m["vtm"][o:o + CH, cc // 2, :], start=True, stop=True)
            elif step == 8:
                pe.wait_ge(s["sf"], 11 * h + 11)
                pe.wait_ge(s["sb"], 11 * h + 11)
                pe.wait_ge(s["att"], h + 1)
                for c in range(NCH):
                    o = CH * (c % 2)
                    to = S[:, bank + c % 2, (c // 2) * CH:(c // 2 + 1) * CH]
                    inter = [d for d in (0, 1) if c != ORDER[d][0]]
                    pe.matmul(to, m["vtm"][o:o + CH, c // 2, :], m["attS"][o:o + CH, c // 2, :],
                              start=True, stop=False)
                    for d in inter:
                        ins = pe.matmul(to, sin[d][:, c, :], chunks(qe[d][:, :])[:, c, :],
                                        start=False, stop=(d == inter[-1]))
            elif step == 9:
                pe.wait_ge(s["osq"], h + 1)
                for b in range(NBLK):
                    ins = pe.matmul(S[:, 0, b:b + 1], block(m["osq"][:, :], b), ones[:, :],
                                    start=True, stop=True)
            else:
                spread_pe(pe, h + 1, NBLK, pair)
                return
            ins.then_inc(s["step"], 1)

        STEPS_AFTER = {0: (1,), 1: (2, 3), 2: (4, 5, 6), 3: (7, 8), 4: (9, 10)}

        def hg_tensor(pe, hg, hn_, hp, h, pn_par, ps_par):
            for j in range(5):
                if hg is not None:
                    pn = hg + j
                    product(pe, pn, pn, m["hhi"], m["hlo"], KT, SEGS,
                            need=h_need(pe, 0) if h is None and j == 0 else None)
                if h is not None:
                    for step in STEPS_AFTER[j]:
                        hg_tensor_scan(pe, hp, h, step)

        def step_done(eng, h, step):
            eng.wait_ge(s["step"], 9 * h + step)

        def hg_scalar(act, hg, hn_, hp, h, pn_par, ps_par):
            for j in range(5):
                if hg is not None:
                    pn = hg + j
                    split_hi(act, pn + 2, KT)
                if j == 4 and h is not None:
                    step_done(act, h, 8)
                    o4 = S[:, 2:4, 0:NBLK * CH].rearrange("p q (b l) -> p q b l", l=CH)
                    act.activation(by_parity(m["osb"]), o4, ACT.Copy)
                    act.activation(by_parity(m["osq"]), o4, ACT.Square).then_inc(s["osq"], 1)
                if hg is not None:
                    tile = G[:, pn.slot, 0:T]
                    if j == 0:
                        if h is not None:
                            act.wait_ge(s["qk"], hn_)
                        ins = act.activation(m["qs"][:, :], tile, ACT.Silu)
                    elif j == 1:
                        ins = act.activation(gs[pn_par][:, :], tile, ACT.Silu)
                    elif j in (2, 3):
                        ins = act.activation(th[j - 2][:, :], tile, ACT.Tanh, scale=0.5)
                    else:
                        ins = act.activation(m["vT"][:, :], tile, ACT.Copy)
                    ins.then_inc(took[pn.slot], 1)
                    if j == 3:
                        for d in (0, 1):
                            act.wait_ge(s["sig"], 4 * hn_ + d + 1)
                            act.activation(lf[d][:, :], lf[d][:, :], ACT.Ln, bias=m["lb"][:, d, bass.ds(hn_, 1)],
                                           scale=m["oml"][:, d, bass.ds(hn_, 1)]).then_inc(s["lf"], 1)
                    if j == 4:
                        for d in (0, 1):
                            act.wait_ge(s["dif"], 4 * hn_ + 2 * d + 1)
                            act.activation(qr[d][:, :], kr[d][:, :], ACT.Exp).then_inc(s["eq"], 1)
                            act.activation(qe[d][:, :], cum[d][:, :], ACT.Exp)
                            act.activation(gl[d][:, :], chunks(cum[d][:, :])[:, :, LAST[d]], ACT.Exp)
                            act.wait_ge(s["dif"], 4 * hn_ + 2 * d + 2)
                            act.activation(kd[d][:, :], kd[d][:, :], ACT.Exp, scale=-1.0)
                            act.wait_ge(s["eq"], 2 * hn_ + d + 1)
                            act.activation(kr[d][:, :], kr[d][:, :], ACT.Exp, scale=-1.0).then_inc(s["ex"], 1)
                if h is not None and j == 0:
                    step_done(act, h, 1)
                    act.activation(m["vtm"][:, :, :].rearrange("p b n -> p (b n)"), PAIR[0][:, 0:T],
                                   ACT.Copy).then_inc(s["vtm"], 1)
                if h is not None and j == 1:
                    for d in (0, 1):
                        step_done(act, h, 2 + d)
                        act.activation(kdtm[d][:, :, :].rearrange("p b n -> p (b n)"),
                                       PAIR[1 - d][:, 0:T], ACT.Copy).then_inc(s["kdtm"], 1)

        def states(dve, h, step):
            bank = 2 * ((step - 1) % 2)
            for d, cc, bk, pos in ds_place(step - 5, step - 5):
                i = ORDER[d].index(cc)
                to, new = sin[d][:, ORDER[d][i + 1], :], S[:, bank + bk, pos * P:(pos + 1) * P]
                own = s["sf" if d == 0 else "sb"]
                if i == 0:
                    dve.tensor_copy(to, new).then_inc(own, 1)
                else:
                    dve.wait_ge(own, 11 * h + i)
                    dve.scalar_tensor_tensor(to, sin[d][:, cc, :], gl[d][:, cc:cc + 1], new,
                                             ALU.mult, ALU.add).then_inc(own, 1)

        def hg_vector(dve, hg, hn_, hp, h, pn_par, ps_par):
            for j in range(5):
                if hg is not None:
                    pn = hg + j
                    split_lo(dve, pn + 2, KT)
                if h is not None and j == 0:
                    dve.wait_ge(s["ex"], 2 * h + 2)
                    dve.wait_ge(s["sig"], 4 * h + 4)
                    for d in (0, 1):
                        o = m["oml"][:, d, bass.ds(h, 1)]
                        dve.scalar_tensor_tensor(kd[d][:, :], kd[d][:, :], o, th[d][:, :], ALU.mult, ALU.mult)\
                            .then_inc(s["kd"], 1)
                    for d in (0, 1):
                        o = m["oml"][:, d, bass.ds(h, 1)]
                        dve.scalar_tensor_tensor(kr[d][:, :], kr[d][:, :], o, th[d][:, :], ALU.mult, ALU.mult)
                        dve.tensor_tensor(qr[d][:, :], qr[d][:, :], m["qs"][:, :], ALU.mult)
                        ins = dve.tensor_tensor(qe[d][:, :], qe[d][:, :], m["qs"][:, :], ALU.mult)
                    ins.then_inc(s["qk"], 1)
                if h is not None and j == 2:
                    step_done(dve, h, 4)
                    dve.memset(m["carry"][:, :], 0.0)
                    for d in (0, 1):
                        dve.copy_predicated(att[d][:, :, :], mask[d][:, :, :].bitcast(I32),
                                            PAIR[1][:, d * NBLK * CH:(d + 1) * NBLK * CH].rearrange("p (b l) -> p b l", l=CH))\
                            .then_inc(s["cp"], 1)
                    dve.wait_ge(s["cp"], 2 * h + 2)
                    dve.tensor_tensor(m["attS"][:, :, :], att[0][:, :, :], att[1][:, :, :], ALU.add)\
                        .then_inc(s["att"], 1)
                    for step in (5, 6):
                        step_done(dve, h, step)
                        states(dve, h, step)
                if h is not None and j == 3:
                    step_done(dve, h, 7)
                    states(dve, h, 7)
                if hg is not None and j == 3:
                    for d in (0, 1):
                        tl = hg + 2 + d
                        dve.wait_ge(took[tl.slot], tl.turn + 1)
                        dve.tensor_scalar(lf[d][:, :], th[d][:, :], 0.5, 0.5, ALU.mult, ALU.add)\
                            .then_inc(s["sig"], 1)
                    for d in (0, 1):
                        dve.wait_ge(s["sig"], 4 * hn_ + d + 1)
                        dve.tensor_scalar(th[d][:, :], th[d][:, :], -0.5, 0.5, ALU.mult, ALU.add)\
                            .then_inc(s["sig"], 1)
                if hg is not None and j == 4:
                    for d in (0, 1):
                        back = slice(None, None, -1 if d else 1)
                        dve.wait_ge(s["lf"], 2 * hn_ + d + 1)
                        dve.tensor_tensor_scan(cum[d][:, back], m["segm"][:, :], lf[d][:, back], 0.0,
                                               ALU.mult, ALU.add).then_inc(s["cum"], 1)
                    for d in (0, 1):
                        dve.wait_ge(s["cum"], 2 * hn_ + d + 1)
                        for to, t in ((kr, REF[d]), (kd, LAST[d])):
                            dve.tensor_tensor(chunks(to[d][:, :]), chunks(cum[d][:, :]),
                                              at_token(cum[d][:, :], t), ALU.subtract).then_inc(s["dif"], 1)
                if h is not None and j == 4:
                    step_done(dve, h, 9)
                    mean_dve(dve, NBLK, P)
                    dve.wait_ge(s["rbc"], h + 2)
                    dve.scalar_tensor_tensor(m["osb"][:, :], m["osb"][:, :], m["colA"][:, COL_GN:COL_GN + 1],
                                             PAIR[1][:, 0:T], ALU.mult, ALU.mult).then_inc(s["og0"], 1)
                    dve.wait_ge(s["og0"], h + 2)
                    dve.tensor_tensor(m["og"][:, bass.ds(h, 1), :].rearrange("p a t -> p (a t)"),
                                      m["osb"][:, :], gs[ps_par][:, :], ALU.mult).then_inc(s["og"], 1)

        def hg_all(eng, one):
            one(At(PAN_HG), 0, None, None, 0, 0)
            with eng.Fori(0, (HEADS - 2) // 2) as i:
                for u in (0, 1):
                    one(At(PAN_HG + 5 * (u + 1), i * 5), i * 2 + (u + 1), At(PAN_HG + 5 * u, i * 5), i * 2 + u,
                        1 - u, u)
            one(At(PAN_HG + 5 * (HEADS - 1)), HEADS - 1, At(PAN_HG + 5 * (HEADS - 2)), HEADS - 2, 1, 0)
            one(None, None, At(PAN_HG + 5 * (HEADS - 1)), HEADS - 1, 0, 1)

        def ffn_at(l, hf):
            return At((PAN_F0, PAN_F1)[l] + hf * (2 * FH + KT)), At((PAN_F0, TIL_F1)[l] + hf * (2 * FH + KT))

        def ffn_loop(eng, gate_up, down, l):
            for hf in (0, 1):
                pn, tl = ffn_at(l, hf)
                done_before = (2 * l + hf) * FH
                with eng.Fori(0, FH - 1) as i:
                    gate_up(At(pn.c, i), At(tl.c, i), i, i + done_before, KT, hf)
                gate_up(pn + 2 * (FH - 1), tl + 2 * (FH - 1), FH - 1, FH - 1 + done_before, FH, hf)
                pn, tl = pn + 2 * FH, tl + 2 * FH
                with eng.Fori(0, KT // 2 - 1) as i:
                    for u in (0, 1):
                        down(At(pn.c + u, i), At(tl.c + u, i), i * 2 + u, FH, hf)
                for j in (KT - 2, KT - 1):
                    ahead = KT if (l, hf) != (1, 1) else None
                    down(pn + j, tl + j, j, ahead, hf)

        def ffn_tensor(pe, l, segs):
            def gate_up(pn, tl, i, cnt, ahead, hf):
                norm = 1 + 2 * l
                first = isinstance(i, int)
                need = h_need(pe, norm) if hf == 0 else None
                product(pe, pn, tl, m["hhi"], m["hlo"], KT, segs, need=need)
                product(pe, pn + 1, tl + 1, m["hhi"], m["hlo"], KT, segs)

            def down(pn, tl, j, ahead, hf):
                product(pe, pn, tl, m["mhi"], m["mlo"], FH, segs,
                        need=lambda k: pe.wait_ge(s["mlo"], (2 * l + hf) * FH + k + 1))

            ffn_loop(pe, gate_up, down, l)

        def ffn_scalar(act, l, segs):
            nt = segs[-1][0] + segs[-1][1]

            def gate_up(pn, tl, i, cnt, ahead, hf):
                split_hi(act, pn + 2, ahead)
                act.activation(m["act0"][:, 0:nt], G[:, tl.slot, 0:nt], ACT.Silu).then_inc(took[tl.slot], 1)
                split_hi(act, pn + 3, ahead)
                up = tl + 1
                act.wait_ge(took[up.slot], up.turn + 1)
                act.activation(m["mhi"][:, bass.ds(i, 1), 0:nt].rearrange("p a t -> p (a t)"),
                               m["mid0"][:, 0:nt], ACT.Copy).then_inc(s["mhi"], 1)

            def down(pn, tl, j, ahead, hf):
                if ahead:
                    split_hi(act, pn + 2, ahead)

            ffn_loop(act, gate_up, down, l)

        def ffn_vector(dve, l, segs):
            nt = segs[-1][0] + segs[-1][1]

            def gate_up(pn, tl, i, cnt, ahead, hf):
                split_lo(dve, pn + 2, ahead)
                split_lo(dve, pn + 3, ahead)
                up = tl + 1
                dve.wait_ge(took[tl.slot], tl.turn + 1)
                dve.tensor_tensor(m["mid0"][:, 0:nt], m["act0"][:, 0:nt], G[:, up.slot, 0:nt], ALU.mult)\
                    .then_inc(took[up.slot], 1)
                dve.wait_ge(s["mhi"], cnt + 1)
                dve.tensor_tensor(m["mlo"][:, bass.ds(i, 1), 0:nt].rearrange("p a t -> p (a t)"),
                                  m["mid0"][:, 0:nt],
                                  f32(m["mhi"][:, bass.ds(i, 1), 0:nt]).rearrange("p a t -> p (a t)"),
                                  ALU.subtract).then_inc(s["mlo"], 1)
                dve.wait_ge(s["mlo"], cnt + 1)

            def down(pn, tl, j, ahead, hf):
                if ahead:
                    split_lo(dve, pn + 2, ahead)
                else:
                    done(dve, pn)
                add_gated(dve, tl, j, l, 5, segs)

            ffn_loop(dve, gate_up, down, l)

        def add_gated(dve, tl, j, l, part, segs):
            for g, (t0, n) in enumerate(segs):
                xj = m["x1"][:, bass.ds(j, 1), t0:t0 + n].rearrange("p a t -> p (a t)")
                gate = m["mods"][:, l, bass.ds(j + part * KT, 1), g:g + 1].rearrange("p a b -> p (a b)")
                ins = dve.scalar_tensor_tensor(xj, G[:, tl.slot, t0:t0 + n], gate, xj, ALU.mult, ALU.add)
            ins.then_inc(took[tl.slot], 1)

        def ffn_sync(sp, l):
            w_in, w_out = ffn_w_in[l], ffn_w_out[l]

            def gate_up(pn, tl, i, cnt, ahead, hf):
                load_panel(sp, pn, cols_of(w_in, i * P + hf * FH * P), KT)
                load_panel(sp, pn + 1, cols_of(w_in, i * P + (FFN + hf * FH * P)), KT)

            def down(pn, tl, j, ahead, hf):
                load_panel(sp, pn, cols_of(w_out[hf * FH * P:(hf + 1) * FH * P, :], j * P), FH)

            ffn_loop(sp, gate_up, down, l)

        def slabs(eng, one):
            for u in (0, 1):
                one(At(u), 0, u)
            with eng.Fori(1, 6) as i:
                for u in (0, 1):
                    one(At(u, i), 0, i * 2 + u)
            with eng.Fori(0, 6) as i:
                for u in (0, 1):
                    one(At(12 + u, i), 1, i * 2 + u)

        ada = (m["ada0"], m["ada1"])

        def slab_sync(sp):
            def one(n, l, cc):
                if n.past(2):
                    sp.wait_ge(s["modev"], n.n - 1)
                sp.dma_start(ada[n.slot][:, :, :],
                             ada_w[l][:, bass.ds(cc * 512, 512)].rearrange("(k p) n -> p k n", p=P))\
                    .then_inc(s[f"slab{n.slot}"], 16)
            slabs(sp, one)

        def slab_tensor(pe):
            def one(n, l, cc):
                pe.wait_ge(s[f"slab{n.slot}"], (n.turn + 1) * 16)
                if n.past(2):
                    pe.wait_ge(s["modev"], n.n - 1)
                for sub in range(4):
                    for k in range(KT):
                        ins = pe.matmul(S[:, n.slot, 2 * sub:2 * sub + 2],
                                        ada[n.slot][:, k, sub * P:(sub + 1) * P], m["csil"][:, k, :],
                                        start=(k == 0), stop=(k == KT - 1))
                ins.then_inc(s["ada"], 1)
            slabs(pe, one)

        def slab_vector(dve):
            def one(n, l, cc):
                dve.wait_ge(s["ada"], n.n + 1)
                bias = m["colB"][:, bass.ds(cc * 4 + l * 48, 4)].rearrange("p (t a) -> p t a", a=1)
                dve.tensor_tensor(m["mods"][:, l, bass.ds(cc * 4, 4), :],
                                  S[:, n.slot, 0:8].rearrange("p (t a) -> p t a", a=2),
                                  bias.to_broadcast([P, 4, 2]), ALU.add).then_inc(s["modev"], 1)
            slabs(dve, one)

        LAT = SEGS[:1]
        N2, K2 = 2, HEADS + 2
        xpad = (m["xpad0"], m["xpad1"])
        CONV_N = T + CONV_W // 2
        PANELS = [("z", i) for i in range(GT)] + [("b", 0), ("c", 0)] + [("x", i) for i in range(GT)]
        CONV_TILES = (DI + 2 * GROUPS * P) // P

        def ss_cols(kind, i, g):
            start = {"z": i * P, "b": BC0, "c": CC0, "x": XBC0 + i * P}[kind]
            return g * (P if kind in "bc" else GW) + start

        def conv_tile(kind, i, g):
            return {"x": g * GT + i, "b": g + NH // 2, "c": g + (NH // 2 + GROUPS)}[kind]

        def conv_to(kind, i):
            return {"b": m["bfm"][:, :], "c": m["cfm"][:, :]}[kind] if kind in "bc" else m["xfm"][:, i, :]

        def per_head(t, b, d, g):
            return t[:, b, bass.ds(g * HPG + d * NH, HPG)].rearrange("p (h a) -> p h a", a=1)\
                .to_broadcast([P, HPG, HP])

        def hd(ap):
            return ap.rearrange("p (h c) -> p h c", c=HP)

        def dt_scalar(act):
            act.wait_ge(s["parked1"], 16)
            pn = At(PAN_DT)
            split_hi(act, pn + 2, KT)
            zt, za, e, ln = (m[n] for n in ("xpad0", "xpad1", "acc", "bfm"))
            act.activation(zt[0:2 * NH, 0:T], G[P - 2 * NH:P, pn.slot, 0:T], ACT.Copy).then_inc(took[pn.slot], 1)
            act.wait_ge(s["small"], 64)
            act.activation(m["aneg"][:, 1:2], m["aneg"][:, 0:1], ACT.Exp).then_inc(s["dts"], 1)
            act.wait_ge(s["dtv"], 1)
            act.activation(e[0:2 * NH, 0:T], za[0:2 * NH, 0:T], ACT.Abs).then_inc(s["dts"], 1)
            act.wait_ge(s["dts"], 2)
            act.activation(zt[0:2 * NH, 0:T], e[0:2 * NH, 0:T], ACT.Exp, scale=-1.0).then_inc(s["dts"], 1)
            act.wait_ge(s["dts"], 3)
            act.activation(ln[0:2 * NH, 0:T], zt[0:2 * NH, 0:T], ACT.Ln, bias=1.0).then_inc(s["dts"], 1)
            act.wait_ge(s["dtv"], DT_D)
            act.activation(zt[0:2 * NH, 0:T], za[0:2 * NH, 0:T], ACT.Exp, scale=-1.0).then_inc(s["dts"], 1)
            act.wait_ge(s["pdt"], 1)
            act.activation(m["ecT"][:, :, :].rearrange("p b h -> p (b h)"), PAIR[0][:, 0:NBLK * 2 * NH], ACT.Exp)
            act.activation(m["ncumT"][:, :, :].rearrange("p b h -> p (b h)"), PAIR[0][:, 0:NBLK * 2 * NH],
                           ACT.Copy, scale=-1.0)
            act.activation(m["dtT"][:, :, :].rearrange("p b h -> p (b h)"),
                           PAIR[0][:, NBLK * 2 * NH:2 * NBLK * 2 * NH], ACT.Copy)
            act.activation(m["wT"][:, :, :].rearrange("p b h -> p (b h)"), PAIR[1][:, 0:NBLK * 2 * NH], ACT.Copy)
            act.activation(m["dec"][:, :, :].rearrange("p b h -> p (b h)"),
                           PAIR[1][:, NBLK * 2 * NH:2 * NBLK * 2 * NH], ACT.Exp).then_inc(s["dtT"], 1)

        DT_D = 17

        def dt_vector(dve):
            n = [0]

            def link(ins):
                n[0] += 1
                ins.then_inc(s["dtv"], 1)
                dve.wait_ge(s["dtv"], n[0])

            pn = At(PAN_DT)
            dve.wait_ge(s["parked1"], 16)
            split_lo(dve, pn + 2, KT)
            zt, z, e, ln, den, iz = (m[n_][0:2 * NH, 0:T] for n_ in ("xpad0", "xpad1", "acc", "bfm", "dt", "cumS"))
            t2 = m["cfm"][0:2 * NH, 0:T]
            dve.wait_ge(took[pn.slot], pn.turn + 1)
            dve.wait_ge(s["small"], 64)
            link(dve.tensor_scalar(z, zt, m["dtb"][:, 0:1], None, ALU.add))
            dve.wait_ge(s["dts"], 4)
            link(dve.tensor_scalar(den, zt, 1.0, -1.0, ALU.add, ALU.add))
            link(dve.tensor_scalar(iz, den, 0.0, None, ALU.is_equal))
            link(dve.tensor_tensor(den, den, iz, ALU.add))
            link(dve.reciprocal(t2, den))
            link(dve.tensor_tensor(t2, t2, zt, ALU.mult))
            link(dve.tensor_tensor(ln, ln, t2, ALU.mult))
            link(dve.tensor_tensor(t2, iz, zt, ALU.mult))
            link(dve.tensor_tensor(ln, ln, t2, ALU.add))
            link(dve.scalar_tensor_tensor(den, z, 0.0, ln, ALU.max, ALU.add))
            link(dve.tensor_scalar(m["aneg"][:, 2:3], m["aneg"][:, 1:2], -1.0, None, ALU.mult))
            link(dve.tensor_scalar(t2, den, m["aneg"][:, 2:3], None, ALU.mult))
            dve.wait_ge(s["negm"], 3)
            for d in (0, 1):
                r = slice(d * NH, (d + 1) * NH)
                back = slice(None, None, -1 if d else 1)
                link(dve.tensor_tensor_scan(m["cumS"][r, back], m["segm"][r, :], m["cfm"][r, back], 0.0,
                                            ALU.mult, ALU.add))
            cum3 = m["cumS"][:, :].rearrange("h (b t) -> h b t", t=P)
            for d in (0, 1):
                r = slice(d * NH, (d + 1) * NH)
                t = 0 if d else P - 1
                ins = dve.tensor_copy(m["cl"][r, :], cum3[r, :, t])
            link(ins)
            for d in (0, 1):
                r = slice(d * NH, (d + 1) * NH)
                ins = dve.tensor_tensor(m["xpad1"][r, 0:T].rearrange("h (b t) -> h b t", t=P), cum3[r, :, :],
                                        m["cl"][r, :].rearrange("h (b a) -> h b a", a=1).to_broadcast([NH, NBLK, P]),
                                        ALU.subtract)
                if d == 0:
                    link(ins)
            link(ins)
            assert n[0] == DT_D, n
            dve.wait_ge(s["dts"], 5)
            dve.tensor_tensor(zt, zt, den, ALU.mult).then_inc(s["ynorm"], 1)

        def dt_tensor(pe):
            pn = At(PAN_DT)
            product(pe, pn, pn, m["hhi"], m["hlo"], KT, SEGS, need=h_need(pe, N2))
            pe.wait_ge(s["ynorm"], 1)
            H2 = 2 * NH
            for i, src in enumerate(("cumS", "dt", "xpad0")):
                for b in range(NBLK):
                    pe.transpose(PAIR[i // 2][:, ((i % 2) * NBLK + b) * H2:((i % 2) * NBLK + b + 1) * H2],
                                 m[src][0:H2, b * P:(b + 1) * P], ident[0:H2, 0:H2])
            for b in range(NBLK):
                ins = pe.matmul(PAIR[1][:, (NBLK + b) * H2:(NBLK + b + 1) * H2],
                                m["cl"][:, b:b + 1].to_broadcast([H2, P]), ident[0:H2, 0:H2],
                                start=True, stop=True)
            ins.then_inc(s["pdt"], 1)

        CONVS = [(k, i) for k, i in PANELS if k != "z"]

        def ss_scalar(act, ss, g, q):
            def silu(ci, gg):
                kind, i = CONVS[ci]
                act.wait_ge(s["tap"], 24 * gg + 4 * ci + 4)
                to = conv_to(kind, i)
                act.activation(to[:, 0:NLAT], m["acc"][:, 0:NLAT], ACT.Silu)
                act.activation(to[:, NLAT:T], m["acc"][:, NLAT + 2:T + 2], ACT.Silu).then_inc(s["conv"], 1)

            for j, (kind, i) in enumerate(PANELS):
                if ss is not None:
                    pn = ss + j
                    split_hi(act, pn + 2, KT)
                    if kind == "z":
                        act.activation(m["z"][:, bass.ds(g % 2, 1), i, :].rearrange("p a t -> p (a t)"),
                                       G[:, pn.slot, 0:NLAT], ACT.Silu).then_inc(took[pn.slot], 1)
                    else:
                        ci = CONVS.index((kind, i))
                        xp = xpad[ci % 2]
                        act.activation(xp[:, 2:2 + NLAT], G[:, pn.slot, 0:NLAT], ACT.Copy)
                        act.activation(xp[:, 4 + NLAT:4 + T], G[:, pn.slot, NLAT:T], ACT.Copy)\
                            .then_inc(took[pn.slot], 1)
                        if ci:
                            silu(ci - 1, g)
                if j == 0 and q is not None:
                    silu(5, q)
                if ss is not None and kind != "z":
                    if ci:
                        act.wait_ge(s["conv"], 6 * g + ci)
                    act.wait_ge(took[pn.slot], pn.turn + 1)
                    ct = conv_tile(kind, i, g)
                    act.activation(m["acc"][:, :], xp[:, 0:T + 2], ACT.Identity,
                                   bias=m["colA"][:, bass.ds(ct + COL_CB, 1)],
                                   scale=m["colC"][:, bass.ds(ct, 1)]).then_inc(s["xp"], 1)
                if q is None:
                    continue
                if j == 1:
                    cnt = 6 * q
                    act.wait_ge(s["ytr"], cnt + 1)
                    act.activation(m["btm"][:, :, :].rearrange("p b n -> p (b n)"), PAIR[0][:, 0:T], ACT.Copy)\
                        .then_inc(s["stc"], 1)
                    act.wait_ge(s["ytr"], cnt + 2)
                    act.activation(m["cb"][:, :], S[:, 2, :], ACT.Copy).then_inc(s["stc"], 1)
                    for i_ in range(GT):
                        act.wait_ge(s["ytr"], cnt + 3 + i_)
                        act.activation(m["xtm"][:, :, i_ * P:(i_ + 1) * P],
                                       PAIR[i_ % 2][:, 0:T].rearrange("p (b n) -> p b n", n=P), ACT.Copy)\
                            .then_inc(s["stc"], 1)
                    act.wait_ge(s["yout"], 16 * q + 16)
                    for i_ in range(GT):
                        act.activation(m["yb"][:, i_, :], m["xfm"][:, i_, 0:NLAT], ACT.Identity,
                                       scale=m["dsk"][:, bass.ds(q * GT + i_, 1)])
                if 4 <= j < 8:
                    for hh in (2 * (j - 4), 2 * (j - 4) + 1):
                        r = hh % 2
                        act.wait_ge(s["sm"], HPG * q + hh + 1)
                        if hh >= 2:
                            act.wait_ge(s["yd"], HPG * q + hh - 1)
                        for d in (0, 1):
                            for b in range(LBLK):
                                ins = act.activation(block(m[f"e{d}{r}"][:, :], b), block(S[:, d, :], b), ACT.Exp,
                                                     bias=m["ncumT"][:, b, bass.ds(q * HPG + (d * NH + hh), 1)])
                        ins.then_inc(s["em"], 1)
                if j == 8:
                    for i_ in range(GT):
                        act.wait_ge(s["yz"], GT * q + i_ + 1)
                        if i_ >= 2:
                            act.wait_ge(s["yr"], GT * q + i_ - 1)
                        act.activation(m[f"sc{i_ % 2}"][:, :], m["yb"][:, i_, :], ACT.Square).then_inc(s["ysq"], 1)

        def ss_vector(dve, ss, g, q):
            for j, (kind, i) in enumerate(PANELS):
                if ss is not None:
                    pn = ss + j
                    split_lo(dve, pn + 2, KT)
                    if kind != "z":
                        ci = CONVS.index((kind, i))
                        ct = conv_tile(kind, i, g)
                        dve.wait_ge(s["xp"], 6 * g + ci + 1)
                        for k in range(1, CONV_W):
                            if k > 1:
                                dve.wait_ge(s["tap"], 24 * g + 4 * ci + k - 1)
                            dve.scalar_tensor_tensor(m["acc"][:, :], xpad[ci % 2][:, k:k + T + 2],
                                                     m["colC"][:, bass.ds(ct + k * CONV_TILES, 1)], m["acc"][:, :],
                                                     ALU.mult, ALU.add).then_inc(s["tap"], 1)
                if q is None:
                    continue
                if j == 0:
                    for d in (0, 1):
                        ins = dve.tensor_copy(m["sel"][:, d * HPG:(d + 1) * HPG],
                                              ident[0:2 * NH, bass.ds(q * HPG + d * NH, HPG)])
                    ins.then_inc(s["cbs"], 1)
                if j in (2, 3):
                    d = j - 2
                    ww = 5 * (2 * q + d)
                    st = (m["st0"], m["st1"])
                    for k in range(NBLK):
                        b = BORDER[d][k]
                        if k < NBLK - 1:
                            if k == 0 and d == 0:
                                dve.wait_ge(s["stc"], 6 * q + 6)
                            if k >= 2:
                                dve.wait_ge(s["ds"], ww + k - 1)
                            dve.tensor_tensor(hd(m[f"wx{k % 2}"][:, :]), hd(m["xtm"][:, b, :]),
                                              per_head(m["wT"], b, d, q), ALU.mult).then_inc(s["xw"], 1)
                        if b < LBLK:
                            yy = LBLK * (2 * q + d) + k - 2
                            dve.wait_ge(s["yo"], yy + 1)
                            if d == 0:
                                dve.tensor_tensor(hd(m["ytm"][:, b, :]), hd(S[:, 2 + k % 2, :]),
                                                  per_head(m["ecT"], b, d, q), ALU.mult).then_inc(s["ymc"], 1)
                            else:
                                dve.tensor_tensor(hd(m["sc0"][:, :]), hd(S[:, 2 + k % 2, :]),
                                                  per_head(m["ecT"], b, d, q), ALU.mult).then_inc(s["ymc"], 1)
                                dve.wait_ge(s["ymc"], 12 * q + 4 + 2 * (k - 2) + 1)
                                dve.tensor_tensor(m["ytm"][:, b, :], m["ytm"][:, b, :], m["sc0"][:, :], ALU.add)\
                                    .then_inc(s["ymc"], 1)
                                dve.wait_ge(s["ymc"], 12 * q + 4 + 2 * (k - 2) + 2)
                        if k < NBLK - 1:
                            dve.wait_ge(s["ds"], ww + k + 1)
                            new = S[:, k % 2, :]
                            if k == 0:
                                dve.tensor_copy(st[0][:, :], new).then_inc(s["dsm"], 1)
                            else:
                                dve.wait_ge(s["dsm"], 9 * (2 * q + d) + 2 * k - 1)
                                dve.tensor_tensor(hd(m["sc1"][:, :]), hd(st[(k - 1) % 2][:, :]),
                                                  per_head(m["dec"], b, d, q), ALU.mult).then_inc(s["dsm"], 1)
                                dve.wait_ge(s["dsm"], 9 * (2 * q + d) + 2 * k)
                                dve.tensor_tensor(st[k % 2][:, :], m["sc1"][:, :], new, ALU.add)\
                                    .then_inc(s["dsm"], 1)
                if 4 <= j < 8:
                    for hh in (2 * (j - 4), 2 * (j - 4) + 1):
                        r = hh % 2
                        dve.wait_ge(s["em"], HPG * q + hh + 1)
                        for d in (0, 1):
                            for b in range(LBLK):
                                e = block(m[f"e{d}{r}"][:, :], b)
                                ins = dve.scalar_tensor_tensor(
                                    e, e, m["dtT"][:, b, bass.ds(q * HPG + (d * NH + hh), 1)],
                                    block(m["cb"][:, :], b), ALU.mult, ALU.mult)
                        ins.then_inc(s["mm"], 1)
                        dve.wait_ge(s["mm"], 2 * (HPG * q + hh) + 1)
                        dve.tensor_tensor(m[f"e0{r}"][:, :], m[f"e0{r}"][:, :], m[f"e1{r}"][:, :], ALU.add)\
                            .then_inc(s["mm"], 1)
                        dve.wait_ge(s["yd"], HPG * q + hh + 1)
                        yt = m["ytm"][:, :, hh * HP:(hh + 1) * HP]
                        dve.tensor_tensor(yt, yt, S[:, 2 + r, 0:LBLK * HP].rearrange("p (b c) -> p b c", c=HP),
                                          ALU.add).then_inc(s["ym2"], 1)
                if j == 8:
                    for i_ in range(GT):
                        yb = m["yb"][:, i_, :]
                        dve.wait_ge(s["ytt"], GT * q + i_ + 1)
                        dve.tensor_tensor(yb, yb, S[:, i_, :], ALU.add).then_inc(s["ya"], 1)
                    for i_ in range(GT):
                        yb = m["yb"][:, i_, :]
                        dve.wait_ge(s["ya"], GT * q + i_ + 1)
                        dve.tensor_tensor(yb, yb, m["z"][:, bass.ds(q % 2, 1), i_, :].rearrange("p a t -> p (a t)"),
                                          ALU.mult).then_inc(s["yz"], 1)
                if j == 9:
                    dve.wait_ge(s["yr"], GT * q + GT)
                    mean_dve(dve, LBLK, GW)
                    dve.wait_ge(s["rbc"], q + (K2 + 2))
                    for i_ in range(GT):
                        yb = m["yb"][:, i_, :]
                        ins = dve.scalar_tensor_tensor(yb, yb, m["colA"][:, bass.ds(q * GT + (COL_SN + i_), 1)],
                                                       S[:, 1, :], ALU.mult, ALU.mult)
                    ins.then_inc(s["ynorm"], 1)

        def ss_tensor(pe, ss, g, q):
            for j, (kind, i) in enumerate(PANELS):
                if ss is not None:
                    product(pe, ss + j, ss + j, m["hhi"], m["hlo"], KT, LAT if kind == "z" else SEGS)
                if q is None:
                    continue
                if j == 1:
                    pe.wait_ge(s["conv"], 6 * q + 6)
                    pe.wait_ge(s["dtT"], 1)
                    pe.wait_ge(s["ynorm"], q + 1)
                    for b in range(NBLK):
                        ins = pe.transpose(block(PAIR[0], b), block(m["bfm"][:, :], b), ident[:, :])
                    ins.then_inc(s["ytr"], 1)
                    for b in range(LBLK):
                        ins = pe.matmul(block(S[:, 2, :], b), block(m["bfm"][:, :], b), block(m["cfm"][:, :], b),
                                        start=True, stop=True)
                    ins.then_inc(s["ytr"], 1)
                    for i_ in range(GT):
                        pe.wait_ge(s["stc"], 6 * q + 1 + i_)
                        for b in range(NBLK):
                            ins = pe.transpose(block(PAIR[i_ % 2], b), block(m["xfm"][:, i_, :], b), ident[:, :])
                        ins.then_inc(s["ytr"], 1)
                if j in (2, 3):
                    d = j - 2
                    ww = 5 * (2 * q + d)
                    st = (m["st0"], m["st1"])
                    if d == 0:
                        pe.wait_ge(s["stc"], 6 * q + 6)
                    for k in range(NBLK):
                        b = BORDER[d][k]
                        if b < LBLK:
                            pe.wait_ge(s["dsm"], 9 * (2 * q + d) + 2 * k - 1)
                            if k >= 4:
                                pe.wait_ge(s["ymc"], 12 * q + (k - 3 if d == 0 else 4 + 2 * (k - 3)))
                            elif d == 1:
                                pe.wait_ge(s["ymc"], 12 * q + 4)
                            pe.matmul(S[:, 2 + k % 2, :], block(m["cfm"][:, :], b), st[(k - 1) % 2][:, :],
                                      start=True, stop=True).then_inc(s["yo"], 1)
                        if k < NBLK - 1:
                            pe.wait_ge(s["xw"], ww + k + 1)
                            if k >= 2:
                                pe.wait_ge(s["dsm"], 9 * (2 * q + d) + 2 * k - 3)
                            elif d == 1:
                                pe.wait_ge(s["dsm"], 9 * (2 * q + d))
                            pe.matmul(S[:, k % 2, :], m["btm"][:, b, :], m[f"wx{k % 2}"][:, :],
                                      start=True, stop=True).then_inc(s["ds"], 1)
                if 4 <= j < 8:
                    for hh in (2 * (j - 4), 2 * (j - 4) + 1):
                        heads_seg(pe, q, hh)
                        if hh:
                            heads_y(pe, q, hh - 1)
                    if j == 7:
                        heads_y(pe, q, HPG - 1)
                if j == 8:
                    pe.wait_ge(s["ym2"], HPG * q + HPG)
                    for i_ in range(GT):
                        for b in range(LBLK):
                            ins = pe.transpose(block(S[:, i_, :], b), m["ytm"][:, b, i_ * P:(i_ + 1) * P], ident[:, :])
                        ins.then_inc(s["ytt"], 1)
                if j == 9:
                    pe.wait_ge(s["ya"], GT * q + GT)
                    for i_ in range(GT):
                        pe.wait_ge(s["ysq"], GT * q + i_ + 1)
                        for b in range(LBLK):
                            ins = pe.matmul(S[:, 0, b:b + 1], block(m[f"sc{i_ % 2}"][:, :], b), ones[:, :],
                                            start=(i_ == 0 and b == 0), stop=(i_ == GT - 1),
                                            skip_group_check=True)
                        ins.then_inc(s["yr"], 1)
                    spread_pe(pe, q + (K2 + 1), LBLK, S[:, 1, :])

        def heads_seg(pe, q, hh):
            if hh == 0:
                pe.wait_ge(s["dsm"], 9 * (2 * q + 2))
                pe.wait_ge(s["cbs"], q + 1)
            else:
                pe.wait_ge(s["em"], HPG * q + hh)
            for d in (0, 1):
                pe.matmul(S[:, d, :], m["sel"][:, d * HPG + hh:d * HPG + hh + 1].to_broadcast([2 * NH, P]),
                          m["cumS"][:, 0:NLAT], start=True, stop=False)
                ins = pe.matmul(S[:, d, :], m["identb"][:, :], m[f"neg{d}"][:, :], start=False, stop=True)
            ins.then_inc(s["sm"], 1)

        def heads_y(pe, q, hh):
            r = hh % 2
            pe.wait_ge(s["mm"], 2 * (HPG * q + hh) + 2)
            if hh < 2:
                pe.wait_ge(s["ymc"], 12 * q + 12)
            else:
                pe.wait_ge(s["ym2"], HPG * q + hh - 1)
            for b in range(LBLK):
                ins = pe.matmul(S[:, 2 + r, b * HP:(b + 1) * HP], block(m[f"e0{r}"][:, :], b),
                                m["xtm"][:, b, hh * HP:(hh + 1) * HP], start=True, stop=True)
            ins.then_inc(s["yd"], 1)

        def ss_all(eng, one):
            one(At(PAN_SS), 0, None)
            with eng.Fori(0, GROUPS - 1) as i:
                one(At(PAN_SS + 10, i * 5), i + 1, i)
            one(None, None, GROUPS - 1)

        def so_pairs(eng, one):
            with eng.Fori(0, KT // 2) as i:
                for u in (0, 1):
                    for half in (0, 1):
                        one(At(PAN_SO + 2 * u + half, i * 2), At(TIL_SO + u, i), i * 2 + u, half)

        ymid_hi = m["mhi"][:, :, :].rearrange("p f t -> p (f t)")[:, 0:2 * KT * NLAT].rearrange("p (k t) -> p k t", t=NLAT)
        ymid_lo = m["mlo"][:, :, :].rearrange("p f t -> p (f t)")[:, 0:2 * KT * NLAT].rearrange("p (k t) -> p k t", t=NLAT)
        yin = (m["act0"], m["act1"])

        def l1_sync(sp):
            load_panel(sp, At(PAN_DT), cols_of(ssm_w_in[0], SSM_IN - P), KT)

            def loads(ss, g, q):
                if ss is not None:
                    for j, (kind, i) in enumerate(PANELS):
                        load_panel(sp, ss + j, cols_of(ssm_w_in[0], ss_cols(kind, i, g)), KT)
            ss_all(sp, loads)

            def so(pn, tl, j, half):
                load_panel(sp, pn, cols_of(ssm_w_out[0][half * D:(half + 1) * D, :], j * P), KT)
            so_pairs(sp, so)
            ffn_sync(sp, 1)
            for b in range(LBLK):
                sp.wait_ge(s["fo"], KT)
                sp.dma_start(out[0, b * P:(b + 1) * P, :], m["ofin"][:, b, :]).then_inc(s["outd"], 16)
            sp.wait_ge(s["outd"], 16 * LBLK)

        def l1_pool(pool):
            for j in (KT - 2, KT - 1):
                tile_ready(ffn_at(0, 1)[1] + 2 * FH)(pool, j)
            pool.dma_start(x_park, m["x1"][:, :, 0:NLAT]).then_inc(s["parked1"], 16)
            rsqrt_pool(pool, K2, NBLK)
            pool.wait_ge(s["parked1"], 16)
            for d in (0, 1):
                pool.dma_start(m["dtb"][d * NH:(d + 1) * NH, 0:1], ssm_dt_bias[0, d].rearrange("(h a) -> h a", a=1))\
                    .then_inc(s["small"], 16)
                pool.dma_start(m["aneg"][d * NH:(d + 1) * NH, 0:1], ssm_a_log[0, d].rearrange("(h a) -> h a", a=1))\
                    .then_inc(s["small"], 16)
            pool.dma_start(m["dall"][:, :], ssm_d.to_broadcast([P, NH])).then_inc(s["yout"], 16)
            pool.wait_ge(s["yout"], 16)
            for q in (0, 1):
                pool.tensor_copy(m["dsk"][q * HP:(q + 1) * HP, :], m["dall"][q * HP:(q + 1) * HP, q::2])\
                    .then_inc(s["dskin"], 1)
                pool.wait_ge(s["dskin"], q + 1)
            pool.memset(chunks(m["segm"][:, :])[:, 1::2, 0:1], 1.0).then_inc(s["negm"], 1)
            pool.wait_ge(s["hlo"], 8 * (N2 + 1))
            for d in (0, 1):
                pool.memset(m[f"neg{d}"][:, :], 0.0).then_inc(s["negz"], 1)
                pool.wait_ge(s["negz"], d + 1)
                v = m[f"neg{d}"][:, :].rearrange("p (b t) -> p b t", t=P)
                pool.affine_select(out=v, in_=v, compare_op=ALU.is_ge, fill=-1e30, base=0,
                                   pattern=[[0, LBLK], [1 - 2 * d, P]], channel_multiplier=2 * d - 1)\
                    .then_inc(s["negm"], 1)
            pool.wait_ge(s["dtT"], 1)
            for i, xp in enumerate(xpad):
                for j, (c0, c1) in enumerate(((0, 2), (2 + NLAT, 4 + NLAT), (4 + T, 8 + T))):
                    pool.memset(xp[:, c0:c1], 0.0).then_inc(s["halo"], 1)
            for g in range(GROUPS):
                rsqrt_pool(pool, K2 + 1 + g, LBLK)
                pool.wait_ge(s["ynorm"], g + 2)
                pool.dma_start(y_park[g], m["yb"][:, :, :]).then_inc(s["yout"], 16)
            pool.wait_ge(s["yout"], 16 * GROUPS + 16)
            pool.dma_start(m["x1"][:, :, 0:NLAT], x_park).then_inc(s["back1"], 16)
            for k in range(2 * KT):
                if k >= 2:
                    pool.wait_ge(s["yl"], k - 1)
                pool.dma_start(yin[k % 2][:, 0:NLAT], y_park[k // GT, :, k % GT, :]).then_inc(s[f"yin{k % 2}"], 16)
            rsqrt_pool(pool, K2 + 1 + GROUPS, LBLK)
            rsqrt_pool(pool, K2 + 2 + GROUPS, LBLK)

        def l1_scalar(act):
            norm_act(act, m["x1"], N2, SEGS, tile_ready(ffn_at(0, 1)[1] + 2 * FH), 1, 0)
            dt_scalar(act)
            act.wait_ge(s["halo"], 6)
            act.wait_ge(s["dskin"], 2)
            ss_all(act, lambda *a: ss_scalar(act, *a))
            for k in range(2 * KT):
                act.wait_ge(s[f"yin{k % 2}"], 16 * (k // 2 + 1))
                act.activation(ymid_hi[:, k, :], yin[k % 2][:, 0:NLAT], ACT.Copy).then_inc(s["yh"], 1)
            so_pairs(act, lambda pn, tl, j, half: split_hi(act, pn + 2, KT))
            norm_act(act, m["x1"], 3, LAT, tile_ready(At(TIL_SO)), 1, 1)
            ffn_scalar(act, 1, LAT)
            squares_act(act, m["x1"], 4, LAT, tile_ready(ffn_at(1, 1)[1] + 2 * FH))
            for j in range(KT):
                act.wait_ge(s["ft"], j + 1)
                act.activation(m["ofin"][:, :, j * P:(j + 1) * P],
                               Gq[:, j % 4, :].rearrange("p (b f) -> p b f", f=P), ACT.Copy).then_inc(s["fo"], 1)

        def l1_vector(dve):
            norm_dve(dve, m["x1"], N2, K2, SEGS, 1, 0)
            dt_vector(dve)
            ss_all(dve, lambda *a: ss_vector(dve, *a))
            for k in range(2 * KT):
                dve.wait_ge(s["yh"], k + 1)
                dve.tensor_tensor(ymid_lo[:, k, :], yin[k % 2][:, 0:NLAT], f32(ymid_hi[:, k, :]), ALU.subtract)\
                    .then_inc(s["yl"], 1)
            dve.wait_ge(s["back1"], 16)

            def so(pn, tl, j, half):
                split_lo(dve, pn + 2, KT)
                if half:
                    add_gated(dve, tl, j, 1, 2, LAT)
            so_pairs(dve, so)
            norm_dve(dve, m["x1"], 3, K2 + 1 + GROUPS, LAT, 1, 1)
            ffn_vector(dve, 1, LAT)
            dve.wait_ge(s["sqd"], 8 * 5)
            mean_dve(dve, LBLK, D)
            dve.wait_ge(s["rbc"], K2 + 3 + GROUPS)
            for j in range(KT):
                if j >= 2:
                    dve.wait_ge(s["ft"], j - 1)
                dve.scalar_tensor_tensor(hn[j % 2][:, 0:NLAT], m["x1"][:, j, 0:NLAT],
                                         m["colA"][:, COL_FIN + j:COL_FIN + j + 1], PAIR[1][:, 0:NLAT],
                                         ALU.mult, ALU.mult).then_inc(s["fn"], 1)

        def l1_tensor(pe):
            norm_pe(pe, N2, K2, NBLK)
            dt_tensor(pe)
            ss_all(pe, lambda *a: ss_tensor(pe, *a))

            def so(pn, tl, j, half):
                product(pe, pn, tl, ymid_hi, ymid_lo, KT, LAT, k_base=half * KT, first=(half == 0),
                        last=(half == 1), need=lambda k: pe.wait_ge(s["yl"], half * KT + k + 1))
            so_pairs(pe, so)
            norm_pe(pe, 3, K2 + 1 + GROUPS, LBLK)
            ffn_tensor(pe, 1, LAT)
            norm_pe(pe, 4, K2 + 2 + GROUPS, LBLK)
            for j in range(KT):
                pe.wait_ge(s["fn"], j + 1)
                if j >= 4:
                    pe.wait_ge(s["fo"], j - 3)
                for b in range(LBLK):
                    ins = pe.transpose(block(Gq[:, j % 4, :], b), block(hn[j % 2][:, 0:NLAT], b), ident[:, :])
                ins.then_inc(s["ft"], 1)

        block_ = ctx.enter_context(nc.Block())

        @block_.sync
        def _(sp):
            rows = ((m["rowA"], COL_NORM, norm_w.rearrange("l i (j p) -> (l i j) p", p=P)),
                    (m["rowA"], COL_FIN, final_norm_w.rearrange("(j p) -> j p", p=P)),
                    (m["rowA"], COL_C, c.rearrange("b (j p) -> (b j) p", p=P)),
                    (m["rowA"], COL_CC, c_ctx.rearrange("(j p) -> j p", p=P)),
                    (m["rowA"], COL_SN, ssm_norm_w.rearrange("b (j p) -> (b j) p", p=P)),
                    (m["rowA"], COL_CB, ssm_conv_b.rearrange("b (j p) -> (b j) p", p=P)),
                    (m["rowA"], COL_GN, hg_norm_w),
                    (m["rowB"], 0, ada_b.rearrange("l (t p) -> (l t) p", p=P)),
                    (m["rowC"], 0, ssm_conv_w.rearrange("b k (t p) -> (b k t) p", p=P)),
                    (m["rowD"], 0, hg_lb.rearrange("d r (h p) -> (d r h) p", p=P)))
            for to, r0, src in rows:
                sp.dma_start(to[r0:r0 + src.shape[0], :], src).then_inc(s["rows"], 16)
            for b in range(NBLK):
                src = x[0] if b < LBLK else ctx_x[0]
                b0 = b if b < LBLK else b - LBLK
                sp.dma_start(m["xin"][:, b, :], src[b0 * P:(b0 + 1) * P, :]).then_inc(s["xin"], 16)
            slab_sync(sp)

            def hg_loads(hg, hn_, hp, h, pn_par, ps_par):
                if hg is not None:
                    for j, off in enumerate(HG_OFF):
                        load_panel(sp, hg + j, cols_of(hg_w_in[0], hn_ * P + off), KT)
            hg_all(sp, hg_loads)
            with sp.Fori(0, KT // 2) as i:
                for u in (0, 1):
                    load_panel(sp, At(PAN_HGO + u, i), cols_of(hg_w_out[0], i * 2 * P + u * P), KT)
            ffn_sync(sp, 0)
            l1_sync(sp)

        @block_.gpsimd
        def _(pool):
            n = [0]

            def link(ins):
                n[0] += 1
                ins.then_inc(s["ps"], 1)
                pool.wait_ge(s["ps"], n[0])

            link(pool.memset(ident[:, :], 0.0))
            pool.affine_select(out=ident[:, :], in_=ident[:, :], compare_op=ALU.not_equal, fill=1.0, base=0,
                               pattern=[[-1, P]], channel_multiplier=1).then_inc(s["ident"], 1)
            pool.wait_ge(s["ident"], 1)
            link(pool.memset(ones[:, :], 1.0))
            link(pool.memset(m["mhalf"][:, :], -0.5))
            link(pool.memset(m["segm"][:, :], 1.0))
            link(pool.memset(chunks(m["segm"][:, :])[:, :, 0:1], 0.0))
            for d in (0, 1):
                link(pool.memset(mask[d][:, :, :], 1.0))
                for o in (0, CH):
                    link(pool.affine_select(out=mask[d][o:o + CH, :, :], in_=mask[d][o:o + CH, :, :],
                                            compare_op=ALU.is_ge, fill=0.0, base=0,
                                            pattern=[[0, NBLK], [1 - 2 * d, CH]], channel_multiplier=2 * d - 1))
            pool.tensor_copy(m["identb"][:, :], ident[:, :]).then_inc(s["const"], 1)
            pool.wait_ge(s["const"], 1)
            rsqrt_pool(pool, 0, NBLK)
            pool.wait_ge(s["x"], NBLK * 2)
            pool.dma_start(x_park0, m["x0"][:, :, :]).then_inc(s["parked0"], 16)
            for h in range(HEADS):
                rsqrt_pool(pool, h + 1, NBLK)
            pool.wait_ge(s["og"], HEADS)
            pool.wait_ge(s["parked0"], 16)
            pool.dma_start(m["x1"][:, :, :], x_park0).then_inc(s["back0"], 16)
            rsqrt_pool(pool, HEADS + 1, NBLK)
            l1_pool(pool)

        @block_.scalar
        def _(act):
            act.wait_ge(s["cols"], 1)
            for i, col in ((0, COL_C), (1, COL_CC)):
                ins = act.activation(m["csil"][:, :, i], m["colA"][:, col:col + KT], ACT.Silu)
            ins.then_inc(s["csil"], 1)
            act.wait_ge(s["tdve"], 3)
            act.activation(m["lbe"][:, :, :, :], m["lbe"][:, :, :, :], ACT.Exp).then_inc(s["lbs"], 1)
            split_hi(act, At(0), KT)
            split_hi(act, At(1), KT)
            norm_act(act, m["x0"], 0, SEGS, x_loaded, 0, 0)
            hg_all(act, lambda *a: hg_scalar(act, *a))
            act.wait_ge(s["og"], HEADS)
            for j in range(HEADS):
                act.activation(m["hhi"][:, j, :], m["og"][:, j, :], ACT.Copy).then_inc(s["osp_hi"], 1)
            with act.Fori(0, KT // 2) as i:
                for u in (0, 1):
                    split_hi(act, At(PAN_HGO + 2 + u, i), KT)
            norm_act(act, m["x1"], 1, SEGS, tile_ready(At(PAN_HGO)), 0, 1)
            ffn_scalar(act, 0, SEGS)
            l1_scalar(act)

        @block_.vector
        def _(dve):
            n = [0]

            def link(ins):
                n[0] += 1
                ins.then_inc(s["tdve"], 1)
                dve.wait_ge(s["tdve"], n[0])

            dve.wait_ge(s["tpe"], 1)
            dve.tensor_copy(m["colA"][:, :], S[:, 2, 0:97]).then_inc(s["cols"], 1)
            dve.tensor_copy(m["colB"][:, :], S[:, 2, 128:224])
            dve.tensor_copy(m["colC"][:, :], S[:, 2, 256:376])
            dve.tensor_copy(m["colD"][:, :, :, :].rearrange("p d r h -> p (d r h)"), S[:, 2, 384:432])\
                .then_inc(s["cols"], 1)
            dve.wait_ge(s["cols"], 2)
            D3, lbt, lbe = m["colD"], m["lbt"], m["lbe"]
            link(dve.tensor_tensor(lbt[:, :, :], D3[:, :, 0, :], D3[:, :, 1, :], ALU.max))
            link(dve.tensor_tensor(lbt[:, :, :], lbt[:, :, :], D3[:, :, 2, :], ALU.max))
            for r in range(3):
                ins = dve.tensor_tensor(lbe[:, :, r, :], D3[:, :, r, :], lbt[:, :, :], ALU.subtract)
            link(ins)
            for u in range(2 * NBLK):
                b, q = u // 2, u % 2
                dve.wait_ge(s["xt"], u + 1)
                dve.tensor_copy(m["x0"][:, 4 * q:4 * q + 4, b * P:(b + 1) * P],
                                Gq[:, u % 4, :].rearrange("p (j t) -> p j t", j=4)).then_inc(s["x"], 1)
            dve.wait_ge(s["lbs"], 1)
            link(dve.tensor_tensor(lbt[:, :, :], lbe[:, :, 0, :], lbe[:, :, 1, :], ALU.add))
            link(dve.tensor_tensor(lbt[:, :, :], lbt[:, :, :], lbe[:, :, 2, :], ALU.add))
            link(dve.reciprocal(lbt[:, :, :], lbt[:, :, :]))
            link(dve.tensor_tensor(m["lb"][:, :, :], lbe[:, :, 0, :], lbt[:, :, :], ALU.mult))
            link(dve.tensor_scalar(m["oml"][:, :, :], m["lb"][:, :, :], -1.0, 1.0, ALU.mult, ALU.add))
            slab_vector(dve)
            dve.wait_ge(s["modev"], 24)
            for l in (0, 1):
                for i in (0, 1):
                    w = m["colA"][:, (l * 2 + i) * KT:(l * 2 + i + 1) * KT].rearrange("p (t a) -> p t a", a=1)
                    ins = dve.scalar_tensor_tensor(m["afac"][:, l, i, :, :],
                                                   m["mods"][:, l, (3 * i + 1) * KT:(3 * i + 2) * KT, :], 1.0,
                                                   w.to_broadcast([P, KT, 2]), ALU.add, ALU.mult)
            ins.then_inc(s["afac"], 1)
            split_lo(dve, At(0), KT)
            split_lo(dve, At(1), KT)
            dve.wait_ge(s["afac"], 1)
            norm_dve(dve, m["x0"], 0, 0, SEGS, 0, 0)
            for d in (0, 1):
                ins = dve.memset(att[d][:, :, :], 0.0)
            ins.then_inc(s["og0"], 1)
            dve.wait_ge(s["og0"], 1)
            dve.wait_ge(s["const"], 1)
            dve.wait_ge(s["parked0"], 16)
            hg_all(dve, lambda *a: hg_vector(dve, *a))
            for j in range(HEADS):
                dve.wait_ge(s["osp_hi"], j + 1)
                dve.tensor_tensor(m["hlo"][:, j, :], m["og"][:, j, :], f32(m["hhi"][:, j, :]), ALU.subtract)\
                    .then_inc(s["osp_lo"], 1)
            dve.wait_ge(s["back0"], 16)
            with dve.Fori(0, KT // 2) as i:
                for u in (0, 1):
                    split_lo(dve, At(PAN_HGO + 2 + u, i), KT)
                    add_gated(dve, At(PAN_HGO + u, i), i * 2 + u, 0, 2, SEGS)
            norm_dve(dve, m["x1"], 1, HEADS + 1, SEGS, 0, 1)
            ffn_vector(dve, 0, SEGS)
            l1_vector(dve)

        @block_.tensor
        def _(pe):
            pe.wait_ge(s["ident"], 1)
            pe.wait_ge(s["rows"], 160)
            for name, n, at in (("rowA", 97, 0), ("rowB", 96, 128), ("rowC", 120, 256), ("rowD", 48, 384)):
                ins = pe.transpose(S[:, 2, at:at + n], m[name][:, :], ident[0:n, 0:n])
            ins.then_inc(s["tpe"], 1)
            pe.wait_ge(s["xin"], 16 * NBLK)
            for u in range(2 * NBLK):
                b, q = u // 2, u % 2
                if u >= 4:
                    pe.wait_ge(s["x"], u - 3)
                for j in range(4):
                    ins = pe.transpose(Gq[:, u % 4, j * P:(j + 1) * P],
                                       m["xin"][:, b, (4 * q + j) * P:(4 * q + j + 1) * P], ident[:, :])
                ins.then_inc(s["xt"], 1)
            pe.wait_ge(s["csil"], 1)
            slab_tensor(pe)
            pe.wait_ge(s["const"], 1)
            pe.wait_ge(s["modev"], 24)
            norm_pe(pe, 0, 0, NBLK)
            hg_all(pe, lambda *a: hg_tensor(pe, *a))
            with pe.Fori(0, KT // 2) as i:
                for u in (0, 1):
                    pn = At(PAN_HGO + u, i)
                    product(pe, pn, pn, m["hhi"], m["hlo"], KT, SEGS,
                            need=lambda k: pe.wait_ge(s["osp_lo"], k + 1))
            norm_pe(pe, 1, HEADS + 1, NBLK)
            ffn_tensor(pe, 0, SEGS)
            l1_tensor(pe)


_INS = ["x", "c", "ctx", "c_ctx", "ada_w", "ada_b", "norm_w", "ffn_w_in", "ffn_w_out", "final_norm_w", "hg_w_in",
        "hg_lb", "hg_norm_w", "hg_w_out", "ssm_w_in", "ssm_conv_w", "ssm_conv_b", "ssm_dt_bias", "ssm_a_log",
        "ssm_d", "ssm_norm_w", "ssm_w_out"]


def kernel(**inputs):
    import numpy as _np
    import concourse.bacc as _bacc
    from concourse.bass_utils import run_bass_kernel_spmd as _run

    nc = _bacc.Bacc("TRN2", target_bir_lowering=False, num_devices=1)
    arrays, args = {}, []
    for name in _INS:
        a = _np.ascontiguousarray(inputs[name])
        arrays[f"in_{name}_dram"] = a
        args.append(nc.dram_tensor(f"in_{name}_dram", a.shape, mybir.dt.from_np(a.dtype), kind="ExternalInput").ap())
    args.append(nc.dram_tensor("out_0_dram", (1, NLAT, D), F32, kind="ExternalOutput").ap())
    program(nc, *args)
    r = _run(nc, [arrays], core_ids=[0])
    return r.results[0]["out_0_dram"]
```

```python
from contextlib import ExitStack

import concourse.bass as bass
from concourse import mybir

F32 = mybir.dt.float32
F32R = mybir.dt.float32r
BF16 = mybir.dt.bfloat16
I32 = mybir.dt.int32
ALU = mybir.AluOpType
ACT = mybir.ActivationFunctionType

P = 128
D = 1024
KT = D // P
NLAT, NCTX = 512, 256
T = NLAT + NCTX
NBLK = T // P
LBLK = NLAT // P
EPS = 1e-6
SEGS = ((0, NLAT), (NLAT, NCTX))

HEADS = 8
CH = 64
NCH = T // CH
LAT_CH = NLAT // CH
ORDER = (list(range(LAT_CH, NCH)) + list(range(LAT_CH)), list(range(NCH - 1, -1, -1)))
REF = (CH // 2 - 1, CH // 2)
LAST = (CH - 1, 0)

FFN = 2816
FH = FFN // P // 2

DI = 2048
GROUPS = 4
HPG = 8
HP = 64
NH = GROUPS * HPG
GW = DI // GROUPS
GT = GW // P
CONV_W = 5
XBC0 = DI
BC0, CC0 = XBC0 + DI, XBC0 + DI + GROUPS * P
SSM_IN = CC0 + GROUPS * P + 2 * NH
BORDER = ([4, 5, 0, 1, 2, 3], [5, 4, 3, 2, 1, 0])

PAN_HG = 0
PAN_HGO = PAN_HG + 5 * HEADS
PAN_F0 = PAN_HGO + KT
PAN_DT = PAN_F0 + 2 * (2 * FH + KT)
PAN_SS = PAN_DT + 1
PAN_SO = PAN_SS + 10 * GROUPS
PAN_F1 = PAN_SO + 2 * KT
PAN_END = PAN_F1 + 2 * (2 * FH + KT)
TIL_SO = PAN_SO
TIL_F1 = TIL_SO + KT

SLAB = 2 * P
FIRST_SLABS = 2 * D // 512
SL_HG = 0
SL_HGO = SL_HG + 2 * HEADS
SL_F0 = SL_HGO + KT // 2
assert SLAB * SL_HGO == 4 * D and (SL_F0 - SL_HGO + 2 * (FH - 1)) * SLAB == 6 * D

COL_NORM, COL_FIN, COL_C, COL_CC, COL_SN, COL_CB, COL_GN = 0, 32, 40, 48, 56, 72, 96


class At:

    def __init__(self, c, half=0):
        self.c, self.half = c, half

    def __add__(self, n):
        return At(self.c + n, self.half)

    @property
    def slot(self):
        return self.c % 2

    @property
    def turn(self):
        return self.half + self.c // 2

    @property
    def n(self):
        return self.half * 2 + self.c

    def past(self, k):
        return not isinstance(self.half, int) or self.n >= k


def memory(nc):
    m, m_at = {}, {}
    base, limit = 16512, 229344

    def run(at, *items):
        for name, shape, *dt in items:
            dt = dt[0] if dt else F32
            n = 2 if dt == BF16 else 4
            for d in shape[1:]:
                n *= d
            end = at + (n + 31) // 32 * 32
            assert end <= limit, (name, end)
            m_at[name] = at
            m[name] = nc.alloc_sbuf_tensor_at(name, list(shape), dt, offset=at)
            at = end
        return at

    R = run(base,
            ("ident", (P, P)), ("ones", (P, 1)), ("mhalf", (P, 8)), ("carry", (P, 1)), ("csil", (P, KT, 2)),
            ("colA", (P, 97)), ("colB", (P, 96)), ("colC", (P, 120)), ("mods", (P, 2, 48, 2)), ("afac", (P, 2, 2, KT, 2)),
            ("stat", (P, 8)), ("rstd", (P, 8)), ("lb", (P, 2, HEADS)), ("oml", (P, 2, HEADS)),
            ("segm", (P, T)), ("mask0", (P, NBLK, CH), I32), ("mask1", (P, NBLK, CH), I32),
            *[(f"raw{i}", (P, FH, P)) for i in (0, 1)],
            *[(f"w{w}{i}", (P, FH, P), F32R) for i in (0, 1) for w in ("hi", "lo")],
            ("hhi", (P, KT, T), F32R), ("hlo", (P, KT, T), F32R))
    W = 4 * T
    N = limit - 4 * W
    run(N, *[(f"{n}{i}", (P, T)) for n in ("sq", "hn") for i in (0, 1)])
    assert run(R, ("x0", (P, KT, T)), ("xin", (P, NBLK, D)), ("ada0", (P, KT, 512)), ("ada1", (P, KT, 512)),
               ("rowA", (97, P)), ("rowB", (96, P)), ("rowC", (120, P)), ("rowD", (48, P)),
               ("colD", (P, 2, 3, HEADS)),
               ("lbt", (P, 2, HEADS)), ("lbe", (P, 2, 3, HEADS))) <= N
    run(R, ("og", (P, HEADS, T)),
        *[(f"{n}{d}", (P, T)) for n in ("kr", "qr", "qe", "kd", "th", "lf", "cum", "gs") for d in (0, 1)],
        *[(n, (P, T)) for n in ("qs", "vT", "osb", "osq")],
        *[(n, (P, NBLK, P)) for n in ("vtm", "kdtm0", "kdtm1")],
        *[(n, (P, NBLK, CH)) for n in ("att0", "att1", "attS")],
        *[(f"sin{d}", (P, NCH, P)) for d in (0, 1)], *[(f"gl{d}", (P, NCH)) for d in (0, 1)],
        ("adaw", (P, KT, SLAB)))
    at_raw = m_at["raw0"] + 4 * KT * P
    run(at_raw, ("mrow0", (2, SLAB)))
    assert run(R, ("mhi", (P, FH, T), F32R), ("x1", (P, KT, T)), ("mlo", (P, FH, T), F32R),
               ("act0", (P, T)), ("act1", (P, T)), ("mid0", (P, T)), ("mid1", (P, T)), ("mrow1", (2, SLAB))) <= N
    run(R, *[(n, (2 * NH, NBLK)) for n in ("cl", "dtb", "aneg")], ("dt", (2 * NH, T)), ("cumS", (2 * NH, T)),
        *[(n, (P, NBLK, 2 * NH)) for n in ("ncumT", "dtT", "wT", "ecT", "dec")],
        ("sel", (2 * NH, 2 * HPG)), ("identb", (P, P), BF16), ("neg0", (P, NLAT), BF16), ("neg1", (P, NLAT), BF16), ("dsk", (P, NH // 2)), ("dall", (P, NH)),
        ("z", (P, 2, GT, NLAT)), ("xpad0", (P, T + 8)), ("xpad1", (P, T + 8)), ("acc", (P, T + 2)),
        ("bfm", (P, T)), ("cfm", (P, T)), ("xfm", (P, GT, T)), ("btm", (P, NBLK, P)), ("xtm", (P, NBLK, GW)),
        ("cb", (P, NLAT)), *[(f"e{d}{i}", (P, NLAT)) for d in (0, 1) for i in (0, 1)],
        ("wx0", (P, GW)), ("wx1", (P, GW)), ("st0", (P, GW)), ("st1", (P, GW)),
        ("sc0", (P, GW)), ("sc1", (P, GW)), ("yb", (P, GT, NLAT)), ("ytm", (P, LBLK, GW)))
    run(R, ("ofin", (P, LBLK, D)))
    return m


def program(nc, x, c, ctx_x, c_ctx, ada_w, ada_b, norm_w, ffn_w_in, ffn_w_out, final_norm_w, hg_w_in, hg_lb,
            hg_norm_w, hg_w_out, ssm_w_in, ssm_conv_w, ssm_conv_b, ssm_dt_bias, ssm_a_log, ssm_d, ssm_norm_w,
            ssm_w_out, out):
    with ExitStack() as ctx:
        m = memory(nc)
        G = ctx.enter_context(nc.psum_tensor("G", [P, 2, 1024], F32))
        S = ctx.enter_context(nc.psum_tensor("S", [P, 4, 512], F32))
        Gq = G[:, :, :].rearrange("p s (h n) -> p (s h) n", h=2)
        Sf = S[:, :, :].rearrange("p b n -> p (b n)")
        PAIR = (Sf[:, 0:1024], Sf[:, 1024:2048])
        x_park = nc.dram_tensor("x_park", (P, KT, NLAT), F32, kind="Internal").ap()
        x_park0 = nc.dram_tensor("x_park0", (P, KT, T), F32, kind="Internal").ap()
        y_park = nc.dram_tensor("y_park", (GROUPS, P, GT, NLAT), F32, kind="Internal").ap()

        names = """rows xin adain slab0 slab1 raw0 raw1 small parked0 back0 parked1 back1 yout yin0 yin1 outd
            ident cols tpe tdve ada modev modl afac csil lbs hi lo pan took0 took1
            x sq sqd stat rstd rbc hn hhi hlo rused
            sig lf cum dif ex kd qk vtm kdtm step cp att sf sb osq og0 og osp_hi osp_lo
            act mid mhi mlo
            dskin negz halo dtv dts pdt dtT negm xt eq xp tap conv ytr stc sm em cbs mm yo yd xw ds stf stb ymc ym2
            ytt ya yz ysq yr ynorm yh yl fn ft fo ps""".split()
        s = {n: ctx.enter_context(nc.semaphore("s_" + n)) for n in names}
        took = (s["took0"], s["took1"])
        raw, whi, wlo = ([m[f"{n}{i}"] for i in (0, 1)] for n in ("raw", "whi", "wlo"))
        sq, hn = ([m[f"{n}{i}"] for i in (0, 1)] for n in ("sq", "hn"))
        ident, ones = m["ident"], m["ones"]

        def f32(ap):
            return ap.bitcast(F32)

        def mod(l, part, j, seg):
            return m["mods"][:, l, part * KT + j, seg:seg + 1]

        def block(ap, b):
            return ap[:, b * P:(b + 1) * P]

        def cols_of(w, off):
            return w[:, bass.ds(off, P)].rearrange("(k p) n -> p k n", p=P)

        HG_OFF = [0, 4 * D, D, 2 * D, 3 * D]

        def load_panel(sp, pn, src, kt):
            if pn.past(2):
                sp.wait_ge(s["lo"], pn.n - 1)
            sp.dma_start(raw[pn.slot][:, 0:kt, :], src).then_inc(s[f"raw{pn.slot}"], 16)

        def split_hi(act, pn, kt):
            act.wait_ge(s[f"raw{pn.slot}"], (pn.turn + 1) * 16)
            if pn.past(2):
                act.wait_ge(s["pan"], pn.n - 1)
            act.activation(whi[pn.slot][:, 0:kt, :], raw[pn.slot][:, 0:kt, :], ACT.Copy).then_inc(s["hi"], 1)

        def split_lo(dve, pn, kt):
            dve.wait_ge(s["hi"], pn.n + 1)
            dve.tensor_tensor(wlo[pn.slot][:, 0:kt, :], raw[pn.slot][:, 0:kt, :],
                              f32(whi[pn.slot][:, 0:kt, :]), ALU.subtract).then_inc(s["lo"], 1)

        def product(pe, pn, tl, rhi, rlo, kt, segs, k_base=0, first=True, last=True, need=None,
                    rows=None, turn=None, between=None):
            pe.wait_ge(s["lo"], pn.n + 1)
            if first and tl.past(2):
                pe.wait_ge(took[tl.slot], tl.turn)
            for k in range(kt):
                if need is not None:
                    need(k)
                if turn is not None and k == kt - 1:
                    prev = tl + (-1)
                    pe.wait_ge(took[prev.slot], prev.turn + 1)
                for i, (w, r) in enumerate(((whi, rhi), (whi, rlo), (wlo, rhi))):
                    for t0, n in segs:
                        ins = pe.matmul(G[:, tl.slot, t0:t0 + n], w[pn.slot][:, k, :],
                                        r[:, k_base + k, t0:t0 + n],
                                        start=(first and k == 0 and i == 0),
                                        stop=(last and k == kt - 1 and i == 2))
                if between is not None:
                    between(k)
            if rows is not None:
                ins = slab_rows(pe, tl, rows)
            if turn is not None:
                ins = slab_turn(pe, tl, turn)
            ins.then_inc(s["pan"], 1)

        def slab_load(sp, a, l, col, before, norms=1):
            src = ada_w[l][:, bass.ds(col, SLAB)].rearrange("(k p) n -> p k n", p=P)
            sp.wait_ge(s["hlo"], 8 * norms)
            if before is not None:
                sp.wait_ge(s["pan"], before.n + 1)
            sp.dma_start(m["adaw"][:, :, :], src).then_inc(s["adain"], 16)

        def slab_rows(pe, tl, a):
            pe.wait_ge(s["adain"], a * 16 + 16)
            for k in range(KT):
                ins = pe.matmul(G[0:2, tl.slot, T:T + SLAB], m["csil"][:, k, :], m["adaw"][:, k, :],
                                start=(k == 0), stop=(k == KT - 1))
            return ins

        def slab_turn(pe, tl, row):
            for b in (0, 1):
                ins = pe.transpose(G[:, tl.slot, T + 2 * b:T + 2 * b + 2], block(row[:, :], b), ident[0:2, 0:2])
            return ins

        def mods_at(l, t):
            return m["mods"][:, l, bass.ds(t, 2), :]

        def slab_out(dve, tl, l, t):
            bias = m["colB"][:, bass.ds(t + l * 48, 2)].rearrange("p (t a) -> p t a", a=1)
            return dve.tensor_tensor(mods_at(l, t), G[:, tl.slot, T:T + 4].rearrange("p (t a) -> p t a", a=2),
                                     bias.to_broadcast([P, 2, 2]), ALU.add)

        def done(eng, pn):
            eng.wait_ge(s["pan"], pn.n + 1)

        def squares_act(act, xt, N, segs, ready):
            nt = segs[-1][0] + segs[-1][1]
            for j in range(KT):
                ready(act, j)
                if 8 * N + j >= 2:
                    act.wait_ge(s["sqd"], 8 * N + j - 1)
                act.activation(sq[j % 2][:, 0:nt], xt[:, j, 0:nt], ACT.Square).then_inc(s["sq"], 1)

        def norm_act(act, xt, N, segs, ready, l, i):
            squares_act(act, xt, N, segs, ready)
            for j in range(KT):
                act.wait_ge(s["hn"], 8 * N + j + 1)
                for g, (t0, n) in enumerate(segs):
                    ins = act.activation(m["hhi"][:, j, t0:t0 + n], hn[j % 2][:, t0:t0 + n], ACT.Identity,
                                         bias=mod(l, 3 * i, j, g))
                ins.then_inc(s["hhi"], 1)

        def norm_pe(pe, N, K, nb):
            for j in range(KT):
                pe.wait_ge(s["sq"], 8 * N + j + 1)
                for b in range(nb):
                    ins = pe.matmul(S[:, 0, b:b + 1], block(sq[j % 2], b), ones[:, :],
                                    start=(j == 0 and b == 0), stop=(j == KT - 1), skip_group_check=True)
                ins.then_inc(s["sqd"], 1)
            spread_pe(pe, K, nb, PAIR[1])

        def spread_pe(pe, K, nb, to):
            pe.wait_ge(s["rstd"], K + 1)
            for b in range(nb):
                ins = pe.matmul(block(to, b), m["rstd"][:, b:b + 1].to_broadcast([P, P]), ident[:, :],
                                start=True, stop=True)
            ins.then_inc(s["rbc"], 1)

        def mean_dve(dve, nb, n):
            dve.tensor_scalar(m["stat"][:, 0:nb], S[:, 0, 0:nb], 1.0 / n, EPS, ALU.mult, ALU.add)\
               .then_inc(s["stat"], 1)

        def rsqrt_pool(pool, K, nb):
            pool.wait_ge(s["stat"], K + 1)
            pool.tensor_tensor(m["rstd"][:, 0:nb], m["stat"][:, 0:nb], m["mhalf"][:, 0:nb], ALU.pow)\
                .then_inc(s["rstd"], 1)

        def factors(dve, l, i):
            w = m["colA"][:, (l * 2 + i) * KT:(l * 2 + i + 1) * KT].rearrange("p (t a) -> p t a", a=1)
            dve.scalar_tensor_tensor(m["afac"][:, l, i, :, :], m["mods"][:, l, (3 * i + 1) * KT:(3 * i + 2) * KT, :],
                                     1.0, w.to_broadcast([P, KT, 2]), ALU.add, ALU.mult).then_inc(s["afac"], 1)
            dve.wait_ge(s["afac"], 2 * l + i + 1)

        def norm_dve(dve, xt, N, K, segs, l, i):
            dve.wait_ge(s["sqd"], 8 * (N + 1))
            mean_dve(dve, (segs[-1][0] + segs[-1][1]) // P, D)
            dve.wait_ge(s["rbc"], K + 1)

            def scaled(j):
                if j >= 2:
                    dve.wait_ge(s["hlo"], 8 * N + j - 1)
                for g, (t0, n) in enumerate(segs):
                    ins = dve.scalar_tensor_tensor(hn[j % 2][:, t0:t0 + n], xt[:, j, t0:t0 + n],
                                                   m["afac"][:, l, i, j, g:g + 1], PAIR[1][:, t0:t0 + n],
                                                   ALU.mult, ALU.mult)
                ins.then_inc(s["hn"], 1)

            def low(j):
                dve.wait_ge(s["hhi"], 8 * N + j + 1)
                for g, (t0, n) in enumerate(segs):
                    ins = dve.scalar_tensor_tensor(m["hlo"][:, j, t0:t0 + n], hn[j % 2][:, t0:t0 + n],
                                                   mod(l, 3 * i, j, g), f32(m["hhi"][:, j, t0:t0 + n]),
                                                   ALU.add, ALU.subtract)
                ins.then_inc(s["hlo"], 1)

            for j in range(KT + 1):
                if j < KT:
                    scaled(j)
                if j:
                    low(j - 1)

        def h_need(pe, N):
            return lambda k: pe.wait_ge(s["hlo"], 8 * N + k + 1)

        def tile_ready(base):
            def ready(eng, j):
                tl = base + j
                eng.wait_ge(took[tl.slot], tl.turn + 1)
            return ready

        def x_loaded(eng, j):
            eng.wait_ge(s["x"], NBLK * 2)

        heads = HEADS
        th, lf, cum, kr, qr, qe, kd, gs, sin, gl, att, kdtm, mask = (
            [m[f"{n}{d}"] for d in (0, 1)]
            for n in ("th", "lf", "cum", "kr", "qr", "qe", "kd", "gs", "sin", "gl", "att", "kdtm", "mask"))

        def chunks(ap):
            return ap.rearrange("p (c l) -> p c l", l=CH)

        def by_parity(buf):
            return buf[:, :].rearrange("p (b q l) -> p q b l", q=2, l=CH)

        def at_token(ap, t):
            return chunks(ap)[:, :, t:t + 1].to_broadcast([P, NCH, CH])

        def ds_place(d, step):
            if step == 2:
                lot = [(0, c) for c in ORDER[0][8:-1]] + [(1, c) for c in ORDER[1][8:-1]]
            else:
                lot = [(d, c) for c in ORDER[d][:8]]
            seen, res = [0, 0], []
            for dd, cc in lot:
                res.append((dd, cc, cc % 2, seen[cc % 2]))
                seen[cc % 2] += 1
            return res

        def hg_tensor_scan(pe, hp, h, step):
            pair = PAIR[(step - 1) % 2]
            bank = 2 * ((step - 1) % 2)
            if step == 1:
                pe.wait_ge(s["og0"], h + 1)
                v = hp + 4
                pe.wait_ge(took[v.slot], v.turn + 1)
                for b in range(NBLK):
                    ins = pe.transpose(block(pair, b), block(m["vT"][:, :], b), ident[:, :])
            elif step in (2, 3):
                d = step - 2
                if step == 3:
                    pe.wait_ge(s["vtm"], h + 1)
                pe.wait_ge(s["kd"], 2 * h + d + 1)
                for b in range(NBLK):
                    ins = pe.transpose(block(pair, b), block(kd[d][:, :], b), ident[:, :])
            elif step == 4:
                pe.wait_ge(s["kdtm"], 2 * h + 1)
                pe.wait_ge(s["qk"], h + 1)
                H2 = CH // 2
                for d in (0, 1):
                    for c in range(NCH):
                        col, kc, qc = (NBLK * d + c // 2) * CH, chunks(kr[d][:, :])[:, c, :], chunks(qr[d][:, :])[:, c, :]
                        for half in (0, 1):
                            o = CH * (c % 2) + H2 * half
                            q0, q1 = (0, CH) if half == d else (H2 * half, H2 * half + H2)
                            ins = pe.matmul(pair[o:o + H2, col + q0:col + q1],
                                            kc[:, H2 * half:H2 * half + H2], qc[:, q0:q1],
                                            start=True, stop=True)
            elif step in (5, 6, 7):
                if step == 5:
                    pe.wait_ge(s["kdtm"], 2 * h + 2)
                elif step == 6:
                    pe.wait_ge(s["cp"], 2 * h + 2)
                else:
                    pe.wait_ge(s["sf"], 11 * h + 8)
                for d, cc, bk, pos in ds_place(step - 5, step - 5):
                    o = CH * (cc % 2)
                    ins = pe.matmul(S[:, bank + bk, pos * P:(pos + 1) * P], kdtm[d][o:o + CH, cc // 2, :],
                                    m["vtm"][o:o + CH, cc // 2, :], start=True, stop=True)
            elif step == 8:
                pe.wait_ge(s["sf"], 11 * h + 11)
                pe.wait_ge(s["sb"], 11 * h + 11)
                pe.wait_ge(s["att"], h + 1)
                for c in range(NCH):
                    o = CH * (c % 2)
                    to = S[:, bank + c % 2, (c // 2) * CH:(c // 2 + 1) * CH]
                    inter = [d for d in (0, 1) if c != ORDER[d][0]]
                    pe.matmul(to, m["vtm"][o:o + CH, c // 2, :], m["attS"][o:o + CH, c // 2, :],
                              start=True, stop=False)
                    for d in inter:
                        ins = pe.matmul(to, sin[d][:, c, :], chunks(qe[d][:, :])[:, c, :],
                                        start=False, stop=(d == inter[-1]))
            elif step == 9:
                pe.wait_ge(s["osq"], h + 1)
                for b in range(NBLK):
                    ins = pe.matmul(S[:, 0, b:b + 1], block(m["osq"][:, :], b), ones[:, :],
                                    start=True, stop=True)
            else:
                spread_pe(pe, h + 1, NBLK, pair)
                return
            ins.then_inc(s["step"], 1)

        STEP_AT = {(0, 5): 1, (1, 0): 2, (1, 3): 3, (1, 6): 4, (2, 1): 5, (2, 3): 6, (2, 6): 7, (3, 3): 8,
                   (3, 7): 9, (4, 1): 10}

        def hg_tensor(pe, hg, hn_, hp, h, pn_par, ps_par):
            def scan(j, k):
                if h is not None and (j, k) in STEP_AT:
                    hg_tensor_scan(pe, hp, h, STEP_AT[j, k])

            for j in range(5):
                if hg is not None:
                    pn = hg + j
                    product(pe, pn, pn, m["hhi"], m["hlo"], KT, SEGS,
                            need=h_need(pe, 0) if h is None and j == 0 else None,
                            rows=hn_ * 2 + j // 2 if j in (0, 2) else None,
                            turn=m["mrow0"] if j in (1, 3) else None, between=lambda k: scan(j, k))
                else:
                    for k in range(KT):
                        scan(j, k)

        def step_done(eng, h, step):
            eng.wait_ge(s["step"], 9 * h + step)

        def hg_scalar(act, hg, hn_, hp, h, pn_par, ps_par):
            def take(pn, j):
                split_hi(act, pn + 2, KT)
                tile = G[:, pn.slot, 0:T]
                if j == 0:
                    if h is not None:
                        act.wait_ge(s["qk"], hn_)
                    ins = act.activation(m["qs"][:, :], tile, ACT.Silu)
                elif j == 1:
                    ins = act.activation(gs[pn_par][:, :], tile, ACT.Silu)
                elif j in (2, 3):
                    ins = act.activation(th[j - 2][:, :], tile, ACT.Tanh, scale=0.5)
                else:
                    ins = act.activation(m["vT"][:, :], tile, ACT.Copy)
                if j in (0, 2):
                    ins = act.activation(m["mrow0"][:, :], G[0:2, pn.slot, T:T + SLAB], ACT.Copy)
                elif j in (1, 3):
                    for b in (0, 1):
                        t = hn_ * 4 + ((j - 1) + b)
                        ins = act.activation(m["mods"][:, 0, bass.ds(t + 2 * KT, 1), :].rearrange("p a c -> p (a c)"),
                                             G[:, pn.slot, T + 2 * b:T + 2 * b + 2], ACT.Identity,
                                             bias=m["colB"][:, bass.ds(t + 2 * KT, 1)])
                ins.then_inc(took[pn.slot], 1)

            def decays(head, d):
                act.wait_ge(s["dif"], 4 * head + 2 * d + 1)
                act.activation(qr[d][:, :], kr[d][:, :], ACT.Exp).then_inc(s["eq"], 1)
                act.activation(qe[d][:, :], cum[d][:, :], ACT.Exp)
                act.activation(gl[d][:, :], chunks(cum[d][:, :])[:, :, LAST[d]], ACT.Exp)
                act.wait_ge(s["dif"], 4 * head + 2 * d + 2)
                act.activation(kd[d][:, :], kd[d][:, :], ACT.Exp, scale=-1.0)
                act.wait_ge(s["eq"], 2 * head + d + 1)
                act.activation(kr[d][:, :], kr[d][:, :], ACT.Exp, scale=-1.0).then_inc(s["ex"], 1)

            for j in range(5):
                if j and hg is not None:
                    take(hg + (j - 1), j - 1)
                if j == 0 and h is not None:
                    take(hp + 4, 4)
                    decays(h, 1)
                    step_done(act, h, 1)
                    act.activation(m["vtm"][:, :, :].rearrange("p b n -> p (b n)"), PAIR[0][:, 0:T],
                                   ACT.Copy).then_inc(s["vtm"], 1)
                if j == 1 and h is not None:
                    for d in (0, 1):
                        step_done(act, h, 2 + d)
                        act.activation(kdtm[d][:, :, :].rearrange("p b n -> p (b n)"),
                                       PAIR[1 - d][:, 0:T], ACT.Copy).then_inc(s["kdtm"], 1)
                if j == 3 and h is not None:
                    step_done(act, h, 8)
                    o4 = S[:, 2:4, 0:NBLK * CH].rearrange("p q (b l) -> p q b l", l=CH)
                    act.activation(by_parity(m["osb"]), o4, ACT.Copy)
                    act.activation(by_parity(m["osq"]), o4, ACT.Square).then_inc(s["osq"], 1)
                if j == 4 and hg is not None:
                    for d in (0, 1):
                        act.wait_ge(s["sig"], 4 * hn_ + d + 1)
                        act.activation(lf[d][:, :], lf[d][:, :], ACT.Ln, bias=m["lb"][:, d, bass.ds(hn_, 1)],
                                       scale=m["oml"][:, d, bass.ds(hn_, 1)]).then_inc(s["lf"], 1)
                    decays(hn_, 0)

        def states(dve, h, step):
            bank = 2 * ((step - 1) % 2)
            for d, cc, bk, pos in ds_place(step - 5, step - 5):
                i = ORDER[d].index(cc)
                to, new = sin[d][:, ORDER[d][i + 1], :], S[:, bank + bk, pos * P:(pos + 1) * P]
                own = s["sf" if d == 0 else "sb"]
                if i == 0:
                    dve.tensor_copy(to, new).then_inc(own, 1)
                else:
                    dve.wait_ge(own, 11 * h + i)
                    dve.scalar_tensor_tensor(to, sin[d][:, cc, :], gl[d][:, cc:cc + 1], new,
                                             ALU.mult, ALU.add).then_inc(own, 1)

        def hg_vector(dve, hg, hn_, hp, h, pn_par, ps_par):
            for j in range(5):
                if j and hg is not None:
                    split_lo(dve, hg + (j + 1), KT)
                if j == 0 and h is not None:
                    split_lo(dve, hp + 6, KT)
                    dve.wait_ge(s["sig"], 4 * h + 4)
                    for d in (0, 1):
                        dve.wait_ge(s["ex"], 2 * h + d + 1)
                        o = m["oml"][:, d, bass.ds(h, 1)]
                        dve.scalar_tensor_tensor(kd[d][:, :], kd[d][:, :], o, th[d][:, :], ALU.mult, ALU.mult)\
                            .then_inc(s["kd"], 1)
                        dve.scalar_tensor_tensor(kr[d][:, :], kr[d][:, :], o, th[d][:, :], ALU.mult, ALU.mult)
                        dve.tensor_tensor(qr[d][:, :], qr[d][:, :], m["qs"][:, :], ALU.mult)
                        ins = dve.tensor_tensor(qe[d][:, :], qe[d][:, :], m["qs"][:, :], ALU.mult)
                    ins.then_inc(s["qk"], 1)
                if j == 1 and h is not None:
                    step_done(dve, h, 4)
                    dve.memset(m["carry"][:, :], 0.0)
                    for d in (0, 1):
                        dve.copy_predicated(att[d][:, :, :], mask[d][:, :, :].bitcast(I32),
                                            PAIR[1][:, d * NBLK * CH:(d + 1) * NBLK * CH].rearrange("p (b l) -> p b l", l=CH))\
                            .then_inc(s["cp"], 1)
                    dve.wait_ge(s["cp"], 2 * h + 2)
                    dve.tensor_tensor(m["attS"][:, :, :], att[0][:, :, :], att[1][:, :, :], ALU.add)\
                        .then_inc(s["att"], 1)
                if j == 2 and h is not None:
                    for step in (5, 6, 7):
                        step_done(dve, h, step)
                        states(dve, h, step)
                if j == 3 and h is not None:
                    step_done(dve, h, 9)
                    mean_dve(dve, NBLK, P)
                if j == 4 and hg is not None:
                    for d in (0, 1):
                        tl = hg + 2 + d
                        dve.wait_ge(took[tl.slot], tl.turn + 1)
                        dve.tensor_scalar(lf[d][:, :], th[d][:, :], 0.5, 0.5, ALU.mult, ALU.add)\
                            .then_inc(s["sig"], 1)
                    for d in (0, 1):
                        dve.wait_ge(s["sig"], 4 * hn_ + d + 1)
                        dve.tensor_scalar(th[d][:, :], th[d][:, :], -0.5, 0.5, ALU.mult, ALU.add)\
                            .then_inc(s["sig"], 1)
                if j == 4 and h is not None:
                    dve.wait_ge(s["rbc"], h + 2)
                    dve.scalar_tensor_tensor(m["osb"][:, :], m["osb"][:, :], m["colA"][:, COL_GN:COL_GN + 1],
                                             PAIR[1][:, 0:T], ALU.mult, ALU.mult).then_inc(s["og0"], 1)
                if j == 4 and hg is not None:
                    for d in (0, 1):
                        back = slice(None, None, -1 if d else 1)
                        dve.wait_ge(s["lf"], 2 * hn_ + d + 1)
                        dve.tensor_tensor_scan(cum[d][:, back], m["segm"][:, :], lf[d][:, back], 0.0,
                                               ALU.mult, ALU.add).then_inc(s["cum"], 1)
                    for d in (0, 1):
                        dve.wait_ge(s["cum"], 2 * hn_ + d + 1)
                        for to, t in ((kr, REF[d]), (kd, LAST[d])):
                            dve.tensor_tensor(chunks(to[d][:, :]), chunks(cum[d][:, :]),
                                              at_token(cum[d][:, :], t), ALU.subtract).then_inc(s["dif"], 1)
                if j == 4 and h is not None:
                    dve.wait_ge(s["og0"], h + 2)
                    dve.tensor_tensor(m["og"][:, bass.ds(h, 1), :].rearrange("p a t -> p (a t)"),
                                      m["osb"][:, :], gs[ps_par][:, :], ALU.mult).then_inc(s["og"], 1)

        def hg_all(eng, one):
            one(At(PAN_HG), 0, None, None, 0, 0)
            with eng.Fori(0, (HEADS - 2) // 2) as i:
                for u in (0, 1):
                    one(At(PAN_HG + 5 * (u + 1), i * 5), i * 2 + (u + 1), At(PAN_HG + 5 * u, i * 5), i * 2 + u,
                        1 - u, u)
            one(At(PAN_HG + 5 * (HEADS - 1)), HEADS - 1, At(PAN_HG + 5 * (HEADS - 2)), HEADS - 2, 1, 0)
            one(None, None, At(PAN_HG + 5 * (HEADS - 1)), HEADS - 1, 0, 1)

        def ffn_at(l, hf):
            return At((PAN_F0, PAN_F1)[l] + hf * (2 * FH + KT)), At((PAN_F0, TIL_F1)[l] + hf * (2 * FH + KT))

        def ffn_loop(eng, gate_up, down, l):
            for hf in (0, 1):
                pn, tl = ffn_at(l, hf)
                done_before = (2 * l + hf) * FH
                with eng.Fori(0, FH - 1) as i:
                    gate_up(At(pn.c, i), At(tl.c, i), i, i + done_before, KT, hf)
                gate_up(pn + 2 * (FH - 1), tl + 2 * (FH - 1), FH - 1, FH - 1 + done_before, FH, hf)
                pn, tl = pn + 2 * FH, tl + 2 * FH
                with eng.Fori(0, KT // 2 - 1) as i:
                    for u in (0, 1):
                        down(At(pn.c + u, i), At(tl.c + u, i), i * 2 + u, FH, hf)
                for j in (KT - 2, KT - 1):
                    ahead = KT if (l, hf) != (1, 1) else None
                    down(pn + j, tl + j, j, ahead, hf)

        def ffn_tensor(pe, l, segs):
            def gate_up(pn, tl, i, cnt, ahead, hf):
                norm = 1 + 2 * l
                peeled = isinstance(i, int)
                need = h_need(pe, norm) if hf == 0 else None
                slab = l == 0 and not peeled
                product(pe, pn, tl, m["hhi"], m["hlo"], KT, segs, need=need,
                        rows=i + (SL_F0 + hf * (FH - 1)) if slab else None)
                product(pe, pn + 1, tl + 1, m["hhi"], m["hlo"], KT, segs,
                        turn=m["mrow1"] if slab else None)

            def down(pn, tl, j, ahead, hf):
                product(pe, pn, tl, m["mhi"], m["mlo"], FH, segs,
                        need=lambda k: pe.wait_ge(s["mlo"], (2 * l + hf) * FH + k + 1))

            ffn_loop(pe, gate_up, down, l)

        def ffn_scalar(act, l, segs):
            nt = segs[-1][0] + segs[-1][1]

            def gate_up(pn, tl, i, cnt, ahead, hf):
                split_hi(act, pn + 2, ahead)
                ins = act.activation(m["act0"][:, 0:nt], G[:, tl.slot, 0:nt], ACT.Silu)
                if l == 0 and not isinstance(i, int):
                    ins = act.activation(m["mrow1"][:, :], G[0:2, tl.slot, T:T + SLAB], ACT.Copy)
                ins.then_inc(took[tl.slot], 1)
                split_hi(act, pn + 3, ahead)
                up = tl + 1
                act.wait_ge(took[up.slot], up.turn + 1)
                act.activation(m["mhi"][:, bass.ds(i, 1), 0:nt].rearrange("p a t -> p (a t)"),
                               m["mid0"][:, 0:nt], ACT.Copy).then_inc(s["mhi"], 1)

            def down(pn, tl, j, ahead, hf):
                if ahead:
                    split_hi(act, pn + 2, ahead)

            ffn_loop(act, gate_up, down, l)

        def ffn_vector(dve, l, segs):
            nt = segs[-1][0] + segs[-1][1]

            def gate_up(pn, tl, i, cnt, ahead, hf):
                split_lo(dve, pn + 2, ahead)
                split_lo(dve, pn + 3, ahead)
                up = tl + 1
                dve.wait_ge(took[tl.slot], tl.turn + 1)
                if l == 0 and not isinstance(i, int):
                    slab_out(dve, up, 1, i * 2 + 2 * (SL_F0 - SL_HGO + hf * (FH - 1)))
                dve.tensor_tensor(m["mid0"][:, 0:nt], m["act0"][:, 0:nt], G[:, up.slot, 0:nt], ALU.mult)\
                    .then_inc(took[up.slot], 1)
                dve.wait_ge(s["mhi"], cnt + 1)
                dve.tensor_tensor(m["mlo"][:, bass.ds(i, 1), 0:nt].rearrange("p a t -> p (a t)"),
                                  m["mid0"][:, 0:nt],
                                  f32(m["mhi"][:, bass.ds(i, 1), 0:nt]).rearrange("p a t -> p (a t)"),
                                  ALU.subtract).then_inc(s["mlo"], 1)
                dve.wait_ge(s["mlo"], cnt + 1)

            def down(pn, tl, j, ahead, hf):
                if ahead:
                    split_lo(dve, pn + 2, ahead)
                else:
                    done(dve, pn)
                add_gated(dve, tl, j, l, 5, segs)

            ffn_loop(dve, gate_up, down, l)

        def add_gated(dve, tl, j, l, part, segs):
            for g, (t0, n) in enumerate(segs):
                xj = m["x1"][:, bass.ds(j, 1), t0:t0 + n].rearrange("p a t -> p (a t)")
                gate = m["mods"][:, l, bass.ds(j + part * KT, 1), g:g + 1].rearrange("p a b -> p (a b)")
                ins = dve.scalar_tensor_tensor(xj, G[:, tl.slot, t0:t0 + n], gate, xj, ALU.mult, ALU.add)
            ins.then_inc(took[tl.slot], 1)

        def ffn_sync(sp, l):
            w_in, w_out = ffn_w_in[l], ffn_w_out[l]

            def gate_up(pn, tl, i, cnt, ahead, hf):
                load_panel(sp, pn, cols_of(w_in, i * P + hf * FH * P), KT)
                load_panel(sp, pn + 1, cols_of(w_in, i * P + (FFN + hf * FH * P)), KT)
                if l == 0 and not isinstance(i, int):
                    a = i + (SL_F0 + hf * (FH - 1))
                    slab_load(sp, a, 1, i * SLAB + (SL_F0 - SL_HGO + hf * (FH - 1)) * SLAB, pn + (-2), norms=2)

            def down(pn, tl, j, ahead, hf):
                load_panel(sp, pn, cols_of(w_out[hf * FH * P:(hf + 1) * FH * P, :], j * P), FH)

            ffn_loop(sp, gate_up, down, l)

        def slabs(eng, one):
            for n in range(FIRST_SLABS):
                one(At(n), 0, n)

        ada = (m["ada0"], m["ada1"])

        def slab_sync(sp):
            def one(n, l, cc):
                if n.past(2):
                    sp.wait_ge(s["modev"], n.n - 1)
                sp.dma_start(ada[n.slot][:, :, :],
                             ada_w[l][:, bass.ds(cc * 512, 512)].rearrange("(k p) n -> p k n", p=P))\
                    .then_inc(s[f"slab{n.slot}"], 16)
            slabs(sp, one)

        def slab_tensor(pe):
            def one(n, l, cc):
                pe.wait_ge(s[f"slab{n.slot}"], (n.turn + 1) * 16)
                if n.past(2):
                    pe.wait_ge(s["modev"], n.n - 1)
                for sub in range(4):
                    for k in range(KT):
                        ins = pe.matmul(S[:, n.slot, 2 * sub:2 * sub + 2],
                                        ada[n.slot][:, k, sub * P:(sub + 1) * P], m["csil"][:, k, :],
                                        start=(k == 0), stop=(k == KT - 1))
                ins.then_inc(s["ada"], 1)
            slabs(pe, one)

        def slab_vector(dve):
            def one(n, l, cc):
                dve.wait_ge(s["ada"], n.n + 1)
                bias = m["colB"][:, bass.ds(cc * 4 + l * 48, 4)].rearrange("p (t a) -> p t a", a=1)
                dve.tensor_tensor(m["mods"][:, l, bass.ds(cc * 4, 4), :],
                                  S[:, n.slot, 0:8].rearrange("p (t a) -> p t a", a=2),
                                  bias.to_broadcast([P, 4, 2]), ALU.add).then_inc(s["modev"], 1)
            slabs(dve, one)

        N_CONST = 11
        LAT = SEGS[:1]
        N2, K2 = 2, HEADS + 2
        xpad = (m["xpad0"], m["xpad1"])
        CONV_N = T + CONV_W // 2
        PANELS = [("x", i) for i in range(GT)] + [("b", 0), ("c", 0)] + [("z", i) for i in range(GT)]
        CONVS = PANELS[:GT + 2]
        CONV_TILES = (DI + 2 * GROUPS * P) // P

        def ss_cols(kind, i, g):
            start = {"z": i * P, "b": BC0, "c": CC0, "x": XBC0 + i * P}[kind]
            width = P if kind in "bc" else GW
            return (g + (-1)) * width + (start + width)

        def conv_tile(kind, i, g):
            return {"x": g * GT + i, "b": g + NH // 2, "c": g + (NH // 2 + GROUPS)}[kind]

        def conv_to(kind, i):
            return {"b": m["bfm"][:, :], "c": m["cfm"][:, :]}[kind] if kind in "bc" else m["xfm"][:, i, :]

        def per_head(t, b, d, g):
            return t[:, b, bass.ds(g * HPG + d * NH, HPG)].rearrange("p (h a) -> p h a", a=1)\
                .to_broadcast([P, HPG, HP])

        def hd(ap):
            return ap.rearrange("p (h c) -> p h c", c=HP)

        def dt_scalar(act):
            act.wait_ge(s["parked1"], 16)
            pn = At(PAN_DT)
            split_hi(act, pn + 2, KT)
            zt, za, e, ln = (m[n] for n in ("xpad0", "xpad1", "acc", "bfm"))
            act.activation(zt[0:2 * NH, 0:T], G[P - 2 * NH:P, pn.slot, 0:T], ACT.Copy).then_inc(took[pn.slot], 1)
            act.wait_ge(s["small"], 64)
            act.activation(m["aneg"][:, 1:2], m["aneg"][:, 0:1], ACT.Exp).then_inc(s["dts"], 1)
            act.wait_ge(s["dtv"], 1)
            act.activation(e[0:2 * NH, 0:T], za[0:2 * NH, 0:T], ACT.Abs).then_inc(s["dts"], 1)
            act.wait_ge(s["dts"], 2)
            act.activation(zt[0:2 * NH, 0:T], e[0:2 * NH, 0:T], ACT.Exp, scale=-1.0).then_inc(s["dts"], 1)
            act.wait_ge(s["dts"], 3)
            act.activation(ln[0:2 * NH, 0:T], zt[0:2 * NH, 0:T], ACT.Ln, bias=1.0).then_inc(s["dts"], 1)
            act.wait_ge(s["dtv"], DT_D)
            act.activation(zt[0:2 * NH, 0:T], za[0:2 * NH, 0:T], ACT.Exp, scale=-1.0).then_inc(s["dts"], 1)
            act.wait_ge(s["pdt"], 1)
            act.activation(m["ecT"][:, :, :].rearrange("p b h -> p (b h)"), PAIR[0][:, 0:NBLK * 2 * NH], ACT.Exp)
            act.activation(m["ncumT"][:, :, :].rearrange("p b h -> p (b h)"), PAIR[0][:, 0:NBLK * 2 * NH],
                           ACT.Copy, scale=-1.0)
            act.activation(m["dtT"][:, :, :].rearrange("p b h -> p (b h)"),
                           PAIR[0][:, NBLK * 2 * NH:2 * NBLK * 2 * NH], ACT.Copy)
            act.activation(m["wT"][:, :, :].rearrange("p b h -> p (b h)"), PAIR[1][:, 0:NBLK * 2 * NH], ACT.Copy)
            act.activation(m["dec"][:, :, :].rearrange("p b h -> p (b h)"),
                           PAIR[1][:, NBLK * 2 * NH:2 * NBLK * 2 * NH], ACT.Exp).then_inc(s["dtT"], 1)

        DT_D = 17

        def dt_vector(dve):
            n = [0]

            def link(ins):
                n[0] += 1
                ins.then_inc(s["dtv"], 1)
                dve.wait_ge(s["dtv"], n[0])

            pn = At(PAN_DT)
            dve.wait_ge(s["parked1"], 16)
            split_lo(dve, pn + 2, KT)
            zt, z, e, ln, den, iz = (m[n_][0:2 * NH, 0:T] for n_ in ("xpad0", "xpad1", "acc", "bfm", "dt", "cumS"))
            t2 = m["cfm"][0:2 * NH, 0:T]
            dve.wait_ge(took[pn.slot], pn.turn + 1)
            dve.wait_ge(s["small"], 64)
            link(dve.tensor_scalar(z, zt, m["dtb"][:, 0:1], None, ALU.add))
            dve.wait_ge(s["dts"], 4)
            link(dve.tensor_scalar(den, zt, 1.0, -1.0, ALU.add, ALU.add))
            link(dve.tensor_scalar(iz, den, 0.0, None, ALU.is_equal))
            link(dve.tensor_tensor(den, den, iz, ALU.add))
            link(dve.reciprocal(t2, den))
            link(dve.tensor_tensor(t2, t2, zt, ALU.mult))
            link(dve.tensor_tensor(ln, ln, t2, ALU.mult))
            link(dve.tensor_tensor(t2, iz, zt, ALU.mult))
            link(dve.tensor_tensor(ln, ln, t2, ALU.add))
            link(dve.scalar_tensor_tensor(den, z, 0.0, ln, ALU.max, ALU.add))
            link(dve.tensor_scalar(m["aneg"][:, 2:3], m["aneg"][:, 1:2], -1.0, None, ALU.mult))
            link(dve.tensor_scalar(t2, den, m["aneg"][:, 2:3], None, ALU.mult))
            dve.wait_ge(s["negm"], 3)
            for d in (0, 1):
                r = slice(d * NH, (d + 1) * NH)
                back = slice(None, None, -1 if d else 1)
                link(dve.tensor_tensor_scan(m["cumS"][r, back], m["segm"][r, :], m["cfm"][r, back], 0.0,
                                            ALU.mult, ALU.add))
            cum3 = m["cumS"][:, :].rearrange("h (b t) -> h b t", t=P)
            for d in (0, 1):
                r = slice(d * NH, (d + 1) * NH)
                t = 0 if d else P - 1
                ins = dve.tensor_copy(m["cl"][r, :], cum3[r, :, t])
            link(ins)
            for d in (0, 1):
                r = slice(d * NH, (d + 1) * NH)
                ins = dve.tensor_tensor(m["xpad1"][r, 0:T].rearrange("h (b t) -> h b t", t=P), cum3[r, :, :],
                                        m["cl"][r, :].rearrange("h (b a) -> h b a", a=1).to_broadcast([NH, NBLK, P]),
                                        ALU.subtract)
                if d == 0:
                    link(ins)
            link(ins)
            assert n[0] == DT_D, n
            dve.wait_ge(s["dts"], 5)
            dve.tensor_tensor(zt, zt, den, ALU.mult).then_inc(s["ynorm"], 1)

        def dt_tensor(pe):
            pn = At(PAN_DT)
            product(pe, pn, pn, m["hhi"], m["hlo"], KT, SEGS, need=h_need(pe, N2))
            pe.wait_ge(s["ynorm"], 1)
            H2 = 2 * NH
            for i, src in enumerate(("cumS", "dt", "xpad0")):
                for b in range(NBLK):
                    pe.transpose(PAIR[i // 2][:, ((i % 2) * NBLK + b) * H2:((i % 2) * NBLK + b + 1) * H2],
                                 m[src][0:H2, b * P:(b + 1) * P], ident[0:H2, 0:H2])
            for b in range(NBLK):
                ins = pe.matmul(PAIR[1][:, (NBLK + b) * H2:(NBLK + b + 1) * H2],
                                m["cl"][:, b:b + 1].to_broadcast([H2, P]), ident[0:H2, 0:H2],
                                start=True, stop=True)
            ins.then_inc(s["pdt"], 1)

        def chain_at(n):
            return n % 2, n // 2, BORDER[n % 2][n // 2]

        def state(q, k):
            return 9 * q + 2 * k - 1

        states_of = (s["stf"], s["stb"])

        def ss_scalar(act, ss, g, q, prev):
            for j in range(len(PANELS)):
                before = (ss + j + (-1) if j else prev) if ss is not None else (prev if j == 0 else None)
                kind, i = PANELS[j - 1]
                gg = g if j else q
                ci = CONVS.index((kind, i)) if before is not None and kind != "z" else None
                if before is not None:
                    split_hi(act, before + 2, KT)
                    if kind == "z":
                        act.activation(m["z"][:, bass.ds(gg % 2, 1), i, :].rearrange("p a t -> p (a t)"),
                                       G[:, before.slot, 0:NLAT], ACT.Silu).then_inc(took[before.slot], 1)
                    else:
                        xp, ct = xpad[ci % 2], conv_tile(kind, i, gg)
                        act.activation(xp[:, 2:2 + NLAT], G[:, before.slot, 0:NLAT], ACT.Copy)
                        act.activation(xp[:, 4 + NLAT:4 + T], G[:, before.slot, NLAT:T], ACT.Copy)\
                            .then_inc(took[before.slot], 1)
                        if ci or q is not None:
                            act.wait_ge(s["conv"], 6 * g + ci)
                        act.wait_ge(took[before.slot], before.turn + 1)
                        act.activation(m["acc"][:, :], xp[:, 0:T + 2], ACT.Identity,
                                       bias=m["colA"][:, bass.ds(ct + COL_CB, 1)],
                                       scale=m["colC"][:, bass.ds(ct, 1)]).then_inc(s["xp"], 1)
                if q is not None and j == 0:
                    act.wait_ge(s["yout"], 16 * q + 16)
                    for i_ in range(GT):
                        act.activation(m["yb"][:, i_, :], m["xfm"][:, i_, 0:NLAT], ACT.Identity,
                                       scale=m["dsk"][:, bass.ds(q * GT + i_, 1)])
                if q is not None and 3 <= j < 7:
                    for hh in (2 * (j - 3), 2 * (j - 3) + 1):
                        r = hh % 2
                        act.wait_ge(s["sm"], HPG * q + hh + 1)
                        if hh >= 2:
                            act.wait_ge(s["yd"], HPG * q + hh - 1)
                        for d in (0, 1):
                            for b in range(LBLK):
                                ins = act.activation(block(m[f"e{d}{r}"][:, :], b), block(S[:, d, :], b), ACT.Exp,
                                                     bias=m["ncumT"][:, b, bass.ds(q * HPG + (d * NH + hh), 1)])
                        ins.then_inc(s["em"], 1)
                if ci is not None:
                    act.wait_ge(s["tap"], 24 * g + 4 * ci + 4)
                    to = conv_to(kind, i)
                    act.activation(to[:, 0:NLAT], m["acc"][:, 0:NLAT], ACT.Silu)
                    act.activation(to[:, NLAT:T], m["acc"][:, NLAT + 2:T + 2], ACT.Silu).then_inc(s["conv"], 1)
                if q is not None and j == 7:
                    for i_ in range(GT):
                        act.wait_ge(s["yz"], GT * q + i_ + 1)
                        if i_ >= 2:
                            act.wait_ge(s["yr"], GT * q + i_ - 1)
                        act.activation(m[f"sc{i_ % 2}"][:, :], m["yb"][:, i_, :], ACT.Square).then_inc(s["ysq"], 1)
                if ss is not None and j == 9:
                    act.wait_ge(s["ytr"], 6 * g + 1)
                    act.activation(m["btm"][:, :, :].rearrange("p b n -> p (b n)"), PAIR[0][:, 0:T], ACT.Copy)\
                        .then_inc(s["stc"], 1)
                    act.wait_ge(s["ytr"], 6 * g + 2)
                    act.activation(m["cb"][:, :], S[:, 2, :], ACT.Copy).then_inc(s["stc"], 1)
                    for i_ in range(GT):
                        act.wait_ge(s["ytr"], 6 * g + 3 + i_)
                        act.activation(m["xtm"][:, :, i_ * P:(i_ + 1) * P],
                                       PAIR[i_ % 2][:, 0:T].rearrange("p (b n) -> p b n", n=P), ACT.Copy)\
                            .then_inc(s["stc"], 1)

        def chain_values(dve, q, n):
            d, k, b = chain_at(n)
            if n == 0:
                dve.wait_ge(s["stc"], 6 * q + 6)
            if k < NBLK - 1:
                dve.tensor_tensor(hd(m[f"wx{d}"][:, :]), hd(m["xtm"][:, b, :]), per_head(m["wT"], b, d, q),
                                  ALU.mult).then_inc(s["xw"], 1)

        def chain_vector(dve, q, n):
            d, k, b = chain_at(n)
            st, own = m[f"st{d}"], states_of[d]
            if n == 0:
                chain_values(dve, q, 0)
            if n + 1 < 2 * NBLK:
                chain_values(dve, q, n + 1)
            if b < LBLK:
                dve.wait_ge(s["yo"], 2 * LBLK * q + 2 * (k - 2) + d + 1)
                if k < 4:
                    dve.tensor_tensor(hd(m["ytm"][:, b, :]), hd(S[:, 2 + d, :]),
                                      per_head(m["ecT"], b, d, q), ALU.mult).then_inc(s["ymc"], 1)
                else:
                    dve.tensor_tensor(hd(m["sc0"][:, :]), hd(S[:, 2 + d, :]),
                                      per_head(m["ecT"], b, d, q), ALU.mult).then_inc(s["ymc"], 1)
            if 0 < k < NBLK - 1:
                dve.wait_ge(own, state(q, k))
                dve.tensor_tensor(hd(st[:, :]), hd(st[:, :]), per_head(m["dec"], b, d, q), ALU.mult)\
                    .then_inc(own, 1)
            if b < LBLK and k >= 4:
                y0 = 12 * q + 4 + 4 * (k - 4) + 2 * d
                dve.wait_ge(s["ymc"], y0 + 1)
                dve.tensor_tensor(m["ytm"][:, b, :], m["ytm"][:, b, :], m["sc0"][:, :], ALU.add)\
                    .then_inc(s["ymc"], 1)
                dve.wait_ge(s["ymc"], y0 + 2)
            if k < NBLK - 1:
                dve.wait_ge(s["ds"], 2 * (NBLK - 1) * q + 2 * k + d + 1)
                if k == 0:
                    dve.tensor_copy(st[:, :], S[:, d, :]).then_inc(own, 1)
                else:
                    dve.wait_ge(own, state(q, k) + 1)
                    dve.tensor_tensor(st[:, :], st[:, :], S[:, d, :], ALU.add).then_inc(own, 1)

        def chain_tensor(pe, q, n):
            d, k, b = chain_at(n)
            if k:
                pe.wait_ge(states_of[d], state(q, k))
            if b < LBLK:
                pe.matmul(S[:, 2 + d, :], block(m["cfm"][:, :], b), m[f"st{d}"][:, :],
                          start=True, stop=True).then_inc(s["yo"], 1)
            if k < NBLK - 1:
                pe.wait_ge(s["xw"], 2 * (NBLK - 1) * q + 2 * k + d + 1)
                pe.matmul(S[:, d, :], m["btm"][:, b, :], m[f"wx{d}"][:, :],
                          start=True, stop=True).then_inc(s["ds"], 1)

        def head_weights(dve, q, hh):
            r = hh % 2
            dve.wait_ge(s["em"], HPG * q + hh + 1)
            for d in (0, 1):
                for b in range(LBLK):
                    e = block(m[f"e{d}{r}"][:, :], b)
                    ins = dve.scalar_tensor_tensor(e, e, m["dtT"][:, b, bass.ds(q * HPG + (d * NH + hh), 1)],
                                                   block(m["cb"][:, :], b), ALU.mult, ALU.mult)
            ins.then_inc(s["mm"], 1)
            dve.wait_ge(s["mm"], 2 * (HPG * q + hh) + 1)
            dve.tensor_tensor(m[f"e0{r}"][:, :], m[f"e0{r}"][:, :], m[f"e1{r}"][:, :], ALU.add).then_inc(s["mm"], 1)

        def head_out(dve, q, hh):
            dve.wait_ge(s["yd"], HPG * q + hh + 1)
            yt = m["ytm"][:, :, hh * HP:(hh + 1) * HP]
            dve.tensor_tensor(yt, yt, S[:, 2 + hh % 2, 0:LBLK * HP].rearrange("p (b c) -> p b c", c=HP),
                              ALU.add).then_inc(s["ym2"], 1)

        def ss_vector(dve, ss, g, q, prev):
            for j in range(len(PANELS)):
                before = (ss + j + (-1) if j else prev) if ss is not None else (prev if j == 0 else None)
                kind, i = PANELS[j - 1]
                ci = CONVS.index((kind, i)) if before is not None and kind != "z" else None

                def tap(k):
                    if ci is None:
                        return
                    if k == 1:
                        dve.wait_ge(s["xp"], 6 * g + ci + 1)
                    else:
                        dve.wait_ge(s["tap"], 24 * g + 4 * ci + k - 1)
                    dve.scalar_tensor_tensor(m["acc"][:, :], xpad[ci % 2][:, k:k + T + 2],
                                             m["colC"][:, bass.ds(conv_tile(kind, i, g) + k * CONV_TILES, 1)],
                                             m["acc"][:, :], ALU.mult, ALU.add).then_inc(s["tap"], 1)

                if before is not None:
                    split_lo(dve, before + 2, KT)
                if q is not None and j == 0:
                    for d in (0, 1):
                        ins = dve.tensor_copy(m["sel"][:, d * HPG:(d + 1) * HPG],
                                              ident[0:2 * NH, bass.ds(q * HPG + d * NH, HPG)])
                    ins.then_inc(s["cbs"], 1)
                for u in range(4):
                    if q is not None:
                        if j < 3:
                            chain_vector(dve, q, 4 * j + u)
                        elif j < 7:
                            hh = 2 * (j - 3) + u // 2
                            if u % 2 == 0:
                                head_weights(dve, q, hh)
                            elif hh:
                                head_out(dve, q, hh - 1)
                    tap(u + 1)
                if q is not None and j == 7:
                    head_out(dve, q, HPG - 1)
                    for i_ in range(GT):
                        yb = m["yb"][:, i_, :]
                        dve.wait_ge(s["ytt"], GT * q + i_ + 1)
                        dve.tensor_tensor(yb, yb, S[:, i_, :], ALU.add).then_inc(s["ya"], 1)
                    for i_ in range(GT):
                        yb = m["yb"][:, i_, :]
                        dve.wait_ge(s["ya"], GT * q + i_ + 1)
                        dve.tensor_tensor(yb, yb, m["z"][:, bass.ds(q % 2, 1), i_, :].rearrange("p a t -> p (a t)"),
                                          ALU.mult).then_inc(s["yz"], 1)
                if q is not None and j == 8:
                    dve.wait_ge(s["yr"], GT * q + GT)
                    mean_dve(dve, LBLK, GW)
                    dve.wait_ge(s["rbc"], q + (K2 + 2))
                    for i_ in range(GT):
                        yb = m["yb"][:, i_, :]
                        ins = dve.scalar_tensor_tensor(yb, yb, m["colA"][:, bass.ds(q * GT + (COL_SN + i_), 1)],
                                                       S[:, 1, :], ALU.mult, ALU.mult)
                    ins.then_inc(s["ynorm"], 1)

        TURNS = {0: 0, 1: 1, 2: 2, 3: 3, 5: 4, 7: 5}

        def ss_between(pe, g, q, j, k):
            if q is not None:
                if j < 3 and k % 2 == 0:
                    chain_tensor(pe, q, 4 * j + k // 2)
                if 3 <= j < 7:
                    hh = 2 * (j - 3) + k // 4
                    if k % 4 == 0:
                        heads_seg(pe, q, hh)
                    elif k % 4 == 2 and hh:
                        heads_y(pe, q, hh - 1)
                if (j, k) == (7, 1):
                    heads_y(pe, q, HPG - 1)
                if (j, k) == (7, 3):
                    pe.wait_ge(s["ym2"], HPG * q + HPG)
                    for i_ in range(GT):
                        for b in range(LBLK):
                            ins = pe.transpose(block(S[:, i_, :], b), m["ytm"][:, b, i_ * P:(i_ + 1) * P], ident[:, :])
                        ins.then_inc(s["ytt"], 1)
                if (j, k) == (8, 1):
                    pe.wait_ge(s["ya"], GT * q + GT)
                    for i_ in range(GT):
                        pe.wait_ge(s["ysq"], GT * q + i_ + 1)
                        for b in range(LBLK):
                            ins = pe.matmul(S[:, 0, b:b + 1], block(m[f"sc{i_ % 2}"][:, :], b), ones[:, :],
                                            start=(i_ == 0 and b == 0), stop=(i_ == GT - 1),
                                            skip_group_check=True)
                        ins.then_inc(s["yr"], 1)
                if (j, k) == (8, 4):
                    spread_pe(pe, q + (K2 + 1), LBLK, S[:, 1, :])
            if g is not None and j == 9 and k in TURNS:
                n = TURNS[k]
                if n == 0:
                    pe.wait_ge(s["conv"], 6 * g + 6)
                    pe.wait_ge(s["dtT"], 1)
                    pe.wait_ge(s["ynorm"], g + 1)
                    for b in range(NBLK):
                        ins = pe.transpose(block(PAIR[0], b), block(m["bfm"][:, :], b), ident[:, :])
                elif n == 1:
                    for b in range(LBLK):
                        ins = pe.matmul(block(S[:, 2, :], b), block(m["bfm"][:, :], b), block(m["cfm"][:, :], b),
                                        start=True, stop=True)
                else:
                    pe.wait_ge(s["stc"], 6 * g + n - 1)
                    for b in range(NBLK):
                        ins = pe.transpose(block(PAIR[n % 2], b), block(m["xfm"][:, n - 2, :], b), ident[:, :])
                ins.then_inc(s["ytr"], 1)

        def ss_tensor(pe, ss, g, q, prev):
            for j, (kind, i) in enumerate(PANELS):
                if ss is not None:
                    product(pe, ss + j, ss + j, m["hhi"], m["hlo"], KT, LAT if kind == "z" else SEGS,
                            between=lambda k: ss_between(pe, g, q, j, k))
                else:
                    for k in range(KT):
                        ss_between(pe, None, q, j, k)

        def heads_seg(pe, q, hh):
            if hh == 0:
                for d in (0, 1):
                    pe.wait_ge(states_of[d], state(q, NBLK - 1))
                pe.wait_ge(s["cbs"], q + 1)
            else:
                pe.wait_ge(s["em"], HPG * q + hh)
            for d in (0, 1):
                pe.matmul(S[:, d, :], m["sel"][:, d * HPG + hh:d * HPG + hh + 1].to_broadcast([2 * NH, P]),
                          m["cumS"][:, 0:NLAT], start=True, stop=False)
                ins = pe.matmul(S[:, d, :], m["identb"][:, :], m[f"neg{d}"][:, :], start=False, stop=True)
            ins.then_inc(s["sm"], 1)

        def heads_y(pe, q, hh):
            r = hh % 2
            pe.wait_ge(s["mm"], 2 * (HPG * q + hh) + 2)
            if hh < 2:
                pe.wait_ge(s["ymc"], 12 * q + 12)
            else:
                pe.wait_ge(s["ym2"], HPG * q + hh - 1)
            for b in range(LBLK):
                ins = pe.matmul(S[:, 2 + r, b * HP:(b + 1) * HP], block(m[f"e0{r}"][:, :], b),
                                m["xtm"][:, b, hh * HP:(hh + 1) * HP], start=True, stop=True)
            ins.then_inc(s["yd"], 1)

        def ss_all(eng, one):
            one(At(PAN_SS), 0, None, None)
            with eng.Fori(0, GROUPS - 1) as i:
                one(At(PAN_SS + 10, i * 5), i + 1, i, At(PAN_SS + 9, i * 5))
            one(None, None, GROUPS - 1, At(PAN_SO - 1))

        def so_pairs(eng, one):
            with eng.Fori(0, KT // 2) as i:
                for u in (0, 1):
                    for half in (0, 1):
                        one(At(PAN_SO + 2 * u + half, i * 2), At(TIL_SO + u, i), i * 2 + u, half)

        ymid_hi = m["mhi"][:, :, :].rearrange("p f t -> p (f t)")[:, 0:2 * KT * NLAT].rearrange("p (k t) -> p k t", t=NLAT)
        ymid_lo = m["mlo"][:, :, :].rearrange("p f t -> p (f t)")[:, 0:2 * KT * NLAT].rearrange("p (k t) -> p k t", t=NLAT)
        yin = (m["act0"], m["act1"])

        def l1_sync(sp):
            load_panel(sp, At(PAN_DT), cols_of(ssm_w_in[0], SSM_IN - P), KT)

            def loads(ss, g, q, prev):
                if ss is not None:
                    for j, (kind, i) in enumerate(PANELS):
                        load_panel(sp, ss + j, cols_of(ssm_w_in[0], ss_cols(kind, i, g)), KT)
            ss_all(sp, loads)

            def so(pn, tl, j, half):
                load_panel(sp, pn, cols_of(ssm_w_out[0][half * D:(half + 1) * D, :], j * P), KT)
            so_pairs(sp, so)
            ffn_sync(sp, 1)
            for b in range(LBLK):
                sp.wait_ge(s["fo"], KT)
                sp.dma_start(out[0, b * P:(b + 1) * P, :], m["ofin"][:, b, :]).then_inc(s["outd"], 16)
            sp.wait_ge(s["outd"], 16 * LBLK)

        def l1_pool(pool):
            for j in (KT - 2, KT - 1):
                tile_ready(ffn_at(0, 1)[1] + 2 * FH)(pool, j)
            pool.dma_start(x_park, m["x1"][:, :, 0:NLAT]).then_inc(s["parked1"], 16)
            rsqrt_pool(pool, K2, NBLK)
            pool.wait_ge(s["parked1"], 16)
            for d in (0, 1):
                pool.dma_start(m["dtb"][d * NH:(d + 1) * NH, 0:1], ssm_dt_bias[0, d].rearrange("(h a) -> h a", a=1))\
                    .then_inc(s["small"], 16)
                pool.dma_start(m["aneg"][d * NH:(d + 1) * NH, 0:1], ssm_a_log[0, d].rearrange("(h a) -> h a", a=1))\
                    .then_inc(s["small"], 16)
            pool.dma_start(m["dall"][:, :], ssm_d.to_broadcast([P, NH])).then_inc(s["yout"], 16)
            pool.wait_ge(s["yout"], 16)
            for q in (0, 1):
                pool.tensor_copy(m["dsk"][q * HP:(q + 1) * HP, :], m["dall"][q * HP:(q + 1) * HP, q::2])\
                    .then_inc(s["dskin"], 1)
                pool.wait_ge(s["dskin"], q + 1)
            pool.memset(chunks(m["segm"][:, :])[:, 1::2, 0:1], 1.0).then_inc(s["negm"], 1)
            pool.wait_ge(s["hlo"], 8 * (N2 + 1))
            pool.tensor_copy(m["identb"][:, :], ident[:, :])
            for d in (0, 1):
                pool.memset(m[f"neg{d}"][:, :], 0.0).then_inc(s["negz"], 1)
                pool.wait_ge(s["negz"], d + 1)
                v = m[f"neg{d}"][:, :].rearrange("p (b t) -> p b t", t=P)
                pool.affine_select(out=v, in_=v, compare_op=ALU.is_ge, fill=-1e30, base=0,
                                   pattern=[[0, LBLK], [1 - 2 * d, P]], channel_multiplier=2 * d - 1)\
                    .then_inc(s["negm"], 1)
            pool.wait_ge(s["dtT"], 1)
            for i, xp in enumerate(xpad):
                for j, (c0, c1) in enumerate(((0, 2), (2 + NLAT, 4 + NLAT), (4 + T, 8 + T))):
                    pool.memset(xp[:, c0:c1], 0.0).then_inc(s["halo"], 1)
            for g in range(GROUPS):
                rsqrt_pool(pool, K2 + 1 + g, LBLK)
                pool.wait_ge(s["ynorm"], g + 2)
                pool.dma_start(y_park[g], m["yb"][:, :, :]).then_inc(s["yout"], 16)
            pool.wait_ge(s["yout"], 16 * GROUPS + 16)
            pool.dma_start(m["x1"][:, :, 0:NLAT], x_park).then_inc(s["back1"], 16)
            for k in range(2 * KT):
                if k >= 2:
                    pool.wait_ge(s["yl"], k - 1)
                pool.dma_start(yin[k % 2][:, 0:NLAT], y_park[k // GT, :, k % GT, :]).then_inc(s[f"yin{k % 2}"], 16)
            rsqrt_pool(pool, K2 + 1 + GROUPS, LBLK)
            rsqrt_pool(pool, K2 + 2 + GROUPS, LBLK)

        def l1_scalar(act):
            norm_act(act, m["x1"], N2, SEGS, tile_ready(ffn_at(0, 1)[1] + 2 * FH), 1, 0)
            dt_scalar(act)
            act.wait_ge(s["halo"], 6)
            act.wait_ge(s["dskin"], 2)
            ss_all(act, lambda *a: ss_scalar(act, *a))
            for k in range(2 * KT):
                act.wait_ge(s[f"yin{k % 2}"], 16 * (k // 2 + 1))
                act.activation(ymid_hi[:, k, :], yin[k % 2][:, 0:NLAT], ACT.Copy).then_inc(s["yh"], 1)
            so_pairs(act, lambda pn, tl, j, half: split_hi(act, pn + 2, KT))
            norm_act(act, m["x1"], 3, LAT, tile_ready(At(TIL_SO)), 1, 1)
            ffn_scalar(act, 1, LAT)
            squares_act(act, m["x1"], 4, LAT, tile_ready(ffn_at(1, 1)[1] + 2 * FH))
            for j in range(KT):
                act.wait_ge(s["ft"], j + 1)
                act.activation(m["ofin"][:, :, j * P:(j + 1) * P],
                               Gq[:, j % 4, :].rearrange("p (b f) -> p b f", f=P), ACT.Copy).then_inc(s["fo"], 1)

        def l1_vector(dve):
            factors(dve, 1, 0)
            norm_dve(dve, m["x1"], N2, K2, SEGS, 1, 0)
            dt_vector(dve)
            ss_all(dve, lambda *a: ss_vector(dve, *a))
            for k in range(2 * KT):
                dve.wait_ge(s["yh"], k + 1)
                dve.tensor_tensor(ymid_lo[:, k, :], yin[k % 2][:, 0:NLAT], f32(ymid_hi[:, k, :]), ALU.subtract)\
                    .then_inc(s["yl"], 1)
            dve.wait_ge(s["back1"], 16)

            def so(pn, tl, j, half):
                split_lo(dve, pn + 2, KT)
                if half:
                    add_gated(dve, tl, j, 1, 2, LAT)
            so_pairs(dve, so)
            factors(dve, 1, 1)
            norm_dve(dve, m["x1"], 3, K2 + 1 + GROUPS, LAT, 1, 1)
            ffn_vector(dve, 1, LAT)
            dve.wait_ge(s["sqd"], 8 * 5)
            mean_dve(dve, LBLK, D)
            dve.wait_ge(s["rbc"], K2 + 3 + GROUPS)
            for j in range(KT):
                if j >= 2:
                    dve.wait_ge(s["ft"], j - 1)
                dve.scalar_tensor_tensor(hn[j % 2][:, 0:NLAT], m["x1"][:, j, 0:NLAT],
                                         m["colA"][:, COL_FIN + j:COL_FIN + j + 1], PAIR[1][:, 0:NLAT],
                                         ALU.mult, ALU.mult).then_inc(s["fn"], 1)

        def l1_tensor(pe):
            norm_pe(pe, N2, K2, NBLK)
            dt_tensor(pe)
            ss_all(pe, lambda *a: ss_tensor(pe, *a))

            def so(pn, tl, j, half):
                product(pe, pn, tl, ymid_hi, ymid_lo, KT, LAT, k_base=half * KT, first=(half == 0),
                        last=(half == 1), need=lambda k: pe.wait_ge(s["yl"], half * KT + k + 1))
            so_pairs(pe, so)
            norm_pe(pe, 3, K2 + 1 + GROUPS, LBLK)
            ffn_tensor(pe, 1, LAT)
            norm_pe(pe, 4, K2 + 2 + GROUPS, LBLK)
            for j in range(KT):
                pe.wait_ge(s["fn"], j + 1)
                if j >= 4:
                    pe.wait_ge(s["fo"], j - 3)
                for b in range(LBLK):
                    ins = pe.transpose(block(Gq[:, j % 4, :], b), block(hn[j % 2][:, 0:NLAT], b), ident[:, :])
                ins.then_inc(s["ft"], 1)

        block_ = ctx.enter_context(nc.Block())

        @block_.sync
        def _(sp):
            rows = ((m["rowA"], COL_NORM, norm_w.rearrange("l i (j p) -> (l i j) p", p=P)),
                    (m["rowA"], COL_FIN, final_norm_w.rearrange("(j p) -> j p", p=P)),
                    (m["rowA"], COL_C, c.rearrange("b (j p) -> (b j) p", p=P)),
                    (m["rowA"], COL_CC, c_ctx.rearrange("(j p) -> j p", p=P)),
                    (m["rowA"], COL_SN, ssm_norm_w.rearrange("b (j p) -> (b j) p", p=P)),
                    (m["rowA"], COL_CB, ssm_conv_b.rearrange("b (j p) -> (b j) p", p=P)),
                    (m["rowA"], COL_GN, hg_norm_w),
                    (m["rowB"], 0, ada_b.rearrange("l (t p) -> (l t) p", p=P)),
                    (m["rowC"], 0, ssm_conv_w.rearrange("b k (t p) -> (b k t) p", p=P)),
                    (m["rowD"], 0, hg_lb.rearrange("d r (h p) -> (d r h) p", p=P)))
            for to, r0, src in rows:
                sp.dma_start(to[r0:r0 + src.shape[0], :], src).then_inc(s["rows"], 16)
            for b in range(NBLK):
                src = x[0] if b < LBLK else ctx_x[0]
                b0 = b if b < LBLK else b - LBLK
                sp.dma_start(m["xin"][:, b, :], src[b0 * P:(b0 + 1) * P, :]).then_inc(s["xin"], 16)
            slab_sync(sp)

            def hg_loads(hg, hn_, hp, h, pn_par, ps_par):
                if hg is not None:
                    for j, off in enumerate(HG_OFF):
                        load_panel(sp, hg + j, cols_of(hg_w_in[0], hn_ * P + off), KT)
                        if j == 1:
                            slab_load(sp, hn_ * 2, 0, hn_ * (2 * SLAB) + 2 * D,
                                      None if h is None else hp + 2)
                        if j == 4:
                            slab_load(sp, hn_ * 2 + 1, 0, hn_ * (2 * SLAB) + (2 * D + SLAB), hg)
            hg_all(sp, hg_loads)
            with sp.Fori(0, KT // 2) as i:
                for u in (0, 1):
                    load_panel(sp, At(PAN_HGO + u, i), cols_of(hg_w_out[0], i * 2 * P + u * P), KT)
                slab_load(sp, i + SL_HGO, 1, i * SLAB, At(PAN_HGO - 2, i))
            ffn_sync(sp, 0)
            l1_sync(sp)

        @block_.gpsimd
        def _(pool):
            n = [0]

            def link(ins):
                n[0] += 1
                ins.then_inc(s["ps"], 1)
                pool.wait_ge(s["ps"], n[0])

            link(pool.memset(ident[:, :], 0.0))
            pool.affine_select(out=ident[:, :], in_=ident[:, :], compare_op=ALU.not_equal, fill=1.0, base=0,
                               pattern=[[-1, P]], channel_multiplier=1).then_inc(s["ident"], 1)
            pool.wait_ge(s["ident"], 1)
            link(pool.memset(ones[:, :], 1.0))
            link(pool.memset(m["mhalf"][:, :], -0.5))
            link(pool.memset(m["segm"][:, :], 1.0))
            link(pool.memset(chunks(m["segm"][:, :])[:, :, 0:1], 0.0))
            for d in (0, 1):
                link(pool.memset(mask[d][:, :, :], 1.0))
                for o in (0, CH):
                    link(pool.affine_select(out=mask[d][o:o + CH, :, :], in_=mask[d][o:o + CH, :, :],
                                            compare_op=ALU.is_ge, fill=0.0, base=0,
                                            pattern=[[0, NBLK], [1 - 2 * d, CH]], channel_multiplier=2 * d - 1))
            assert n[0] == N_CONST
            rsqrt_pool(pool, 0, NBLK)
            pool.wait_ge(s["x"], NBLK * 2)
            pool.dma_start(x_park0, m["x0"][:, :, :]).then_inc(s["parked0"], 16)
            for h in range(HEADS):
                rsqrt_pool(pool, h + 1, NBLK)
            pool.wait_ge(s["og"], HEADS)
            pool.wait_ge(s["parked0"], 16)
            pool.dma_start(m["x1"][:, :, :], x_park0).then_inc(s["back0"], 16)
            rsqrt_pool(pool, HEADS + 1, NBLK)
            l1_pool(pool)

        @block_.scalar
        def _(act):
            act.wait_ge(s["cols"], 1)
            for i, col in ((0, COL_C), (1, COL_CC)):
                ins = act.activation(m["csil"][:, :, i], m["colA"][:, col:col + KT], ACT.Silu)
            ins.then_inc(s["csil"], 1)
            act.wait_ge(s["tdve"], 3)
            act.activation(m["lbe"][:, :, :, :], m["lbe"][:, :, :, :], ACT.Exp).then_inc(s["lbs"], 1)
            split_hi(act, At(0), KT)
            split_hi(act, At(1), KT)
            norm_act(act, m["x0"], 0, SEGS, x_loaded, 0, 0)
            hg_all(act, lambda *a: hg_scalar(act, *a))
            act.wait_ge(s["og"], HEADS)
            for j in range(HEADS):
                act.activation(m["hhi"][:, j, :], m["og"][:, j, :], ACT.Copy).then_inc(s["osp_hi"], 1)
            with act.Fori(0, KT // 2) as i:
                for u in (0, 1):
                    split_hi(act, At(PAN_HGO + 2 + u, i), KT)
            norm_act(act, m["x1"], 1, SEGS, tile_ready(At(PAN_HGO)), 0, 1)
            ffn_scalar(act, 0, SEGS)
            l1_scalar(act)

        @block_.vector
        def _(dve):
            n = [0]

            def link(ins):
                n[0] += 1
                ins.then_inc(s["tdve"], 1)
                dve.wait_ge(s["tdve"], n[0])

            dve.wait_ge(s["tpe"], 1)
            dve.tensor_copy(m["colA"][:, :], S[:, 2, 0:97]).then_inc(s["cols"], 1)
            dve.tensor_copy(m["colB"][:, :], S[:, 2, 128:224])
            dve.tensor_copy(m["colC"][:, :], S[:, 2, 256:376])
            dve.tensor_copy(m["colD"][:, :, :, :].rearrange("p d r h -> p (d r h)"), S[:, 2, 384:432])\
                .then_inc(s["cols"], 1)
            dve.wait_ge(s["cols"], 2)
            D3, lbt, lbe = m["colD"], m["lbt"], m["lbe"]
            link(dve.tensor_tensor(lbt[:, :, :], D3[:, :, 0, :], D3[:, :, 1, :], ALU.max))
            link(dve.tensor_tensor(lbt[:, :, :], lbt[:, :, :], D3[:, :, 2, :], ALU.max))
            for r in range(3):
                ins = dve.tensor_tensor(lbe[:, :, r, :], D3[:, :, r, :], lbt[:, :, :], ALU.subtract)
            link(ins)
            for u in range(2 * NBLK):
                b, q = u // 2, u % 2
                dve.wait_ge(s["xt"], u + 1)
                dve.tensor_copy(m["x0"][:, 4 * q:4 * q + 4, b * P:(b + 1) * P],
                                Gq[:, u % 4, :].rearrange("p (j t) -> p j t", j=4)).then_inc(s["x"], 1)
            dve.wait_ge(s["lbs"], 1)
            link(dve.tensor_tensor(lbt[:, :, :], lbe[:, :, 0, :], lbe[:, :, 1, :], ALU.add))
            link(dve.tensor_tensor(lbt[:, :, :], lbt[:, :, :], lbe[:, :, 2, :], ALU.add))
            link(dve.reciprocal(lbt[:, :, :], lbt[:, :, :]))
            link(dve.tensor_tensor(m["lb"][:, :, :], lbe[:, :, 0, :], lbt[:, :, :], ALU.mult))
            link(dve.tensor_scalar(m["oml"][:, :, :], m["lb"][:, :, :], -1.0, 1.0, ALU.mult, ALU.add))
            slab_vector(dve)
            dve.wait_ge(s["modev"], FIRST_SLABS)
            factors(dve, 0, 0)
            split_lo(dve, At(0), KT)
            split_lo(dve, At(1), KT)
            norm_dve(dve, m["x0"], 0, 0, SEGS, 0, 0)
            for d in (0, 1):
                ins = dve.memset(att[d][:, :, :], 0.0)
            ins.then_inc(s["og0"], 1)
            dve.wait_ge(s["og0"], 1)
            dve.wait_ge(s["ps"], N_CONST)
            dve.wait_ge(s["parked0"], 16)
            hg_all(dve, lambda *a: hg_vector(dve, *a))
            for j in range(HEADS):
                dve.wait_ge(s["osp_hi"], j + 1)
                dve.tensor_tensor(m["hlo"][:, j, :], m["og"][:, j, :], f32(m["hhi"][:, j, :]), ALU.subtract)\
                    .then_inc(s["osp_lo"], 1)
            dve.wait_ge(s["back0"], 16)
            with dve.Fori(0, KT // 2) as i:
                for u in (0, 1):
                    split_lo(dve, At(PAN_HGO + 2 + u, i), KT)
                    tl = At(PAN_HGO + u, i)
                    if u:
                        slab_out(dve, tl, 1, i * 2)
                    else:
                        dve.tensor_copy(m["mrow0"][:, :], G[0:2, tl.slot, T:T + SLAB])
                    add_gated(dve, tl, i * 2 + u, 0, 2, SEGS)
            factors(dve, 0, 1)
            norm_dve(dve, m["x1"], 1, HEADS + 1, SEGS, 0, 1)
            ffn_vector(dve, 0, SEGS)
            l1_vector(dve)

        @block_.tensor
        def _(pe):
            pe.wait_ge(s["ident"], 1)
            pe.wait_ge(s["rows"], 160)
            for name, n, at in (("rowA", 97, 0), ("rowB", 96, 128), ("rowC", 120, 256), ("rowD", 48, 384)):
                ins = pe.transpose(S[:, 2, at:at + n], m[name][:, :], ident[0:n, 0:n])
            ins.then_inc(s["tpe"], 1)
            pe.wait_ge(s["xin"], 16 * NBLK)
            for u in range(2 * NBLK):
                b, q = u // 2, u % 2
                if u >= 4:
                    pe.wait_ge(s["x"], u - 3)
                for j in range(4):
                    ins = pe.transpose(Gq[:, u % 4, j * P:(j + 1) * P],
                                       m["xin"][:, b, (4 * q + j) * P:(4 * q + j + 1) * P], ident[:, :])
                ins.then_inc(s["xt"], 1)
            pe.wait_ge(s["csil"], 1)
            slab_tensor(pe)
            pe.wait_ge(s["ps"], N_CONST)
            pe.wait_ge(s["modev"], FIRST_SLABS)
            norm_pe(pe, 0, 0, NBLK)
            hg_all(pe, lambda *a: hg_tensor(pe, *a))
            with pe.Fori(0, KT // 2) as i:
                for u in (0, 1):
                    pn = At(PAN_HGO + u, i)
                    product(pe, pn, pn, m["hhi"], m["hlo"], KT, SEGS,
                            need=lambda k: pe.wait_ge(s["osp_lo"], k + 1),
                            rows=None if u else i + SL_HGO, turn=m["mrow0"] if u else None)
            norm_pe(pe, 1, HEADS + 1, NBLK)
            ffn_tensor(pe, 0, SEGS)
            l1_tensor(pe)


_INS = ["x", "c", "ctx", "c_ctx", "ada_w", "ada_b", "norm_w", "ffn_w_in", "ffn_w_out", "final_norm_w", "hg_w_in",
        "hg_lb", "hg_norm_w", "hg_w_out", "ssm_w_in", "ssm_conv_w", "ssm_conv_b", "ssm_dt_bias", "ssm_a_log",
        "ssm_d", "ssm_norm_w", "ssm_w_out"]


def kernel(**inputs):
    import numpy as _np
    import concourse.bacc as _bacc
    from concourse.bass_utils import run_bass_kernel_spmd as _run

    nc = _bacc.Bacc("TRN2", target_bir_lowering=False, num_devices=1)
    arrays, args = {}, []
    for name in _INS:
        a = _np.ascontiguousarray(inputs[name])
        arrays[f"in_{name}_dram"] = a
        args.append(nc.dram_tensor(f"in_{name}_dram", a.shape, mybir.dt.from_np(a.dtype), kind="ExternalInput").ap())
    args.append(nc.dram_tensor("out_0_dram", (1, NLAT, D), F32, kind="ExternalOutput").ap())
    program(nc, *args)
    r = _run(nc, [arrays], core_ids=[0])
    return r.results[0]["out_0_dram"]
```

```python
from contextlib import ExitStack

import concourse.bass as bass
from concourse import mybir

F32 = mybir.dt.float32
F32R = mybir.dt.float32r
BF16 = mybir.dt.bfloat16
I32 = mybir.dt.int32
ALU = mybir.AluOpType
ACT = mybir.ActivationFunctionType

P = 128
D = 1024
KT = D // P
NLAT, NCTX = 512, 256
T = NLAT + NCTX
NBLK = T // P
LBLK = NLAT // P
EPS = 1e-6
SEGS = ((0, NLAT), (NLAT, NCTX))

HEADS = 8
CH = 64
NCH = T // CH
LAT_CH = NLAT // CH
ORDER = (list(range(LAT_CH, NCH)) + list(range(LAT_CH)), list(range(NCH - 1, -1, -1)))
REF = (CH // 2 - 1, CH // 2)
LAST = (CH - 1, 0)

FFN = 2816
FH = FFN // P // 2

DI = 2048
GROUPS = 4
HPG = 8
HP = 64
NH = GROUPS * HPG
GW = DI // GROUPS
GT = GW // P
CONV_W = 5
XBC0 = DI
BC0, CC0 = XBC0 + DI, XBC0 + DI + GROUPS * P
SSM_IN = CC0 + GROUPS * P + 2 * NH
BORDER = ([4, 5, 0, 1, 2, 3], [5, 4, 3, 2, 1, 0])

PAN_HG = 0
PAN_HGO = PAN_HG + 5 * HEADS
PAN_F0 = PAN_HGO + KT
PAN_DT = PAN_F0 + 2 * (2 * FH + KT)
PAN_SS = PAN_DT + 1
PAN_SO = PAN_SS + 10 * GROUPS
PAN_F1 = PAN_SO + 2 * KT
TIL_SO = PAN_SO
TIL_F1 = TIL_SO + KT

SLAB = 2 * P
SL_HG = 0
SL_HGO = SL_HG + 2 * HEADS
SL_F0 = SL_HGO + KT // 2
assert SLAB * SL_HGO == 4 * D and (SL_F0 - SL_HGO + 2 * (FH - 1)) * SLAB == 6 * D

COL_NORM, COL_FIN, COL_C, COL_CC, COL_SN, COL_CB, COL_GN = 0, 32, 40, 48, 56, 72, 96


class At:

    def __init__(self, c, half=0):
        self.c, self.half = c, half

    def __add__(self, n):
        return At(self.c + n, self.half)

    @property
    def slot(self):
        return self.c % 2

    @property
    def turn(self):
        return self.half + self.c // 2

    @property
    def n(self):
        return self.half * 2 + self.c

    def past(self, k):
        return not isinstance(self.half, int) or self.n >= k


def memory(nc):
    m, m_at = {}, {}
    base, limit = 16512, 229344

    def run(at, *items):
        for name, shape, *dt in items:
            dt = dt[0] if dt else F32
            n = 2 if dt == BF16 else 4
            for d in shape[1:]:
                n *= d
            end = at + (n + 31) // 32 * 32
            assert end <= limit, (name, end)
            m_at[name] = at
            m[name] = nc.alloc_sbuf_tensor_at(name, list(shape), dt, offset=at)
            at = end
        return at

    R = run(base,
            ("ident", (P, P)), ("ones", (P, 1)), ("mhalf", (P, 8)), ("carry", (P, 1)), ("csil", (P, KT, 2)),
            ("colA", (P, 97)), ("colB", (P, 96)), ("colC", (P, 120)), ("mods", (P, 2, 48, 2)), ("afac", (P, 2, 2, KT, 2)),
            ("stat", (P, 8)), ("rstd", (P, 8)), ("lb", (P, 2, HEADS)), ("oml", (P, 2, HEADS)),
            ("segm", (P, T)), ("mask0", (P, NBLK, CH), I32), ("mask1", (P, NBLK, CH), I32),
            *[(f"raw{i}", (P, FH, P)) for i in (0, 1)],
            *[(f"w{w}{i}", (P, FH, P), F32R) for i in (0, 1) for w in ("hi", "lo")],
            ("hhi", (P, KT, T), F32R), ("hlo", (P, KT, T), F32R))
    W = 4 * T
    N = limit - 4 * W
    run(N, *[(f"{n}{i}", (P, T)) for n in ("sq", "hn") for i in (0, 1)])
    assert run(R, ("x0", (P, KT, T)), ("xin", (P, NBLK, D)), ("ada0", (P, KT, 512)), ("ada1", (P, KT, 512)),
               ("rowA", (97, P)), ("rowB", (96, P)), ("rowC", (120, P)), ("rowD", (48, P)), ("arow0", (2, 512)), ("arow1", (2, 512)),
               ("colD", (P, 2, 3, HEADS)),
               ("lbt", (P, 2, HEADS)), ("lbe", (P, 2, 3, HEADS))) <= N
    run(R, ("og", (P, HEADS, T)),
        *[(f"{n}{d}", (P, T)) for n in ("kr", "qr", "qe", "kd", "th", "lf", "cum", "gs") for d in (0, 1)],
        *[(n, (P, T)) for n in ("qs", "vT", "osb", "osq")],
        *[(n, (P, NBLK, P)) for n in ("vtm", "kdtm0", "kdtm1")],
        *[(n, (P, NBLK, CH)) for n in ("att0", "att1", "attS")],
        *[(f"sin{d}", (P, NCH, P)) for d in (0, 1)], *[(f"gl{d}", (P, NCH)) for d in (0, 1)],
        ("adaw", (P, KT, SLAB)))
    at_raw = m_at["raw0"] + 4 * KT * P
    run(at_raw, ("mrow0", (2, SLAB)))
    assert run(R, ("mhi", (P, FH, T), F32R), ("x1", (P, KT, T)), ("mlo", (P, FH, T), F32R),
               ("act0", (P, T)), ("act1", (P, T)), ("mid0", (P, T)), ("mid1", (P, T)), ("mrow1", (2, SLAB))) <= N
    run(m_at["mlo"], ("sqb0", (P, T)), ("sqb1", (P, T)), ("sumb", (P, T)))
    run(R, *[(n, (2 * NH, NBLK)) for n in ("cl", "dtb", "aneg")], ("dt", (2 * NH, T)), ("cumS", (2 * NH, T)),
        *[(n, (P, NBLK, 2 * NH)) for n in ("shiftT", "wT", "ecT", "dec")],
        ("sel", (2 * NH, 2 * HPG), F32R), ("identb", (P, P), BF16), ("neg0", (P, NLAT), BF16), ("neg1", (P, NLAT), BF16), ("dsk", (P, NH // 2)), ("dall", (P, NH)),
        ("z", (P, 2, GT, NLAT)), ("xpad0", (P, T + 8)), ("xpad1", (P, T + 8)), ("acc", (P, T + 2)),
        ("bfm", (P, T)), ("cfm", (P, T)), ("xfm", (P, GT, T)), ("btm", (P, NBLK, P)), ("xtm", (P, NBLK, GW)),
        ("cb", (P, NLAT)), *[(f"e{d}{i}", (P, NLAT)) for d in (0, 1) for i in (0, 1)],
        ("wx0", (P, GW)), ("wx1", (P, GW)), ("st0", (P, GW)), ("st1", (P, GW)),
        ("sc0", (P, GW)), ("sc1", (P, GW)), ("yb", (P, GT, NLAT)), ("ytm", (P, LBLK, GW)),
        *[(n, (2 * NH, NLAT), F32R) for n in ("cuhi", "culo")])
    assert run(N, *[(f"yin{i}", (P, 3, NLAT)) for i in (0, 1)]) <= limit
    run(R, ("ofin", (P, LBLK, D)))
    return m


def program(nc, x, c, ctx_x, c_ctx, ada_w, ada_b, norm_w, ffn_w_in, ffn_w_out, final_norm_w, hg_w_in, hg_lb,
            hg_norm_w, hg_w_out, ssm_w_in, ssm_conv_w, ssm_conv_b, ssm_dt_bias, ssm_a_log, ssm_d, ssm_norm_w,
            ssm_w_out, out):
    with ExitStack() as ctx:
        m = memory(nc)
        G = ctx.enter_context(nc.psum_tensor("G", [P, 2, 1024], F32))
        S = ctx.enter_context(nc.psum_tensor("S", [P, 4, 512], F32))
        Gq = G[:, :, :].rearrange("p s (h n) -> p (s h) n", h=2)
        Sf = S[:, :, :].rearrange("p b n -> p (b n)")
        PAIR = (Sf[:, 0:1024], Sf[:, 1024:2048])
        x_park = nc.dram_tensor("x_park", (P, KT, NLAT), F32, kind="Internal").ap()
        x_park0 = nc.dram_tensor("x_park0", (P, KT, T), F32, kind="Internal").ap()
        y_park = nc.dram_tensor("y_park", (P, (GROUPS - 1) * GT, NLAT), F32, kind="Internal").ap()

        names = """rows xin adain slab0 slab1 raw0 raw1 small parked0 back0 parked1 back1 yout yin0 yin1 outd
            ident cols tpe tdve ada modev afac csil lbs hi lo pan took0 took1
            x sq sqd ssum stat rstd rbc hn hhi hlo
            sig lf cum dif ex kd qk vtm kdtm step cp att sf sb osq og0 og osp_hi osp_lo
            mhi mlo
            dskin negz halo dtv dts pdt dtT negm xt eq xp tap conv ytr stc sm em cbs mm yo yd xw ds stf stb ymc ym2
            ytt ya yz ysq yr ysum ynorm yh yl fn ft fo ps""".split()
        s = {n: ctx.enter_context(nc.semaphore("s_" + n)) for n in names}
        took = (s["took0"], s["took1"])
        raw, whi, wlo = ([m[f"{n}{i}"] for i in (0, 1)] for n in ("raw", "whi", "wlo"))
        sq, hn = ([m[f"{n}{i}"] for i in (0, 1)] for n in ("sq", "hn"))
        ident, ones = m["ident"], m["ones"]

        def f32(ap):
            return ap.bitcast(F32)

        def mod(l, part, j, seg):
            return m["mods"][:, l, part * KT + j, seg:seg + 1]

        def block(ap, b):
            return ap[:, b * P:(b + 1) * P]

        def cols_of(w, off):
            return w[:, bass.ds(off, P)].rearrange("(k p) n -> p k n", p=P)

        HG_OFF = [0, 4 * D, D, 2 * D, 3 * D]

        def load_panel(sp, pn, src, kt):
            if pn.past(2):
                sp.wait_ge(s["lo"], pn.n - 1)
            sp.dma_start(raw[pn.slot][:, 0:kt, :], src).then_inc(s[f"raw{pn.slot}"], 16)

        def split_hi(act, pn, kt):
            act.wait_ge(s[f"raw{pn.slot}"], (pn.turn + 1) * 16)
            if pn.past(2):
                act.wait_ge(s["pan"], pn.n - 1)
            act.activation(whi[pn.slot][:, 0:kt, :], raw[pn.slot][:, 0:kt, :], ACT.Copy).then_inc(s["hi"], 1)

        def split_lo(dve, pn, kt):
            dve.wait_ge(s["hi"], pn.n + 1)
            dve.tensor_tensor(wlo[pn.slot][:, 0:kt, :], raw[pn.slot][:, 0:kt, :],
                              f32(whi[pn.slot][:, 0:kt, :]), ALU.subtract).then_inc(s["lo"], 1)

        def product(pe, pn, tl, rhi, rlo, kt, segs, k_base=0, first=True, last=True, need=None,
                    rows=None, turn=None, between=None):
            pe.wait_ge(s["lo"], pn.n + 1)
            if first and tl.past(2):
                pe.wait_ge(took[tl.slot], tl.turn)
            for k in range(kt):
                if need is not None:
                    need(k)
                if turn is not None and k == kt - 1:
                    prev = tl + (-1)
                    pe.wait_ge(took[prev.slot], prev.turn + 1)
                for i, (w, r) in enumerate(((whi, rhi), (whi, rlo), (wlo, rhi))):
                    for t0, n in segs:
                        ins = pe.matmul(G[:, tl.slot, t0:t0 + n], w[pn.slot][:, k, :],
                                        r[:, k_base + k, t0:t0 + n],
                                        start=(first and k == 0 and i == 0),
                                        stop=(last and k == kt - 1 and i == 2))
                if between is not None:
                    between(k)
            if rows is not None:
                ins = slab_rows(pe, tl, rows)
            if turn is not None:
                ins = slab_turn(pe, tl, turn)
            ins.then_inc(s["pan"], 1)

        def slab_load(sp, a, l, col, before, norms=1):
            src = ada_w[l][:, bass.ds(col, SLAB)].rearrange("(k p) n -> p k n", p=P)
            sp.wait_ge(s["hlo"], 8 * norms)
            if before is not None:
                sp.wait_ge(s["pan"], before.n + 1)
            sp.dma_start(m["adaw"][:, :, :], src).then_inc(s["adain"], 16)

        def slab_rows(pe, tl, a):
            pe.wait_ge(s["adain"], a * 16 + 16)
            for k in range(KT):
                ins = pe.matmul(G[0:2, tl.slot, T:T + SLAB], m["csil"][:, k, :], m["adaw"][:, k, :],
                                start=(k == 0), stop=(k == KT - 1))
            return ins

        def slab_turn(pe, tl, row):
            for b in (0, 1):
                ins = pe.transpose(G[:, tl.slot, T + 2 * b:T + 2 * b + 2], block(row[:, :], b), ident[0:2, 0:2])
            return ins

        def mods_at(l, t):
            return m["mods"][:, l, bass.ds(t, 2), :]

        def slab_out(dve, tl, l, t):
            bias = m["colB"][:, bass.ds(t + l * 48, 2)].rearrange("p (t a) -> p t a", a=1)
            return dve.tensor_tensor(mods_at(l, t), G[:, tl.slot, T:T + 4].rearrange("p (t a) -> p t a", a=2),
                                     bias.to_broadcast([P, 2, 2]), ALU.add)

        def done(eng, pn):
            eng.wait_ge(s["pan"], pn.n + 1)

        def squares_of(N):
            return ([m["sqb0"], m["sqb1"]], m["sumb"]) if N == 1 else (sq, hn[0])

        def square(act, N, xj, j, slot, nt):
            if 8 * N or j >= 2:
                act.wait_ge(s["sqd"], j + (8 * N - 1))
            act.activation(squares_of(N)[0][slot][:, 0:nt], xj, ACT.Square).then_inc(s["sq"], 1)

        def add_square(dve, N, j, slot, nt):
            total = squares_of(N)[1][:, 0:nt]
            dve.wait_ge(s["sq"], j + (8 * N + 1))
            if 8 * N or j:
                dve.wait_ge(s["sqd"], j + 8 * N)
            dve.tensor_tensor(total, total, squares_of(N)[0][slot][:, 0:nt], ALU.add).then_inc(s["sqd"], 1)

        def no_squares(dve, N, nt):
            dve.memset(squares_of(N)[1][:, 0:nt], 0.0)

        def tile_of(x_, j, nt):
            return x_[:, bass.ds(j, 1), 0:nt].rearrange("p a t -> p (a t)")

        def square_new(act, N, tl, j, nt):
            act.wait_ge(took[tl.slot], tl.turn + 1)
            square(act, N, tile_of(m["x1"], j, nt), j, tl.slot, nt)

        def norm_act(act, N, segs, l, i):
            for j in range(KT):
                act.wait_ge(s["hn"], 8 * N + j + 1)
                for g, (t0, n) in enumerate(segs):
                    ins = act.activation(m["hhi"][:, j, t0:t0 + n], hn[j % 2][:, t0:t0 + n], ACT.Identity,
                                         bias=mod(l, 3 * i, j, g))
                ins.then_inc(s["hhi"], 1)

        def norm_pe(pe, N, K, nb):
            pe.wait_ge(s["sqd"], 8 * (N + 1))
            for b in range(nb):
                ins = pe.matmul(S[:, 0, b:b + 1], block(squares_of(N)[1], b), ones[:, :], start=True, stop=True)
            ins.then_inc(s["ssum"], 1)
            spread_pe(pe, K, nb, PAIR[1])

        def spread_pe(pe, K, nb, to):
            pe.wait_ge(s["rstd"], K + 1)
            for b in range(nb):
                ins = pe.matmul(block(to, b), m["rstd"][:, b:b + 1].to_broadcast([P, P]), ident[:, :],
                                start=True, stop=True)
            ins.then_inc(s["rbc"], 1)

        def mean_dve(dve, nb, n):
            dve.tensor_scalar(m["stat"][:, 0:nb], S[:, 0, 0:nb], 1.0 / n, EPS, ALU.mult, ALU.add)\
               .then_inc(s["stat"], 1)

        def rsqrt_pool(pool, K, nb):
            pool.wait_ge(s["stat"], K + 1)
            pool.tensor_tensor(m["rstd"][:, 0:nb], m["stat"][:, 0:nb], m["mhalf"][:, 0:nb], ALU.pow)\
                .then_inc(s["rstd"], 1)

        def factors(dve, l, i):
            w = m["colA"][:, (l * 2 + i) * KT:(l * 2 + i + 1) * KT].rearrange("p (t a) -> p t a", a=1)
            dve.scalar_tensor_tensor(m["afac"][:, l, i, :, :], m["mods"][:, l, (3 * i + 1) * KT:(3 * i + 2) * KT, :],
                                     1.0, w.to_broadcast([P, KT, 2]), ALU.add, ALU.mult).then_inc(s["afac"], 1)
            dve.wait_ge(s["afac"], 2 * l + i + 1)

        def sums_dve(dve, N, segs):
            nt = segs[-1][0] + segs[-1][1]
            dve.wait_ge(s["ssum"], N + 1)
            mean_dve(dve, nt // P, D)

        def norm_dve(dve, xt, N, K, segs, l, i):
            sums_dve(dve, N, segs)
            dve.wait_ge(s["rbc"], K + 1)

            def scaled(j):
                if j >= 2:
                    dve.wait_ge(s["hlo"], 8 * N + j - 1)
                for g, (t0, n) in enumerate(segs):
                    ins = dve.scalar_tensor_tensor(hn[j % 2][:, t0:t0 + n], xt[:, j, t0:t0 + n],
                                                   m["afac"][:, l, i, j, g:g + 1], PAIR[1][:, t0:t0 + n],
                                                   ALU.mult, ALU.mult)
                ins.then_inc(s["hn"], 1)

            def low(j):
                dve.wait_ge(s["hhi"], 8 * N + j + 1)
                for g, (t0, n) in enumerate(segs):
                    ins = dve.scalar_tensor_tensor(m["hlo"][:, j, t0:t0 + n], hn[j % 2][:, t0:t0 + n],
                                                   mod(l, 3 * i, j, g), f32(m["hhi"][:, j, t0:t0 + n]),
                                                   ALU.add, ALU.subtract)
                ins.then_inc(s["hlo"], 1)

            for j in range(KT + 1):
                if j < KT:
                    scaled(j)
                if j:
                    low(j - 1)

        def h_need(pe, N):
            return lambda k: pe.wait_ge(s["hlo"], 8 * N + k + 1)

        def tile_ready(base):
            def ready(eng, j):
                tl = base + j
                eng.wait_ge(took[tl.slot], tl.turn + 1)
            return ready

        heads = HEADS
        th, lf, cum, kr, qr, qe, kd, gs, sin, gl, att, kdtm, mask = (
            [m[f"{n}{d}"] for d in (0, 1)]
            for n in ("th", "lf", "cum", "kr", "qr", "qe", "kd", "gs", "sin", "gl", "att", "kdtm", "mask"))

        def chunks(ap):
            return ap.rearrange("p (c l) -> p c l", l=CH)

        def by_parity(buf):
            return buf[:, :].rearrange("p (b q l) -> p q b l", q=2, l=CH)

        def at_token(ap, t):
            return chunks(ap)[:, :, t:t + 1].to_broadcast([P, NCH, CH])

        def ds_place(d, step):
            if step == 2:
                lot = [(0, c) for c in ORDER[0][8:-1]] + [(1, c) for c in ORDER[1][8:-1]]
            else:
                lot = [(d, c) for c in ORDER[d][:8]]
            seen, res = [0, 0], []
            for dd, cc in lot:
                res.append((dd, cc, cc % 2, seen[cc % 2]))
                seen[cc % 2] += 1
            return res

        def hg_tensor_scan(pe, hp, h, step):
            pair = PAIR[(step - 1) % 2]
            bank = 2 * ((step - 1) % 2)
            if step == 1:
                pe.wait_ge(s["og0"], h + 1)
                v = hp + 4
                pe.wait_ge(took[v.slot], v.turn + 1)
                for b in range(NBLK):
                    ins = pe.transpose(block(pair, b), block(m["vT"][:, :], b), ident[:, :])
            elif step in (2, 3):
                d = step - 2
                if step == 3:
                    pe.wait_ge(s["vtm"], h + 1)
                pe.wait_ge(s["kd"], 2 * h + d + 1)
                for b in range(NBLK):
                    ins = pe.transpose(block(pair, b), block(kd[d][:, :], b), ident[:, :])
            elif step == 4:
                pe.wait_ge(s["kdtm"], 2 * h + 1)
                pe.wait_ge(s["qk"], h + 1)
                H2 = CH // 2
                for d in (0, 1):
                    for c in range(NCH):
                        col, kc, qc = (NBLK * d + c // 2) * CH, chunks(kr[d][:, :])[:, c, :], chunks(qr[d][:, :])[:, c, :]
                        for half in (0, 1):
                            o = CH * (c % 2) + H2 * half
                            q0, q1 = (0, CH) if half == d else (H2 * half, H2 * half + H2)
                            ins = pe.matmul(pair[o:o + H2, col + q0:col + q1],
                                            kc[:, H2 * half:H2 * half + H2], qc[:, q0:q1],
                                            start=True, stop=True)
            elif step in (5, 6, 7):
                if step == 5:
                    pe.wait_ge(s["kdtm"], 2 * h + 2)
                elif step == 6:
                    pe.wait_ge(s["cp"], 2 * h + 2)
                else:
                    pe.wait_ge(s["sf"], 11 * h + 8)
                for d, cc, bk, pos in ds_place(step - 5, step - 5):
                    o = CH * (cc % 2)
                    ins = pe.matmul(S[:, bank + bk, pos * P:(pos + 1) * P], kdtm[d][o:o + CH, cc // 2, :],
                                    m["vtm"][o:o + CH, cc // 2, :], start=True, stop=True)
            elif step == 8:
                pe.wait_ge(s["sf"], 11 * h + 11)
                pe.wait_ge(s["sb"], 11 * h + 11)
                pe.wait_ge(s["att"], h + 1)
                for c in range(NCH):
                    o = CH * (c % 2)
                    to = S[:, bank + c % 2, (c // 2) * CH:(c // 2 + 1) * CH]
                    inter = [d for d in (0, 1) if c != ORDER[d][0]]
                    pe.matmul(to, m["vtm"][o:o + CH, c // 2, :], m["attS"][o:o + CH, c // 2, :],
                              start=True, stop=False)
                    for d in inter:
                        ins = pe.matmul(to, sin[d][:, c, :], chunks(qe[d][:, :])[:, c, :],
                                        start=False, stop=(d == inter[-1]))
            elif step == 9:
                pe.wait_ge(s["osq"], h + 1)
                for b in range(NBLK):
                    ins = pe.matmul(S[:, 0, b:b + 1], block(m["osq"][:, :], b), ones[:, :],
                                    start=True, stop=True)
            else:
                spread_pe(pe, h + 1, NBLK, pair)
                return
            ins.then_inc(s["step"], 1)

        STEP_AT = {(0, 5): 1, (1, 0): 2, (1, 3): 3, (1, 6): 4, (2, 1): 5, (2, 3): 6, (2, 6): 7, (3, 3): 8,
                   (3, 7): 9, (4, 1): 10}

        def hg_tensor(pe, hg, hn_, hp, h, pn_par, ps_par):
            def scan(j, k):
                if h is not None and (j, k) in STEP_AT:
                    hg_tensor_scan(pe, hp, h, STEP_AT[j, k])

            for j in range(5):
                if hg is not None:
                    pn = hg + j
                    product(pe, pn, pn, m["hhi"], m["hlo"], KT, SEGS,
                            need=h_need(pe, 0) if h is None and j == 0 else None,
                            rows=hn_ * 2 + j // 2 if j in (0, 2) else None,
                            turn=m["mrow0"] if j in (1, 3) else None, between=lambda k: scan(j, k))
                else:
                    for k in range(KT):
                        scan(j, k)

        def step_done(eng, h, step):
            eng.wait_ge(s["step"], 9 * h + step)

        def hg_scalar(act, hg, hn_, hp, h, pn_par, ps_par):
            def take(pn, j):
                split_hi(act, pn + 2, KT)
                tile = G[:, pn.slot, 0:T]
                if j == 0:
                    if h is not None:
                        act.wait_ge(s["qk"], hn_)
                    ins = act.activation(m["qs"][:, :], tile, ACT.Silu)
                elif j == 1:
                    ins = act.activation(gs[pn_par][:, :], tile, ACT.Silu)
                elif j in (2, 3):
                    ins = act.activation(th[j - 2][:, :], tile, ACT.Tanh, scale=0.5)
                else:
                    ins = act.activation(m["vT"][:, :], tile, ACT.Copy)
                if j in (0, 2):
                    ins = act.activation(m["mrow0"][:, :], G[0:2, pn.slot, T:T + SLAB], ACT.Copy)
                elif j in (1, 3):
                    for b in (0, 1):
                        t = hn_ * 4 + ((j - 1) + b)
                        ins = act.activation(m["mods"][:, 0, bass.ds(t + 2 * KT, 1), :].rearrange("p a c -> p (a c)"),
                                             G[:, pn.slot, T + 2 * b:T + 2 * b + 2], ACT.Identity,
                                             bias=m["colB"][:, bass.ds(t + 2 * KT, 1)])
                ins.then_inc(took[pn.slot], 1)

            def decays(head, d):
                act.wait_ge(s["dif"], 4 * head + 2 * d + 1)
                act.activation(qr[d][:, :], kr[d][:, :], ACT.Exp).then_inc(s["eq"], 1)
                act.activation(qe[d][:, :], cum[d][:, :], ACT.Exp)
                act.activation(gl[d][:, :], chunks(cum[d][:, :])[:, :, LAST[d]], ACT.Exp)
                act.wait_ge(s["dif"], 4 * head + 2 * d + 2)
                act.activation(kd[d][:, :], kd[d][:, :], ACT.Exp, scale=-1.0)
                act.wait_ge(s["eq"], 2 * head + d + 1)
                act.activation(kr[d][:, :], kr[d][:, :], ACT.Exp, scale=-1.0).then_inc(s["ex"], 1)

            for j in range(5):
                if j and hg is not None:
                    take(hg + (j - 1), j - 1)
                if j == 0 and h is not None:
                    take(hp + 4, 4)
                    decays(h, 1)
                    step_done(act, h, 1)
                    act.activation(m["vtm"][:, :, :].rearrange("p b n -> p (b n)"), PAIR[0][:, 0:T],
                                   ACT.Copy).then_inc(s["vtm"], 1)
                if j == 1 and h is not None:
                    for d in (0, 1):
                        step_done(act, h, 2 + d)
                        act.activation(kdtm[d][:, :, :].rearrange("p b n -> p (b n)"),
                                       PAIR[1 - d][:, 0:T], ACT.Copy).then_inc(s["kdtm"], 1)
                if j == 3 and h is not None:
                    step_done(act, h, 8)
                    o4 = S[:, 2:4, 0:NBLK * CH].rearrange("p q (b l) -> p q b l", l=CH)
                    act.activation(by_parity(m["osb"]), o4, ACT.Copy)
                    act.activation(by_parity(m["osq"]), o4, ACT.Square).then_inc(s["osq"], 1)
                if j == 4 and hg is not None:
                    for d in (0, 1):
                        act.wait_ge(s["sig"], 4 * hn_ + d + 1)
                        act.activation(lf[d][:, :], lf[d][:, :], ACT.Ln, bias=m["lb"][:, d, bass.ds(hn_, 1)],
                                       scale=m["oml"][:, d, bass.ds(hn_, 1)]).then_inc(s["lf"], 1)
                    decays(hn_, 0)

        def states(dve, h, step):
            bank = 2 * ((step - 1) % 2)
            for d, cc, bk, pos in ds_place(step - 5, step - 5):
                i = ORDER[d].index(cc)
                to, new = sin[d][:, ORDER[d][i + 1], :], S[:, bank + bk, pos * P:(pos + 1) * P]
                own = s["sf" if d == 0 else "sb"]
                if i == 0:
                    dve.tensor_copy(to, new).then_inc(own, 1)
                else:
                    dve.wait_ge(own, 11 * h + i)
                    dve.scalar_tensor_tensor(to, sin[d][:, cc, :], gl[d][:, cc:cc + 1], new,
                                             ALU.mult, ALU.add).then_inc(own, 1)

        def hg_vector(dve, hg, hn_, hp, h, pn_par, ps_par):
            for j in range(5):
                if j and hg is not None:
                    split_lo(dve, hg + (j + 1), KT)
                if j == 0 and h is not None:
                    split_lo(dve, hp + 6, KT)
                    dve.wait_ge(s["sig"], 4 * h + 4)
                    for d in (0, 1):
                        dve.wait_ge(s["ex"], 2 * h + d + 1)
                        o = m["oml"][:, d, bass.ds(h, 1)]
                        dve.scalar_tensor_tensor(kd[d][:, :], kd[d][:, :], o, th[d][:, :], ALU.mult, ALU.mult)\
                            .then_inc(s["kd"], 1)
                        dve.scalar_tensor_tensor(kr[d][:, :], kr[d][:, :], o, th[d][:, :], ALU.mult, ALU.mult)
                        dve.tensor_tensor(qr[d][:, :], qr[d][:, :], m["qs"][:, :], ALU.mult)
                        ins = dve.tensor_tensor(qe[d][:, :], qe[d][:, :], m["qs"][:, :], ALU.mult)
                    ins.then_inc(s["qk"], 1)
                if j == 1 and h is not None:
                    step_done(dve, h, 4)
                    dve.memset(m["carry"][:, :], 0.0)
                    for d in (0, 1):
                        dve.copy_predicated(att[d][:, :, :], mask[d][:, :, :].bitcast(I32),
                                            PAIR[1][:, d * NBLK * CH:(d + 1) * NBLK * CH].rearrange("p (b l) -> p b l", l=CH))\
                            .then_inc(s["cp"], 1)
                    dve.wait_ge(s["cp"], 2 * h + 2)
                    dve.tensor_tensor(m["attS"][:, :, :], att[0][:, :, :], att[1][:, :, :], ALU.add)\
                        .then_inc(s["att"], 1)
                if j == 2 and h is not None:
                    for step in (5, 6, 7):
                        step_done(dve, h, step)
                        states(dve, h, step)
                if j == 3 and h is not None:
                    step_done(dve, h, 9)
                    mean_dve(dve, NBLK, P)
                if j == 4 and hg is not None:
                    for d in (0, 1):
                        tl = hg + 2 + d
                        dve.wait_ge(took[tl.slot], tl.turn + 1)
                        dve.tensor_scalar(lf[d][:, :], th[d][:, :], 0.5, 0.5, ALU.mult, ALU.add)\
                            .then_inc(s["sig"], 1)
                    for d in (0, 1):
                        dve.wait_ge(s["sig"], 4 * hn_ + d + 1)
                        dve.tensor_scalar(th[d][:, :], th[d][:, :], -0.5, 0.5, ALU.mult, ALU.add)\
                            .then_inc(s["sig"], 1)
                if j == 4 and h is not None:
                    dve.wait_ge(s["rbc"], h + 2)
                    dve.scalar_tensor_tensor(m["osb"][:, :], m["osb"][:, :], m["colA"][:, COL_GN:COL_GN + 1],
                                             PAIR[1][:, 0:T], ALU.mult, ALU.mult).then_inc(s["og0"], 1)
                if j == 4 and hg is not None:
                    for d in (0, 1):
                        back = slice(None, None, -1 if d else 1)
                        dve.wait_ge(s["lf"], 2 * hn_ + d + 1)
                        dve.tensor_tensor_scan(cum[d][:, back], m["segm"][:, :], lf[d][:, back], 0.0,
                                               ALU.mult, ALU.add).then_inc(s["cum"], 1)
                    for d in (0, 1):
                        dve.wait_ge(s["cum"], 2 * hn_ + d + 1)
                        for to, t in ((kr, REF[d]), (kd, LAST[d])):
                            dve.tensor_tensor(chunks(to[d][:, :]), chunks(cum[d][:, :]),
                                              at_token(cum[d][:, :], t), ALU.subtract).then_inc(s["dif"], 1)
                if j == 4 and h is not None:
                    dve.wait_ge(s["og0"], h + 2)
                    dve.tensor_tensor(m["og"][:, bass.ds(h, 1), :].rearrange("p a t -> p (a t)"),
                                      m["osb"][:, :], gs[ps_par][:, :], ALU.mult).then_inc(s["og"], 1)

        def hg_all(eng, one):
            one(At(PAN_HG), 0, None, None, 0, 0)
            with eng.Fori(0, (HEADS - 2) // 2) as i:
                for u in (0, 1):
                    one(At(PAN_HG + 5 * (u + 1), i * 5), i * 2 + (u + 1), At(PAN_HG + 5 * u, i * 5), i * 2 + u,
                        1 - u, u)
            one(At(PAN_HG + 5 * (HEADS - 1)), HEADS - 1, At(PAN_HG + 5 * (HEADS - 2)), HEADS - 2, 1, 0)
            one(None, None, At(PAN_HG + 5 * (HEADS - 1)), HEADS - 1, 0, 1)

        def ffn_at(l, hf):
            return At((PAN_F0, PAN_F1)[l] + hf * (2 * FH + KT)), At((PAN_F0, TIL_F1)[l] + hf * (2 * FH + KT))

        def ffn_loop(eng, gate_up, down, l):
            for hf in (0, 1):
                pn, tl = ffn_at(l, hf)
                done_before = (2 * l + hf) * FH
                with eng.Fori(0, FH - 1) as i:
                    gate_up(At(pn.c, i), At(tl.c, i), i, i + done_before, KT, hf)
                gate_up(pn + 2 * (FH - 1), tl + 2 * (FH - 1), FH - 1, FH - 1 + done_before, FH, hf)
                pn, tl = pn + 2 * FH, tl + 2 * FH
                with eng.Fori(0, KT // 2 - 1) as i:
                    for u in (0, 1):
                        down(At(pn.c + u, i), At(tl.c + u, i), i * 2 + u, FH, hf)
                for j in (KT - 2, KT - 1):
                    ahead = KT if (l, hf) != (1, 1) else None
                    down(pn + j, tl + j, j, ahead, hf)

        def ffn_tensor(pe, l, segs):
            def gate_up(pn, tl, i, cnt, ahead, hf):
                norm = 1 + 2 * l
                peeled = isinstance(i, int)
                need = h_need(pe, norm) if hf == 0 else None
                slab = l == 0 and not peeled
                product(pe, pn, tl, m["hhi"], m["hlo"], KT, segs, need=need,
                        rows=i + (SL_F0 + hf * (FH - 1)) if slab else None)
                product(pe, pn + 1, tl + 1, m["hhi"], m["hlo"], KT, segs,
                        turn=m["mrow1"] if slab else None)

            def down(pn, tl, j, ahead, hf):
                product(pe, pn, tl, m["mhi"], m["mlo"], FH, segs,
                        need=lambda k: pe.wait_ge(s["mlo"], (2 * l + hf) * FH + k + 1))

            ffn_loop(pe, gate_up, down, l)

        def ffn_scalar(act, l, segs):
            nt = segs[-1][0] + segs[-1][1]

            def gate_up(pn, tl, i, cnt, ahead, hf):
                split_hi(act, pn + 2, ahead)
                ins = act.activation(m["act0"][:, 0:nt], G[:, tl.slot, 0:nt], ACT.Silu)
                if l == 0 and not isinstance(i, int):
                    ins = act.activation(m["mrow1"][:, :], G[0:2, tl.slot, T:T + SLAB], ACT.Copy)
                ins.then_inc(took[tl.slot], 1)
                split_hi(act, pn + 3, ahead)
                up = tl + 1
                act.wait_ge(took[up.slot], up.turn + 1)
                act.activation(m["mhi"][:, bass.ds(i, 1), 0:nt].rearrange("p a t -> p (a t)"),
                               m["mid0"][:, 0:nt], ACT.Copy).then_inc(s["mhi"], 1)

            def down(pn, tl, j, ahead, hf):
                if ahead:
                    split_hi(act, pn + 2, ahead)
                if hf:
                    square_new(act, 2 * l + 2, tl, j, nt)

            ffn_loop(act, gate_up, down, l)

        def ffn_vector(dve, l, segs):
            nt = segs[-1][0] + segs[-1][1]

            def gate_up(pn, tl, i, cnt, ahead, hf):
                split_lo(dve, pn + 2, ahead)
                split_lo(dve, pn + 3, ahead)
                up = tl + 1
                dve.wait_ge(took[tl.slot], tl.turn + 1)
                if l == 0 and not isinstance(i, int):
                    slab_out(dve, up, 1, i * 2 + 2 * (SL_F0 - SL_HGO + hf * (FH - 1)))
                dve.tensor_tensor(m["mid0"][:, 0:nt], m["act0"][:, 0:nt], G[:, up.slot, 0:nt], ALU.mult)\
                    .then_inc(took[up.slot], 1)
                dve.wait_ge(s["mhi"], cnt + 1)
                dve.tensor_tensor(m["mlo"][:, bass.ds(i, 1), 0:nt].rearrange("p a t -> p (a t)"),
                                  m["mid0"][:, 0:nt],
                                  f32(m["mhi"][:, bass.ds(i, 1), 0:nt]).rearrange("p a t -> p (a t)"),
                                  ALU.subtract).then_inc(s["mlo"], 1)
                dve.wait_ge(s["mlo"], cnt + 1)
                if hf and isinstance(i, int):
                    no_squares(dve, 2 * l + 2, nt)

            def down(pn, tl, j, ahead, hf):
                if ahead:
                    split_lo(dve, pn + 2, ahead)
                else:
                    done(dve, pn)
                add_gated(dve, tl, j, l, 5, segs)
                if hf:
                    add_square(dve, 2 * l + 2, j, tl.slot, nt)

            ffn_loop(dve, gate_up, down, l)

        def add_gated(dve, tl, j, l, part, segs):
            for g, (t0, n) in enumerate(segs):
                xj = m["x1"][:, bass.ds(j, 1), t0:t0 + n].rearrange("p a t -> p (a t)")
                gate = m["mods"][:, l, bass.ds(j + part * KT, 1), g:g + 1].rearrange("p a b -> p (a b)")
                ins = dve.scalar_tensor_tensor(xj, G[:, tl.slot, t0:t0 + n], gate, xj, ALU.mult, ALU.add)
            ins.then_inc(took[tl.slot], 1)

        def ffn_sync(sp, l):
            w_in, w_out = ffn_w_in[l], ffn_w_out[l]

            def gate_up(pn, tl, i, cnt, ahead, hf):
                load_panel(sp, pn, cols_of(w_in, i * P + hf * FH * P), KT)
                load_panel(sp, pn + 1, cols_of(w_in, i * P + (FFN + hf * FH * P)), KT)
                if l == 0 and not isinstance(i, int):
                    a = i + (SL_F0 + hf * (FH - 1))
                    slab_load(sp, a, 1, i * SLAB + (SL_F0 - SL_HGO + hf * (FH - 1)) * SLAB, pn + (-2), norms=2)

            def down(pn, tl, j, ahead, hf):
                load_panel(sp, pn, cols_of(w_out[hf * FH * P:(hf + 1) * FH * P, :], j * P), FH)

            ffn_loop(sp, gate_up, down, l)

        ada, arow = (m["ada0"], m["ada1"]), (m["arow0"], m["arow1"])

        def slab_sync(sp, n):
            if n >= 2:
                sp.wait_ge(s["ada"], n - 1)
            sp.dma_start(ada[n % 2][:, :, :], ada_w[0][:, n * 512:(n + 1) * 512].rearrange("(k p) n -> p k n", p=P))\
                .then_inc(s[f"slab{n % 2}"], 16)

        def slabs_tensor(pe, pair):
            for n in (0, 1):
                pe.wait_ge(s[f"slab{n}"], 16 * (pair + 1))
                if pair:
                    pe.wait_ge(s["modev"], 4)
                for k in range(KT):
                    ins = pe.matmul(S[0:2, n, :], m["csil"][:, k, :], ada[n][:, k, :], start=(k == 0),
                                    stop=(k == KT - 1))
                ins.then_inc(s["ada"], 1)
            for n in (0, 1):
                pe.wait_ge(s["modev"], 4 * pair + n + 1)
                for b in range(4):
                    ins = pe.transpose(S[:, 2 + n, 2 * b:2 * b + 2], block(arow[n][:, :], b), ident[0:2, 0:2])
                ins.then_inc(s["ada"], 1)

        def slabs_vector(dve, pair):
            for n in (0, 1):
                dve.wait_ge(s["ada"], 4 * pair + n + 1)
                dve.tensor_copy(arow[n][:, :], S[0:2, n, :]).then_inc(s["modev"], 1)
            for n in (0, 1):
                dve.wait_ge(s["ada"], 4 * pair + n + 3)
                t = (2 * pair + n) * 4
                bias = m["colB"][:, t:t + 4].rearrange("p (t a) -> p t a", a=1)
                dve.tensor_tensor(m["mods"][:, 0, t:t + 4, :], S[:, 2 + n, 0:8].rearrange("p (t a) -> p t a", a=2),
                                  bias.to_broadcast([P, 4, 2]), ALU.add).then_inc(s["modev"], 1)

        N_CONST = 11
        LAT = SEGS[:1]
        N2, K2 = 2, HEADS + 2
        xpad = (m["xpad0"], m["xpad1"])
        PANELS = [("x", i) for i in range(GT)] + [("b", 0), ("c", 0)] + [("z", i) for i in range(GT)]
        CONVS = PANELS[:GT + 2]
        CONV_TILES = (DI + 2 * GROUPS * P) // P

        def ss_cols(kind, i, g):
            start = {"z": i * P, "b": BC0, "c": CC0, "x": XBC0 + i * P}[kind]
            width = P if kind in "bc" else GW
            return (g + (-1)) * width + (start + width)

        def conv_tile(kind, i, g):
            return {"x": g * GT + i, "b": g + NH // 2, "c": g + (NH // 2 + GROUPS)}[kind]

        def conv_to(kind, i):
            return {"b": m["bfm"][:, :], "c": m["cfm"][:, :]}[kind] if kind in "bc" else m["xfm"][:, i, :]

        def per_head(t, b, d, g):
            return t[:, b, bass.ds(g * HPG + d * NH, HPG)].rearrange("p (h a) -> p h a", a=1)\
                .to_broadcast([P, HPG, HP])

        def hd(ap):
            return ap.rearrange("p (h c) -> p h c", c=HP)

        def dt_scalar(act):
            act.wait_ge(s["parked1"], 16)
            pn = At(PAN_DT)
            split_hi(act, pn + 2, KT)
            zt, za, e, ln = (m[n] for n in ("xpad0", "xpad1", "acc", "bfm"))
            act.activation(zt[0:2 * NH, 0:T], G[P - 2 * NH:P, pn.slot, 0:T], ACT.Copy).then_inc(took[pn.slot], 1)
            act.wait_ge(s["small"], 64)
            act.activation(m["aneg"][:, 1:2], m["aneg"][:, 0:1], ACT.Exp).then_inc(s["dts"], 1)
            act.wait_ge(s["dtv"], 1)
            act.activation(e[0:2 * NH, 0:T], za[0:2 * NH, 0:T], ACT.Abs).then_inc(s["dts"], 1)
            act.wait_ge(s["dts"], 2)
            act.activation(zt[0:2 * NH, 0:T], e[0:2 * NH, 0:T], ACT.Exp, scale=-1.0).then_inc(s["dts"], 1)
            act.wait_ge(s["dts"], 3)
            act.activation(ln[0:2 * NH, 0:T], zt[0:2 * NH, 0:T], ACT.Ln, bias=1.0).then_inc(s["dts"], 1)
            act.wait_ge(s["dtv"], DT_LOG)
            act.activation(ln[0:2 * NH, 0:T], ln[0:2 * NH, 0:T], ACT.Ln).then_inc(s["dts"], 1)
            act.wait_ge(s["dtv"], DT_D)
            act.activation(zt[0:2 * NH, 0:T], za[0:2 * NH, 0:T], ACT.Exp, scale=-1.0).then_inc(s["dts"], 1)
            act.activation(m["cuhi"][:, :], m["cumS"][:, 0:NLAT], ACT.Copy).then_inc(s["dts"], 1)
            act.wait_ge(s["pdt"], 1)
            act.activation(m["ecT"][:, :, :].rearrange("p b h -> p (b h)"), PAIR[0][:, 0:NBLK * 2 * NH], ACT.Exp)
            act.activation(m["shiftT"][:, :, :].rearrange("p b h -> p (b h)"),
                           PAIR[0][:, NBLK * 2 * NH:2 * NBLK * 2 * NH], ACT.Copy)
            act.activation(m["wT"][:, :, :].rearrange("p b h -> p (b h)"), PAIR[1][:, 0:NBLK * 2 * NH], ACT.Copy)
            act.activation(m["dec"][:, :, :].rearrange("p b h -> p (b h)"),
                           PAIR[1][:, NBLK * 2 * NH:2 * NBLK * 2 * NH], ACT.Exp).then_inc(s["dtT"], 1)

        DT_LOG, DT_D = 11, 18

        def dt_vector(dve):
            n = [0]

            def link(ins):
                n[0] += 1
                ins.then_inc(s["dtv"], 1)
                dve.wait_ge(s["dtv"], n[0])

            pn = At(PAN_DT)
            dve.wait_ge(s["parked1"], 16)
            split_lo(dve, pn + 2, KT)
            zt, z, e, ln, den, iz = (m[n_][0:2 * NH, 0:T] for n_ in ("xpad0", "xpad1", "acc", "bfm", "dt", "cumS"))
            t2 = m["cfm"][0:2 * NH, 0:T]
            dve.wait_ge(took[pn.slot], pn.turn + 1)
            dve.wait_ge(s["small"], 64)
            link(dve.tensor_scalar(z, zt, m["dtb"][:, 0:1], None, ALU.add))
            dve.wait_ge(s["dts"], 3)
            link(dve.tensor_scalar(den, zt, 1.0, -1.0, ALU.add, ALU.add))
            link(dve.tensor_scalar(iz, den, 0.0, None, ALU.is_equal))
            link(dve.tensor_tensor(den, den, iz, ALU.add))
            link(dve.reciprocal(t2, den))
            link(dve.tensor_tensor(t2, t2, zt, ALU.mult))
            dve.wait_ge(s["dts"], 4)
            link(dve.tensor_tensor(ln, ln, t2, ALU.mult))
            link(dve.tensor_tensor(t2, iz, zt, ALU.mult))
            link(dve.tensor_tensor(ln, ln, t2, ALU.add))
            link(dve.scalar_tensor_tensor(den, z, 0.0, ln, ALU.max, ALU.add))
            link(dve.tensor_scalar(ln, den, 1e-38, None, ALU.max))
            assert n[0] == DT_LOG
            link(dve.tensor_scalar(m["aneg"][:, 2:3], m["aneg"][:, 1:2], -1.0, None, ALU.mult))
            link(dve.tensor_scalar(t2, den, m["aneg"][:, 2:3], None, ALU.mult))
            dve.wait_ge(s["negm"], 3)
            for d in (0, 1):
                r = slice(d * NH, (d + 1) * NH)
                back = slice(None, None, -1 if d else 1)
                link(dve.tensor_tensor_scan(m["cumS"][r, back], m["segm"][r, :], m["cfm"][r, back], 0.0,
                                            ALU.mult, ALU.add))
            cum3 = m["cumS"][:, :].rearrange("h (b t) -> h b t", t=P)
            for d in (0, 1):
                r = slice(d * NH, (d + 1) * NH)
                t = 0 if d else P - 1
                ins = dve.tensor_copy(m["cl"][r, :], cum3[r, :, t])
            link(ins)
            for d in (0, 1):
                r = slice(d * NH, (d + 1) * NH)
                ins = dve.tensor_tensor(m["xpad1"][r, 0:T].rearrange("h (b t) -> h b t", t=P), cum3[r, :, :],
                                        m["cl"][r, :].rearrange("h (b a) -> h b a", a=1).to_broadcast([NH, NBLK, P]),
                                        ALU.subtract)
                if d == 0:
                    link(ins)
            link(ins)
            assert n[0] == DT_D, n
            dve.wait_ge(s["dts"], 7)
            dve.tensor_tensor(ln, ln, m["cumS"][:, :], ALU.subtract)
            dve.tensor_tensor(m["culo"][:, :], m["cumS"][:, 0:NLAT], f32(m["cuhi"][:, :]), ALU.subtract)
            dve.tensor_tensor(zt, zt, den, ALU.mult).then_inc(s["ynorm"], 1)

        def dt_tensor(pe):
            pn = At(PAN_DT)
            product(pe, pn, pn, m["hhi"], m["hlo"], KT, SEGS, need=h_need(pe, N2))

        def dt_turn(pe):
            pe.wait_ge(s["ynorm"], 1)
            H2 = 2 * NH
            for i, src in enumerate(("cumS", "bfm", "xpad0")):
                for b in range(NBLK):
                    pe.transpose(PAIR[i // 2][:, ((i % 2) * NBLK + b) * H2:((i % 2) * NBLK + b + 1) * H2],
                                 m[src][0:H2, b * P:(b + 1) * P], ident[0:H2, 0:H2])
            for b in range(NBLK):
                ins = pe.matmul(PAIR[1][:, (NBLK + b) * H2:(NBLK + b + 1) * H2],
                                m["cl"][:, b:b + 1].to_broadcast([H2, P]), ident[0:H2, 0:H2],
                                start=True, stop=True)
            ins.then_inc(s["pdt"], 1)

        def chain_at(n):
            return n % 2, n // 2, BORDER[n % 2][n // 2]

        def state(q, k):
            return 9 * q + 2 * k - 1

        states_of = (s["stf"], s["stb"])

        def ss_scalar(act, ss, g, q, prev):
            def convolved(ci):
                kind, i = CONVS[ci]
                act.wait_ge(s["tap"], 24 * g + 4 * ci + 4)
                to = conv_to(kind, i)
                ins = act.activation(to[:, 0:NLAT], m["acc"][:, 0:NLAT], ACT.Silu)
                if kind != "c":
                    ins = act.activation(to[:, NLAT:T], m["acc"][:, NLAT + 2:T + 2], ACT.Silu)
                ins.then_inc(s["conv"], 1)

            def pair_decays(hh):
                r = hh % 2
                act.wait_ge(s["sm"], HPG * q + hh + 1)
                if hh >= 2:
                    act.wait_ge(s["yd"], HPG * q + hh - 1)
                for d in (0, 1):
                    for b in range(LBLK):
                        ins = act.activation(block(m[f"e{d}{r}"][:, :], b), block(S[:, d, :], b), ACT.Exp,
                                             bias=m["shiftT"][:, b, bass.ds(q * HPG + (d * NH + hh), 1)])
                ins.then_inc(s["em"], 1)

            for j in range(len(PANELS)):
                before = (ss + j + (-1) if j else prev) if ss is not None else (prev if j == 0 else None)
                kind, i = PANELS[j - 1]
                gg = g if j else q
                ci = CONVS.index((kind, i)) if before is not None and kind != "z" else None
                if before is not None:
                    split_hi(act, before + 2, KT)
                    if kind == "z":
                        act.activation(m["z"][:, bass.ds(gg % 2, 1), i, :].rearrange("p a t -> p (a t)"),
                                       G[:, before.slot, 0:NLAT], ACT.Silu).then_inc(took[before.slot], 1)
                    else:
                        xp, ct = xpad[ci % 2], conv_tile(kind, i, gg)
                        n = NLAT if kind == "c" else T + 2
                        ins = act.activation(xp[:, 2:2 + NLAT], G[:, before.slot, 0:NLAT], ACT.Copy)
                        if kind != "c":
                            ins = act.activation(xp[:, 4 + NLAT:4 + T], G[:, before.slot, NLAT:T], ACT.Copy)
                        ins.then_inc(took[before.slot], 1)
                        if q is not None and 3 <= j < 7:
                            pair_decays(2 * (j - 3))
                        if ci:
                            convolved(ci - 1)
                        if ci or q is not None:
                            act.wait_ge(s["conv"], 6 * g + ci)
                        act.wait_ge(took[before.slot], before.turn + 1)
                        act.activation(m["acc"][:, 0:n], xp[:, 0:n], ACT.Identity,
                                       bias=m["colA"][:, bass.ds(ct + COL_CB, 1)],
                                       scale=m["colC"][:, bass.ds(ct, 1)]).then_inc(s["xp"], 1)
                if ss is not None and j == len(CONVS) + 1:
                    convolved(len(CONVS) - 1)
                if q is not None and j == 0:
                    act.wait_ge(s["yout"], 16 * q + 16)
                    for i_ in range(GT):
                        act.activation(m["yb"][:, i_, :], m["xfm"][:, i_, 0:NLAT], ACT.Identity,
                                       scale=m["dsk"][:, bass.ds(q * GT + i_, 1)])
                if q is not None and 3 <= j < 7:
                    if before is None:
                        pair_decays(2 * (j - 3))
                    pair_decays(2 * (j - 3) + 1)
                if q is not None and j == 7:
                    for i_ in range(GT):
                        act.wait_ge(s["yz"], GT * q + i_ + 1)
                        if i_ >= 2:
                            act.wait_ge(s["yr"], GT * q + i_ - 1)
                        act.activation(m[f"sc{i_ % 2}"][:, :], m["yb"][:, i_, :], ACT.Square).then_inc(s["ysq"], 1)
                if ss is not None and j == 9:
                    act.wait_ge(s["ytr"], 6 * g + 1)
                    act.activation(m["btm"][:, :, :].rearrange("p b n -> p (b n)"), PAIR[0][:, 0:T], ACT.Copy)\
                        .then_inc(s["stc"], 1)
                    act.wait_ge(s["ytr"], 6 * g + 2)
                    act.activation(m["cb"][:, :], S[:, 2, :], ACT.Copy).then_inc(s["stc"], 1)
                    for i_ in range(GT):
                        act.wait_ge(s["ytr"], 6 * g + 3 + i_)
                        act.activation(m["xtm"][:, :, i_ * P:(i_ + 1) * P],
                                       PAIR[i_ % 2][:, 0:T].rearrange("p (b n) -> p b n", n=P), ACT.Copy)\
                            .then_inc(s["stc"], 1)

        def chain_values(dve, q, n):
            d, k, b = chain_at(n)
            if n == 0:
                dve.wait_ge(s["stc"], 6 * q + 6)
            if k < NBLK - 1:
                dve.tensor_tensor(hd(m[f"wx{d}"][:, :]), hd(m["xtm"][:, b, :]), per_head(m["wT"], b, d, q),
                                  ALU.mult).then_inc(s["xw"], 1)

        def chain_vector(dve, q, n):
            d, k, b = chain_at(n)
            st, own = m[f"st{d}"], states_of[d]
            if n == 0:
                chain_values(dve, q, 0)
            if n + 1 < 2 * NBLK:
                chain_values(dve, q, n + 1)
            if b < LBLK:
                dve.wait_ge(s["yo"], 2 * LBLK * q + 2 * (k - 2) + d + 1)
                if k < 4:
                    dve.tensor_tensor(hd(m["ytm"][:, b, :]), hd(S[:, 2 + d, :]),
                                      per_head(m["ecT"], b, d, q), ALU.mult).then_inc(s["ymc"], 1)
                else:
                    dve.tensor_tensor(hd(m["sc0"][:, :]), hd(S[:, 2 + d, :]),
                                      per_head(m["ecT"], b, d, q), ALU.mult).then_inc(s["ymc"], 1)
            if 0 < k < NBLK - 1:
                dve.wait_ge(own, state(q, k))
                dve.tensor_tensor(hd(st[:, :]), hd(st[:, :]), per_head(m["dec"], b, d, q), ALU.mult)\
                    .then_inc(own, 1)
            if b < LBLK and k >= 4:
                y0 = 12 * q + 4 + 4 * (k - 4) + 2 * d
                dve.wait_ge(s["ymc"], y0 + 1)
                dve.tensor_tensor(m["ytm"][:, b, :], m["ytm"][:, b, :], m["sc0"][:, :], ALU.add)\
                    .then_inc(s["ymc"], 1)
                dve.wait_ge(s["ymc"], y0 + 2)
            if k < NBLK - 1:
                dve.wait_ge(s["ds"], 2 * (NBLK - 1) * q + 2 * k + d + 1)
                if k == 0:
                    dve.tensor_copy(st[:, :], S[:, d, :]).then_inc(own, 1)
                else:
                    dve.wait_ge(own, state(q, k) + 1)
                    dve.tensor_tensor(st[:, :], st[:, :], S[:, d, :], ALU.add).then_inc(own, 1)

        def chain_tensor(pe, q, n):
            d, k, b = chain_at(n)
            if k:
                pe.wait_ge(states_of[d], state(q, k))
            if b < LBLK:
                pe.matmul(S[:, 2 + d, :], block(m["cfm"][:, :], b), m[f"st{d}"][:, :],
                          start=True, stop=True).then_inc(s["yo"], 1)
            if k < NBLK - 1:
                pe.wait_ge(s["xw"], 2 * (NBLK - 1) * q + 2 * k + d + 1)
                pe.matmul(S[:, d, :], m["btm"][:, b, :], m[f"wx{d}"][:, :],
                          start=True, stop=True).then_inc(s["ds"], 1)

        def head_weights(dve, q, hh):
            r = hh % 2
            dve.wait_ge(s["em"], HPG * q + hh + 1)
            e0, e1 = m[f"e0{r}"][:, :], m[f"e1{r}"][:, :]
            dve.tensor_tensor(e0, e0, e1, ALU.add).then_inc(s["mm"], 1)
            dve.wait_ge(s["mm"], 2 * (HPG * q + hh) + 1)
            dve.tensor_tensor(e0, e0, m["cb"][:, :], ALU.mult).then_inc(s["mm"], 1)

        def head_out(dve, q, hh):
            dve.wait_ge(s["yd"], HPG * q + hh + 1)
            yt = m["ytm"][:, :, hh * HP:(hh + 1) * HP]
            dve.tensor_tensor(yt, yt, S[:, 2 + hh % 2, 0:LBLK * HP].rearrange("p (b c) -> p b c", c=HP),
                              ALU.add).then_inc(s["ym2"], 1)

        def ss_vector(dve, ss, g, q, prev):
            for j in range(len(PANELS)):
                before = (ss + j + (-1) if j else prev) if ss is not None else (prev if j == 0 else None)
                kind, i = PANELS[j - 1]
                ci = CONVS.index((kind, i)) if before is not None and kind != "z" else None

                def tap(k):
                    if ci is None:
                        return
                    if k == 1:
                        dve.wait_ge(s["xp"], 6 * g + ci + 1)
                    else:
                        dve.wait_ge(s["tap"], 24 * g + 4 * ci + k - 1)
                    n = NLAT if kind == "c" else T + 2
                    dve.scalar_tensor_tensor(m["acc"][:, 0:n], xpad[ci % 2][:, k:k + n],
                                             m["colC"][:, bass.ds(conv_tile(kind, i, g) + k * CONV_TILES, 1)],
                                             m["acc"][:, 0:n], ALU.mult, ALU.add).then_inc(s["tap"], 1)

                if before is not None:
                    split_lo(dve, before + 2, KT)
                if q is not None and j == 0:
                    for d in (0, 1):
                        ins = dve.tensor_copy(m["sel"][:, d * HPG:(d + 1) * HPG],
                                              ident[0:2 * NH, bass.ds(q * HPG + d * NH, HPG)])
                    ins.then_inc(s["cbs"], 1)
                if q is not None and 3 <= j < 7:
                    head_weights(dve, q, 2 * (j - 3))
                    if j > 3:
                        head_out(dve, q, 2 * (j - 3) - 1)
                for u in range(4):
                    if q is not None and j < 3:
                        chain_vector(dve, q, 4 * j + u)
                    tap(u + 1)
                if q is not None and 3 <= j < 7:
                    head_weights(dve, q, 2 * (j - 3) + 1)
                    head_out(dve, q, 2 * (j - 3))
                if q is not None and j == 7:
                    head_out(dve, q, HPG - 1)
                    for i_ in range(GT):
                        yb = m["yb"][:, i_, :]
                        dve.wait_ge(s["ytt"], GT * q + i_ + 1)
                        dve.tensor_tensor(yb, yb, S[:, i_, :], ALU.add).then_inc(s["ya"], 1)
                    for i_ in range(GT):
                        yb = m["yb"][:, i_, :]
                        dve.wait_ge(s["ya"], GT * q + i_ + 1)
                        dve.tensor_tensor(yb, yb, m["z"][:, bass.ds(q % 2, 1), i_, :].rearrange("p a t -> p (a t)"),
                                          ALU.mult).then_inc(s["yz"], 1)
                    total = m["acc"][:, 0:NLAT]
                    for i_ in range(1, GT):
                        dve.wait_ge(s["ysq"], GT * q + i_ + 1)
                        if i_ > 1:
                            dve.wait_ge(s["yr"], GT * q + i_)
                        dve.tensor_tensor(total, m["sc0"][:, :] if i_ == 1 else total, m[f"sc{i_ % 2}"][:, :], ALU.add)\
                            .then_inc(s["yr"], 2 if i_ == 1 else 1)
                if q is not None and j == 8:
                    dve.wait_ge(s["ysum"], q + 1)
                    mean_dve(dve, LBLK, GW)
                    dve.wait_ge(s["rbc"], q + (K2 + 2))
                    for i_ in range(GT):
                        yb = m["yb"][:, i_, :]
                        ins = dve.scalar_tensor_tensor(yb, yb, m["colA"][:, bass.ds(q * GT + (COL_SN + i_), 1)],
                                                       S[:, 1, :], ALU.mult, ALU.mult)
                    ins.then_inc(s["ynorm"], 1)

        TURNS = {0: 0, 1: 1, 2: 2, 3: 3, 5: 4, 7: 5}

        def ss_between(pe, g, q, j, k):
            if q is not None:
                if j < 3 and k % 2 == 0:
                    chain_tensor(pe, q, 4 * j + k // 2)
                if 3 <= j < 7:
                    hh = 2 * (j - 3) + k // 4
                    if k % 4 == 0:
                        heads_seg(pe, q, hh)
                    elif k % 4 == 2 and hh:
                        heads_y(pe, q, hh - 1)
                if (j, k) == (7, 1):
                    heads_y(pe, q, HPG - 1)
                if (j, k) == (7, 3):
                    pe.wait_ge(s["ym2"], HPG * q + HPG)
                    for i_ in range(GT):
                        for b in range(LBLK):
                            ins = pe.transpose(block(S[:, i_, :], b), m["ytm"][:, b, i_ * P:(i_ + 1) * P], ident[:, :])
                        ins.then_inc(s["ytt"], 1)
                if (j, k) == (8, 1):
                    pe.wait_ge(s["yr"], GT * q + GT)
                    for b in range(LBLK):
                        ins = pe.matmul(S[:, 0, b:b + 1], block(m["acc"][:, 0:NLAT], b), ones[:, :],
                                        start=True, stop=True)
                    ins.then_inc(s["ysum"], 1)
                if (j, k) == (8, 4):
                    spread_pe(pe, q + (K2 + 1), LBLK, S[:, 1, :])
            elif (j, k) == (1, KT - 1):
                dt_turn(pe)
            if g is not None and j == 9 and k in TURNS:
                n = TURNS[k]
                if n == 0:
                    pe.wait_ge(s["conv"], 6 * g + 6)
                    pe.wait_ge(s["dtT"], 1)
                    pe.wait_ge(s["ynorm"], g + 1)
                    for b in range(NBLK):
                        ins = pe.transpose(block(PAIR[0], b), block(m["bfm"][:, :], b), ident[:, :])
                elif n == 1:
                    for b in range(LBLK):
                        ins = pe.matmul(block(S[:, 2, :], b), block(m["bfm"][:, :], b), block(m["cfm"][:, :], b),
                                        start=True, stop=True)
                else:
                    pe.wait_ge(s["stc"], 6 * g + n - 1)
                    for b in range(NBLK):
                        ins = pe.transpose(block(PAIR[n % 2], b), block(m["xfm"][:, n - 2, :], b), ident[:, :])
                ins.then_inc(s["ytr"], 1)

        def ss_tensor(pe, ss, g, q, prev):
            for j, (kind, i) in enumerate(PANELS):
                if ss is not None:
                    product(pe, ss + j, ss + j, m["hhi"], m["hlo"], KT, LAT if kind in "zc" else SEGS,
                            between=lambda k: ss_between(pe, g, q, j, k))
                else:
                    for k in range(KT):
                        ss_between(pe, None, q, j, k)

        def heads_seg(pe, q, hh):
            if hh == 0:
                for d in (0, 1):
                    pe.wait_ge(states_of[d], state(q, NBLK - 1))
                pe.wait_ge(s["cbs"], q + 1)
            else:
                pe.wait_ge(s["em"], HPG * q + hh)
            for d in (0, 1):
                for part in ("cuhi", "culo"):
                    pe.matmul(S[:, d, :], m["sel"][:, d * HPG + hh:d * HPG + hh + 1].to_broadcast([2 * NH, P]),
                              m[part][:, :], start=(part == "cuhi"), stop=False)
                ins = pe.matmul(S[:, d, :], m["identb"][:, :], m[f"neg{d}"][:, :], start=False, stop=True)
            ins.then_inc(s["sm"], 1)

        def heads_y(pe, q, hh):
            r = hh % 2
            pe.wait_ge(s["mm"], 2 * (HPG * q + hh) + 2)
            if hh < 2:
                pe.wait_ge(s["ymc"], 12 * q + 12)
            else:
                pe.wait_ge(s["ym2"], HPG * q + hh - 1)
            for b in range(LBLK):
                ins = pe.matmul(S[:, 2 + r, b * HP:(b + 1) * HP], block(m[f"e0{r}"][:, :], b),
                                m["xtm"][:, b, hh * HP:(hh + 1) * HP], start=True, stop=True)
            ins.then_inc(s["yd"], 1)

        def ss_all(eng, one):
            one(At(PAN_SS), 0, None, None)
            with eng.Fori(0, GROUPS - 1) as i:
                one(At(PAN_SS + 10, i * 5), i + 1, i, At(PAN_SS + 9, i * 5))
            one(None, None, GROUPS - 1, At(PAN_SO - 1))

        def so_pairs(eng, one):
            with eng.Fori(0, KT // 2) as i:
                for u in (0, 1):
                    for half in (0, 1):
                        one(At(PAN_SO + 2 * u + half, i * 2), At(TIL_SO + u, i), i * 2 + u, half)

        ymid_hi = m["mhi"][:, :, :].rearrange("p f t -> p (f t)")[:, 0:2 * KT * NLAT].rearrange("p (k t) -> p k t", t=NLAT)
        ymid_lo = m["mlo"][:, :, :].rearrange("p f t -> p (f t)")[:, 0:2 * KT * NLAT].rearrange("p (k t) -> p k t", t=NLAT)
        yin = (m["yin0"], m["yin1"])
        Y_LOTS = [(12, 4)] + [(t, 3) for t in range(0, 12, 3)]

        def l1_sync(sp):
            load_panel(sp, At(PAN_DT), cols_of(ssm_w_in[0], SSM_IN - P), KT)

            def loads(ss, g, q, prev):
                if ss is not None:
                    for j, (kind, i) in enumerate(PANELS):
                        load_panel(sp, ss + j, cols_of(ssm_w_in[0], ss_cols(kind, i, g)), KT)
            ss_all(sp, loads)

            def so(pn, tl, j, half):
                load_panel(sp, pn, cols_of(ssm_w_out[0][half * D:(half + 1) * D, :], j * P), KT)
            so_pairs(sp, so)
            ffn_sync(sp, 1)
            for b in range(LBLK):
                sp.wait_ge(s["fo"], KT)
                sp.dma_start(out[0, b * P:(b + 1) * P, :], m["ofin"][:, b, :]).then_inc(s["outd"], 16)
            sp.wait_ge(s["outd"], 16 * LBLK)

        def l1_pool(pool):
            for j in (KT - 2, KT - 1):
                tile_ready(ffn_at(0, 1)[1] + 2 * FH)(pool, j)
            pool.dma_start(x_park, m["x1"][:, :, 0:NLAT]).then_inc(s["parked1"], 16)
            rsqrt_pool(pool, K2, NBLK)
            pool.wait_ge(s["parked1"], 16)
            for d in (0, 1):
                pool.dma_start(m["dtb"][d * NH:(d + 1) * NH, 0:1], ssm_dt_bias[0, d].rearrange("(h a) -> h a", a=1))\
                    .then_inc(s["small"], 16)
                pool.dma_start(m["aneg"][d * NH:(d + 1) * NH, 0:1], ssm_a_log[0, d].rearrange("(h a) -> h a", a=1))\
                    .then_inc(s["small"], 16)
            pool.dma_start(m["dall"][:, :], ssm_d.to_broadcast([P, NH])).then_inc(s["yout"], 16)
            pool.wait_ge(s["yout"], 16)
            for q in (0, 1):
                pool.tensor_copy(m["dsk"][q * HP:(q + 1) * HP, :], m["dall"][q * HP:(q + 1) * HP, q::2])\
                    .then_inc(s["dskin"], 1)
                pool.wait_ge(s["dskin"], q + 1)
            pool.memset(chunks(m["segm"][:, :])[:, 1::2, 0:1], 1.0).then_inc(s["negm"], 1)
            pool.wait_ge(s["hlo"], 8 * (N2 + 1))
            pool.tensor_copy(m["identb"][:, :], ident[:, :])
            for d in (0, 1):
                pool.memset(m[f"neg{d}"][:, :], 0.0).then_inc(s["negz"], 1)
                pool.wait_ge(s["negz"], d + 1)
                v = m[f"neg{d}"][:, :].rearrange("p (b t) -> p b t", t=P)
                pool.affine_select(out=v, in_=v, compare_op=ALU.is_ge, fill=-1e30, base=0,
                                   pattern=[[0, LBLK], [1 - 2 * d, P]], channel_multiplier=2 * d - 1)\
                    .then_inc(s["negm"], 1)
            pool.wait_ge(s["dtT"], 1)
            for i, xp in enumerate(xpad):
                for j, (c0, c1) in enumerate(((0, 2), (2 + NLAT, 4 + NLAT), (4 + T, 8 + T))):
                    pool.memset(xp[:, c0:c1], 0.0).then_inc(s["halo"], 1)
            for g in range(GROUPS):
                rsqrt_pool(pool, K2 + 1 + g, LBLK)
                pool.wait_ge(s["ynorm"], g + 2)
                if g < GROUPS - 1:
                    pool.dma_start(y_park[:, g * GT:(g + 1) * GT, :], m["yb"][:, :, :]).then_inc(s["yout"], 16)
            pool.wait_ge(s["yout"], 16 * GROUPS)
            for k in range((GROUPS - 1) * GT // 3):
                if k >= 2:
                    pool.wait_ge(s["yl"], k)
                pool.dma_start(yin[k % 2][:, :, :], y_park[:, 3 * k:3 * k + 3, :]).then_inc(s[f"yin{k % 2}"], 16)
                if k == 1:
                    pool.dma_start(m["x1"][:, :, 0:NLAT], x_park).then_inc(s["back1"], 16)
            rsqrt_pool(pool, K2 + 1 + GROUPS, LBLK)
            rsqrt_pool(pool, K2 + 2 + GROUPS, LBLK)

        def l1_scalar(act):
            norm_act(act, N2, SEGS, 1, 0)
            dt_scalar(act)
            act.wait_ge(s["halo"], 6)
            act.wait_ge(s["dskin"], 2)
            ss_all(act, lambda *a: ss_scalar(act, *a))
            act.wait_ge(s["ynorm"], GROUPS + 1)
            for k, (t, n) in enumerate(Y_LOTS):
                if k:
                    act.wait_ge(s[f"yin{(k - 1) % 2}"], 16 * ((k - 1) // 2 + 1))
                act.activation(ymid_hi[:, t:t + n, :], (yin[(k - 1) % 2] if k else m["yb"])[:, :, :], ACT.Copy)\
                    .then_inc(s["yh"], 1)

            def so(pn, tl, j, half):
                split_hi(act, pn + 2, KT)
                if half:
                    square_new(act, 3, tl, j, NLAT)
            so_pairs(act, so)
            norm_act(act, 3, LAT, 1, 1)
            ffn_scalar(act, 1, LAT)
            for j in range(KT):
                act.wait_ge(s["ft"], j + 1)
                act.activation(m["ofin"][:, :, j * P:(j + 1) * P],
                               Gq[:, j % 4, :].rearrange("p (b f) -> p b f", f=P), ACT.Copy).then_inc(s["fo"], 1)

        def l1_vector(dve):
            factors(dve, 1, 0)
            norm_dve(dve, m["x1"], N2, K2, SEGS, 1, 0)
            dt_vector(dve)
            ss_all(dve, lambda *a: ss_vector(dve, *a))
            for k, (t, n) in enumerate(Y_LOTS):
                dve.wait_ge(s["yh"], k + 1)
                dve.tensor_tensor(ymid_lo[:, t:t + n, :], (yin[(k - 1) % 2] if k else m["yb"])[:, :, :],
                                  f32(ymid_hi[:, t:t + n, :]), ALU.subtract).then_inc(s["yl"], 1)
            dve.wait_ge(s["back1"], 16)
            dve.wait_ge(s["yl"], len(Y_LOTS))
            no_squares(dve, 3, NLAT)

            def so(pn, tl, j, half):
                split_lo(dve, pn + 2, KT)
                if half:
                    add_gated(dve, tl, j, 1, 2, LAT)
                    add_square(dve, 3, j, tl.slot, NLAT)
            so_pairs(dve, so)
            factors(dve, 1, 1)
            norm_dve(dve, m["x1"], 3, K2 + 1 + GROUPS, LAT, 1, 1)
            ffn_vector(dve, 1, LAT)
            sums_dve(dve, 4, LAT)
            dve.wait_ge(s["rbc"], K2 + 3 + GROUPS)
            for j in range(KT):
                if j >= 2:
                    dve.wait_ge(s["ft"], j - 1)
                dve.scalar_tensor_tensor(hn[j % 2][:, 0:NLAT], m["x1"][:, j, 0:NLAT],
                                         m["colA"][:, COL_FIN + j:COL_FIN + j + 1], PAIR[1][:, 0:NLAT],
                                         ALU.mult, ALU.mult).then_inc(s["fn"], 1)

        def l1_tensor(pe):
            norm_pe(pe, N2, K2, NBLK)
            dt_tensor(pe)
            ss_all(pe, lambda *a: ss_tensor(pe, *a))

            def so(pn, tl, j, half):
                product(pe, pn, tl, ymid_hi, ymid_lo, KT, LAT, k_base=half * KT, first=(half == 0),
                        last=(half == 1), need=lambda k: pe.wait_ge(s["yl"], min((half * KT + k) // 3 + 2, len(Y_LOTS))))
            so_pairs(pe, so)
            norm_pe(pe, 3, K2 + 1 + GROUPS, LBLK)
            ffn_tensor(pe, 1, LAT)
            norm_pe(pe, 4, K2 + 2 + GROUPS, LBLK)
            for j in range(KT):
                pe.wait_ge(s["fn"], j + 1)
                if j >= 4:
                    pe.wait_ge(s["fo"], j - 3)
                for b in range(LBLK):
                    ins = pe.transpose(block(Gq[:, j % 4, :], b), block(hn[j % 2][:, 0:NLAT], b), ident[:, :])
                ins.then_inc(s["ft"], 1)

        block_ = ctx.enter_context(nc.Block())

        @block_.sync
        def _(sp):
            rows = ((m["rowA"], COL_NORM, norm_w.rearrange("l i (j p) -> (l i j) p", p=P)),
                    (m["rowA"], COL_FIN, final_norm_w.rearrange("(j p) -> j p", p=P)),
                    (m["rowA"], COL_C, c.rearrange("b (j p) -> (b j) p", p=P)),
                    (m["rowA"], COL_CC, c_ctx.rearrange("(j p) -> j p", p=P)),
                    (m["rowA"], COL_SN, ssm_norm_w.rearrange("b (j p) -> (b j) p", p=P)),
                    (m["rowA"], COL_CB, ssm_conv_b.rearrange("b (j p) -> (b j) p", p=P)),
                    (m["rowA"], COL_GN, hg_norm_w),
                    (m["rowB"], 0, ada_b.rearrange("l (t p) -> (l t) p", p=P)),
                    (m["rowC"], 0, ssm_conv_w.rearrange("b k (t p) -> (b k t) p", p=P)),
                    (m["rowD"], 0, hg_lb.rearrange("d r (h p) -> (d r h) p", p=P)))
            for to, r0, src in rows:
                sp.dma_start(to[r0:r0 + src.shape[0], :], src).then_inc(s["rows"], 16)
            for n in (0, 1):
                slab_sync(sp, n)
            for b in range(NBLK):
                src = x[0] if b < LBLK else ctx_x[0]
                b0 = b if b < LBLK else b - LBLK
                sp.dma_start(m["xin"][:, b, :], src[b0 * P:(b0 + 1) * P, :]).then_inc(s["xin"], 16)
            for n in (2, 3):
                slab_sync(sp, n)

            def hg_loads(hg, hn_, hp, h, pn_par, ps_par):
                if hg is not None:
                    for j, off in enumerate(HG_OFF):
                        load_panel(sp, hg + j, cols_of(hg_w_in[0], hn_ * P + off), KT)
                        if j == 1:
                            slab_load(sp, hn_ * 2, 0, hn_ * (2 * SLAB) + 2 * D,
                                      None if h is None else hp + 2)
                        if j == 4:
                            slab_load(sp, hn_ * 2 + 1, 0, hn_ * (2 * SLAB) + (2 * D + SLAB), hg)
            hg_all(sp, hg_loads)
            with sp.Fori(0, KT // 2) as i:
                for u in (0, 1):
                    load_panel(sp, At(PAN_HGO + u, i), cols_of(hg_w_out[0], i * 2 * P + u * P), KT)
                slab_load(sp, i + SL_HGO, 1, i * SLAB, At(PAN_HGO - 2, i))
            ffn_sync(sp, 0)
            l1_sync(sp)

        @block_.gpsimd
        def _(pool):
            n = [0]

            def link(ins):
                n[0] += 1
                ins.then_inc(s["ps"], 1)
                pool.wait_ge(s["ps"], n[0])

            link(pool.memset(ident[:, :], 0.0))
            pool.affine_select(out=ident[:, :], in_=ident[:, :], compare_op=ALU.not_equal, fill=1.0, base=0,
                               pattern=[[-1, P]], channel_multiplier=1).then_inc(s["ident"], 1)
            pool.wait_ge(s["ident"], 1)
            link(pool.memset(ones[:, :], 1.0))
            link(pool.memset(m["mhalf"][:, :], -0.5))
            link(pool.memset(m["segm"][:, :], 1.0))
            link(pool.memset(chunks(m["segm"][:, :])[:, :, 0:1], 0.0))
            for d in (0, 1):
                link(pool.memset(mask[d][:, :, :], 1.0))
                for o in (0, CH):
                    link(pool.affine_select(out=mask[d][o:o + CH, :, :], in_=mask[d][o:o + CH, :, :],
                                            compare_op=ALU.is_ge, fill=0.0, base=0,
                                            pattern=[[0, NBLK], [1 - 2 * d, CH]], channel_multiplier=2 * d - 1))
            assert n[0] == N_CONST
            rsqrt_pool(pool, 0, NBLK)
            pool.wait_ge(s["x"], NBLK * 2)
            pool.dma_start(x_park0, m["x0"][:, :, :]).then_inc(s["parked0"], 16)
            for h in range(HEADS):
                rsqrt_pool(pool, h + 1, NBLK)
            pool.wait_ge(s["og"], HEADS)
            pool.wait_ge(s["parked0"], 16)
            pool.dma_start(m["x1"][:, :, :], x_park0).then_inc(s["back0"], 16)
            rsqrt_pool(pool, HEADS + 1, NBLK)
            l1_pool(pool)

        @block_.scalar
        def _(act):
            act.wait_ge(s["cols"], 1)
            for i, col in ((0, COL_C), (1, COL_CC)):
                ins = act.activation(m["csil"][:, :, i], m["colA"][:, col:col + KT], ACT.Silu)
            ins.then_inc(s["csil"], 1)
            act.wait_ge(s["tdve"], 3)
            act.activation(m["lbe"][:, :, :, :], m["lbe"][:, :, :, :], ACT.Exp).then_inc(s["lbs"], 1)
            act.wait_ge(s["x"], NBLK * 2)
            for j in range(KT):
                square(act, 0, m["x0"][:, j, :], j, j % 2, T)
            split_hi(act, At(0), KT)
            split_hi(act, At(1), KT)
            norm_act(act, 0, SEGS, 0, 0)
            hg_all(act, lambda *a: hg_scalar(act, *a))
            act.wait_ge(s["og"], HEADS)
            for j in range(HEADS):
                act.activation(m["hhi"][:, j, :], m["og"][:, j, :], ACT.Copy).then_inc(s["osp_hi"], 1)
            with act.Fori(0, KT // 2) as i:
                for u in (0, 1):
                    split_hi(act, At(PAN_HGO + 2 + u, i), KT)
                    square_new(act, 1, At(PAN_HGO + u, i), i * 2 + u, T)
            norm_act(act, 1, SEGS, 0, 1)
            ffn_scalar(act, 0, SEGS)
            l1_scalar(act)

        @block_.vector
        def _(dve):
            n = [0]

            def link(ins):
                n[0] += 1
                ins.then_inc(s["tdve"], 1)
                dve.wait_ge(s["tdve"], n[0])

            dve.wait_ge(s["tpe"], 1)
            dve.tensor_copy(m["colA"][:, :], S[:, 2, 0:97]).then_inc(s["cols"], 1)
            dve.tensor_copy(m["colB"][:, :], S[:, 2, 128:224])
            dve.tensor_copy(m["colC"][:, :], S[:, 2, 256:376])
            dve.tensor_copy(m["colD"][:, :, :, :].rearrange("p d r h -> p (d r h)"), S[:, 2, 384:432])\
                .then_inc(s["cols"], 1)
            dve.wait_ge(s["cols"], 2)
            D3, lbt, lbe = m["colD"], m["lbt"], m["lbe"]
            link(dve.tensor_tensor(lbt[:, :, :], D3[:, :, 0, :], D3[:, :, 1, :], ALU.max))
            link(dve.tensor_tensor(lbt[:, :, :], lbt[:, :, :], D3[:, :, 2, :], ALU.max))
            for r in range(3):
                ins = dve.tensor_tensor(lbe[:, :, r, :], D3[:, :, r, :], lbt[:, :, :], ALU.subtract)
            link(ins)
            slabs_vector(dve, 0)
            no_squares(dve, 0, T)
            for u in range(2 * NBLK):
                b, q = u // 2, u % 2
                dve.wait_ge(s["xt"], u + 1)
                dve.tensor_copy(m["x0"][:, 4 * q:4 * q + 4, b * P:(b + 1) * P],
                                Gq[:, u % 4, :].rearrange("p (j t) -> p j t", j=4)).then_inc(s["x"], 1)
            dve.wait_ge(s["lbs"], 1)
            link(dve.tensor_tensor(lbt[:, :, :], lbe[:, :, 0, :], lbe[:, :, 1, :], ALU.add))
            link(dve.tensor_tensor(lbt[:, :, :], lbt[:, :, :], lbe[:, :, 2, :], ALU.add))
            link(dve.reciprocal(lbt[:, :, :], lbt[:, :, :]))
            link(dve.tensor_tensor(m["lb"][:, :, :], lbe[:, :, 0, :], lbt[:, :, :], ALU.mult))
            link(dve.tensor_scalar(m["oml"][:, :, :], m["lb"][:, :, :], -1.0, 1.0, ALU.mult, ALU.add))
            for j in range(KT):
                add_square(dve, 0, j, j % 2, T)
            slabs_vector(dve, 1)
            dve.wait_ge(s["modev"], 8)
            factors(dve, 0, 0)
            split_lo(dve, At(0), KT)
            split_lo(dve, At(1), KT)
            norm_dve(dve, m["x0"], 0, 0, SEGS, 0, 0)
            for d in (0, 1):
                ins = dve.memset(att[d][:, :, :], 0.0)
            ins.then_inc(s["og0"], 1)
            dve.wait_ge(s["og0"], 1)
            dve.wait_ge(s["ps"], N_CONST)
            dve.wait_ge(s["parked0"], 16)
            hg_all(dve, lambda *a: hg_vector(dve, *a))
            for j in range(HEADS):
                dve.wait_ge(s["osp_hi"], j + 1)
                dve.tensor_tensor(m["hlo"][:, j, :], m["og"][:, j, :], f32(m["hhi"][:, j, :]), ALU.subtract)\
                    .then_inc(s["osp_lo"], 1)
            dve.wait_ge(s["back0"], 16)
            no_squares(dve, 1, T)
            with dve.Fori(0, KT // 2) as i:
                for u in (0, 1):
                    split_lo(dve, At(PAN_HGO + 2 + u, i), KT)
                    tl = At(PAN_HGO + u, i)
                    if u:
                        slab_out(dve, tl, 1, i * 2)
                    else:
                        dve.tensor_copy(m["mrow0"][:, :], G[0:2, tl.slot, T:T + SLAB])
                    add_gated(dve, tl, i * 2 + u, 0, 2, SEGS)
                    add_square(dve, 1, i * 2 + u, tl.slot, T)
            factors(dve, 0, 1)
            norm_dve(dve, m["x1"], 1, HEADS + 1, SEGS, 0, 1)
            ffn_vector(dve, 0, SEGS)
            l1_vector(dve)

        @block_.tensor
        def _(pe):
            pe.wait_ge(s["ident"], 1)
            pe.wait_ge(s["rows"], 160)
            for name, n, at in (("rowA", 97, 0), ("rowB", 96, 128), ("rowC", 120, 256), ("rowD", 48, 384)):
                ins = pe.transpose(S[:, 2, at:at + n], m[name][:, :], ident[0:n, 0:n])
            ins.then_inc(s["tpe"], 1)
            pe.wait_ge(s["cols"], 2)
            pe.wait_ge(s["csil"], 1)
            slabs_tensor(pe, 0)
            pe.wait_ge(s["xin"], 16 * NBLK)
            for u in range(2 * NBLK):
                b, q = u // 2, u % 2
                if u >= 4:
                    pe.wait_ge(s["x"], u - 3)
                for j in range(4):
                    ins = pe.transpose(Gq[:, u % 4, j * P:(j + 1) * P],
                                       m["xin"][:, b, (4 * q + j) * P:(4 * q + j + 1) * P], ident[:, :])
                ins.then_inc(s["xt"], 1)
            slabs_tensor(pe, 1)
            pe.wait_ge(s["ps"], N_CONST)
            pe.wait_ge(s["modev"], 8)
            norm_pe(pe, 0, 0, NBLK)
            hg_all(pe, lambda *a: hg_tensor(pe, *a))
            with pe.Fori(0, KT // 2) as i:
                for u in (0, 1):
                    pn = At(PAN_HGO + u, i)
                    product(pe, pn, pn, m["hhi"], m["hlo"], KT, SEGS,
                            need=lambda k: pe.wait_ge(s["osp_lo"], k + 1),
                            rows=None if u else i + SL_HGO, turn=m["mrow0"] if u else None)
            norm_pe(pe, 1, HEADS + 1, NBLK)
            ffn_tensor(pe, 0, SEGS)
            l1_tensor(pe)


_INS = ["x", "c", "ctx", "c_ctx", "ada_w", "ada_b", "norm_w", "ffn_w_in", "ffn_w_out", "final_norm_w", "hg_w_in",
        "hg_lb", "hg_norm_w", "hg_w_out", "ssm_w_in", "ssm_conv_w", "ssm_conv_b", "ssm_dt_bias", "ssm_a_log",
        "ssm_d", "ssm_norm_w", "ssm_w_out"]


def kernel(**inputs):
    import numpy as _np
    import concourse.bacc as _bacc
    from concourse.bass_utils import run_bass_kernel_spmd as _run

    nc = _bacc.Bacc("TRN2", target_bir_lowering=False, num_devices=1)
    arrays, args = {}, []
    for name in _INS:
        a = _np.ascontiguousarray(inputs[name])
        arrays[f"in_{name}_dram"] = a
        args.append(nc.dram_tensor(f"in_{name}_dram", a.shape, mybir.dt.from_np(a.dtype), kind="ExternalInput").ap())
    args.append(nc.dram_tensor("out_0_dram", (1, NLAT, D), F32, kind="ExternalOutput").ap())
    program(nc, *args)
    r = _run(nc, [arrays], core_ids=[0])
    return r.results[0]["out_0_dram"]
```
